# Optimizing a Trainium2 kernel written in Bass

```python
import math
import jax, jax.numpy as jnp
from jax import lax
import numpy as np

D_MODEL = 1024
BATCH = 1
SEQ = 512
DEPTH = 1

N_META = 16
EPS = 1e-6
GLA_HEADS = 4
GLA_DK = 128
GLA_DV = 256
GLA_LOWRANK = 16
GLA_TAU = 16.0
GLA_CHUNK = 64
DSA_HEADS = 8
DSA_DH = 128
IDX_HEADS = 8
IDX_DH = 64
TOPK_MAX = 256
Q_BLOCK = 64
REL_BUCKETS = 32
REL_MAX_DIST = 128
D_FF = 2816

IN_SIZES = (GLA_HEADS * GLA_DK, GLA_HEADS * GLA_DK, GLA_HEADS * GLA_DV, GLA_HEADS * GLA_DV, GLA_LOWRANK,
            DSA_HEADS * DSA_DH, DSA_HEADS * DSA_DH, DSA_HEADS * DSA_DH,
            IDX_HEADS * IDX_DH, IDX_DH, IDX_HEADS, D_MODEL, D_MODEL)
IN_WIDTH = sum(IN_SIZES)

kernel_name = 'gla_dsa_macaron_hybrid'

def rmsnorm(x, g):
    x32 = x.astype(jnp.float32)
    y = x32 * lax.rsqrt(jnp.mean(x32 * x32, axis=-1, keepdims=True) + EPS)
    return (y * g.astype(jnp.float32)).astype(x.dtype)

def swiglu(x, w_gate, w_up, w_down):
    return (jax.nn.silu(x @ w_gate) * (x @ w_up)) @ w_down

def rel_bucket(dist):
    n = jnp.maximum(dist, 0)
    max_exact = REL_BUCKETS // 2
    nf = jnp.maximum(n, max_exact).astype(jnp.float32)
    large = max_exact + (jnp.log(nf / max_exact) / math.log(REL_MAX_DIST / max_exact)
                         * (REL_BUCKETS - max_exact)).astype(jnp.int32)
    large = jnp.minimum(large, REL_BUCKETS - 1)
    return jnp.where(n < max_exact, n, large)

def split_in(z):
    idx = np.cumsum(np.array(IN_SIZES))[:-1].tolist()
    return jnp.split(z, idx, axis=-1)

def gla_mixer(q, k, v, r, lr, w_lr, b_lr, g_norm):
    B, T, _ = q.shape
    H, dk, dv, C = GLA_HEADS, GLA_DK, GLA_DV, GLA_CHUNK
    log_a = jax.nn.log_sigmoid((lr @ w_lr + b_lr).astype(jnp.float32)) / GLA_TAU
    pad = (-N_META) % C
    Tp = T + pad
    n = Tp // C
    def chunks(a, d):
        a = jnp.pad(a.astype(jnp.float32), ((0, 0), (pad, 0), (0, 0)))
        return a.reshape(B, n, C, H, d).transpose(1, 0, 3, 2, 4)
    qc = chunks(q, dk) * (dk ** -0.5)
    kc = chunks(k, dk)
    vc = chunks(v, dv)
    gc = chunks(log_a, dk)
    causal = jnp.tril(jnp.ones((C, C), dtype=bool))

    def step(S, inp):
        qi, ki, vi, gi = inp
        b = jnp.cumsum(gi, axis=2)
        diff = b[:, :, :, None, :] - b[:, :, None, :, :]
        decay = jnp.exp(jnp.where(causal[None, None, :, :, None], diff, -jnp.inf))
        A = jnp.einsum('bhtd,bhsd,bhtsd->bhts', qi, ki, decay)
        o = jnp.einsum('bhts,bhsv->bhtv', A, vi) + jnp.einsum('bhtd,bhdv->bhtv', qi * jnp.exp(b), S)
        b_last = b[:, :, -1:, :]
        S = jnp.exp(b_last[:, :, 0, :])[..., None] * S + jnp.einsum('bhsd,bhsv->bhdv', ki * jnp.exp(b_last - b), vi)
        return S, o

    S0 = jnp.zeros((B, H, dk, dv), jnp.float32)
    _, o = lax.scan(step, S0, (qc, kc, vc, gc))
    o = o.transpose(1, 0, 3, 2, 4).reshape(B, Tp, H, dv)[:, pad:].astype(v.dtype)
    o = rmsnorm(o, g_norm)
    return o.reshape(B, T, H * dv) * jax.nn.silu(r)

def dsa_mixer(q, k, v, iq, ik, iw, rel_bias):
    B, T, _ = q.shape
    H, dh, Hi, di, QB = DSA_HEADS, DSA_DH, IDX_HEADS, IDX_DH, Q_BLOCK
    L = T - N_META
    topk = min(TOPK_MAX, L // 4)
    q = q.reshape(B, T, H, dh) * (dh ** -0.5)
    k = k.reshape(B, T, H, dh)
    v = v.reshape(B, T, H, dh)
    iq = iq.reshape(B, T, Hi, di)
    iw = iw * ((Hi ** -0.5) * (di ** -0.5))
    n_blk = -(-T // QB)
    Tp = n_blk * QB
    def blocks(a):
        a = jnp.pad(a, ((0, 0), (0, Tp - T)) + ((0, 0),) * (a.ndim - 2))
        return jnp.moveaxis(a.reshape((B, n_blk, QB) + a.shape[2:]), 1, 0)
    key_pos = jnp.arange(T, dtype=jnp.int32)
    starts = jnp.arange(n_blk, dtype=jnp.int32) * QB

    def block(args):
        qb, iqb, iwb, start = args
        qpos = start + jnp.arange(QB, dtype=jnp.int32)
        s = jnp.einsum('bqhd,bkd->bqhk', iqb, ik)
        score = jnp.einsum('bqh,bqhk->bqk', iwb, jax.nn.relu(s)).astype(jnp.float32)
        admissible = key_pos[None, :] <= qpos[:, None]
        score = jnp.where(admissible[None], score, -jnp.inf)
        _, idx = lax.top_k(score, topk)
        kg = jax.vmap(lambda kk, ii: kk[ii])(k, idx)
        vg = jax.vmap(lambda vv, ii: vv[ii])(v, idx)
        logits = jnp.einsum('bqhd,bqkhd->bhqk', qb, kg).astype(jnp.float32)
        dist = qpos[None, :, None] - idx
        bias = rel_bias[rel_bucket(dist)].astype(jnp.float32)
        logits = logits + jnp.transpose(bias, (0, 3, 1, 2))
        valid = idx <= qpos[None, :, None]
        logits = jnp.where(valid[:, None], logits, -jnp.inf)
        p = jax.nn.softmax(logits, axis=-1).astype(v.dtype)
        return jnp.einsum('bhqk,bqkhd->bqhd', p, vg)

    out = lax.map(block, (blocks(q), blocks(iq), blocks(iw), starts))
    return jnp.moveaxis(out, 0, 1).reshape(B, Tp, H * dh)[:, :T]

def setup_inputs(seed: int = 0) -> dict:
    key = jax.random.key(seed)
    ks = jax.random.split(key, 24)
    f32 = jnp.float32
    def nrm(k_, shape, scale):
        return jax.random.normal(k_, shape, f32) * scale
    def gain(k_, shape):
        return 1.0 + 0.02 * jax.random.normal(k_, shape, f32)
    Dl = DEPTH
    return {
        'x': jax.random.normal(ks[0], (BATCH, SEQ, D_MODEL), f32),
        'meta_tokens': nrm(ks[1], (N_META, D_MODEL), 1.0),
        'norm_ffn1': gain(ks[2], (Dl, D_MODEL)),
        'ffn1_w_gate': nrm(ks[3], (Dl, D_MODEL, D_FF), D_MODEL ** -0.5),
        'ffn1_w_up': nrm(ks[4], (Dl, D_MODEL, D_FF), D_MODEL ** -0.5),
        'ffn1_w_down': nrm(ks[5], (Dl, D_FF, D_MODEL), D_FF ** -0.5),
        'norm_mix': gain(ks[6], (Dl, D_MODEL)),
        'w_in': nrm(ks[7], (Dl, D_MODEL, IN_WIDTH), D_MODEL ** -0.5),
        'gla_w_lr': nrm(ks[8], (Dl, GLA_LOWRANK, GLA_HEADS * GLA_DK), GLA_LOWRANK ** -0.5),
        'gla_b_lr': nrm(ks[9], (Dl, GLA_HEADS * GLA_DK), 0.1),
        'gla_norm': gain(ks[10], (Dl, GLA_DV)),
        'w_up_a': nrm(ks[11], (Dl, GLA_HEADS * GLA_DV, D_MODEL), (GLA_HEADS * GLA_DV) ** -0.5),
        'w_up_b': nrm(ks[12], (Dl, DSA_HEADS * DSA_DH, D_MODEL), (DSA_HEADS * DSA_DH) ** -0.5),
        'w_out': nrm(ks[13], (Dl, D_MODEL, D_MODEL), D_MODEL ** -0.5),
        'rel_bias': nrm(ks[14], (REL_BUCKETS, DSA_HEADS), 0.5),
        'norm_ffn2': gain(ks[15], (Dl, D_MODEL)),
        'ffn2_w_gate': nrm(ks[16], (Dl, D_MODEL, D_FF), D_MODEL ** -0.5),
        'ffn2_w_up': nrm(ks[17], (Dl, D_MODEL, D_FF), D_MODEL ** -0.5),
        'ffn2_w_down': nrm(ks[18], (Dl, D_FF, D_MODEL), D_FF ** -0.5),
        'norm_final': gain(ks[19], (D_MODEL,)),
    }

def reference(x, meta_tokens, norm_ffn1, ffn1_w_gate, ffn1_w_up, ffn1_w_down, norm_mix, w_in,
              gla_w_lr, gla_b_lr, gla_norm, w_up_a, w_up_b, w_out, rel_bias, norm_ffn2,
              ffn2_w_gate, ffn2_w_up, ffn2_w_down, norm_final):
    B = x.shape[0]
    meta = jnp.broadcast_to(meta_tokens[None].astype(x.dtype), (B, N_META, D_MODEL))
    h = jnp.concatenate([meta, x], axis=1)
    for l in range(DEPTH):
        h = h + 0.5 * swiglu(rmsnorm(h, norm_ffn1[l]), ffn1_w_gate[l], ffn1_w_up[l], ffn1_w_down[l])
        u = rmsnorm(h, norm_mix[l])
        (gq, gk, gv, gr, glr, dq, dk_, dv_, iq, ik, iw, ga, gb) = split_in(u @ w_in[l])
        y_a = gla_mixer(gq, gk, gv, gr, glr, gla_w_lr[l], gla_b_lr[l], gla_norm[l])
        y_b = dsa_mixer(dq, dk_, dv_, iq, ik, iw, rel_bias)
        merged = jax.nn.sigmoid(ga) * (y_a @ w_up_a[l]) + jax.nn.sigmoid(gb) * (y_b @ w_up_b[l])
        h = h + merged @ w_out[l]
        h = h + 0.5 * swiglu(rmsnorm(h, norm_ffn2[l]), ffn2_w_gate[l], ffn2_w_up[l], ffn2_w_down[l])
    h = rmsnorm(h, norm_final)
    return h[:, N_META:]


_drawn_inputs = setup_inputs


def setup_inputs(seed=0):
    import zlib

    import numpy as np

    out = dict(_drawn_inputs(seed))
    spreads = {}
    factors = {'norm_ffn1': 4.752,
     'norm_mix': 3.321,
     'gla_b_lr': 4.247,
     'gla_norm': 8.0,
     'norm_ffn2': 7.591,
     'norm_final': 8.028,
     'rel_bias': 3.112}
    for name, (base, spread) in spreads.items():
        noise = np.random.default_rng([zlib.crc32(name.encode()), seed]).standard_normal(out[name].shape)
        drawn = base * np.exp(spread * noise) if base else spread * noise
        out[name] = __import__('jax').numpy.asarray(drawn.astype(out[name].dtype))
    for name, factor in factors.items():
        out[name] = (out[name] * factor).astype(out[name].dtype)
    return out
```

```python
import math
from contextlib import ExitStack

import numpy as np

import concourse.bass as bass
from concourse import mybir

F32 = mybir.dt.float32
F32R = mybir.dt.float32r
U8 = mybir.dt.uint8
ACT = mybir.ActivationFunctionType
ALU = mybir.AluOpType
AX = mybir.AxisListType

P = 128
D = 1024
KT = D // P
SEQ = 512
META = 16
NT = SEQ + META
HALF = NT // 2
DFF = 2816
FT = DFF // P
DOWN_SPLIT = (6, 6, 5, 5)
EPS = 1e-6
GH, DK, DV = 4, 128, 256
LOWRANK = 16
TAU = 16.0
DH_HEADS, DH = 8, 128
IH, IDH = 8, 64
TOPK = min(256, SEQ // 4)
BUCKETS, MAX_DIST = 32, 128
QT = SEQ // P
LEVELS = (64, 32, 16, 8, 4, 2, 1)
NEG = -3.0e38
MASKED = -1.0e30
GLR_ROW, IW_ROW = 64, 96
WIDTH = [META + P * (i + 1) for i in range(QT)]
COL = [sum(WIDTH[:i]) for i in range(QT)]
LINE = NT + P
SLOTS = 4
BLOCK = KT * P

V_FFN1, V_MIX, V_FFN2, V_FINAL, V_GLA, V_BLR = 0, 8, 16, 24, 32, 34
NVEC = V_BLR + GH

G_UP1 = 0
G_DOWN1 = G_UP1 + 2 * FT
G_IDX = G_DOWN1 + 4 * KT
G_GLA = G_IDX + 5
G_DSA = G_GLA + 4 * GH
G_MERGE = G_DSA + 4 * DH_HEADS
G_OUT = G_MERGE + 4 * KT
G_UP2 = G_OUT + KT
G_DOWN2 = G_UP2 + 2 * FT
G_END = G_DOWN2 + 4 * KT
T_UP1 = 2
T_DOWN1 = T_UP1 + 2 * FT
T_IDX = T_DOWN1 + KT
T_GLA = T_IDX + 5
T_DSA = T_GLA + 4 * GH
T_MERGE = T_DSA + 4 * DH_HEADS
T_OUT = T_MERGE + 4 * KT
T_UP2 = T_OUT + KT
T_DOWN2 = T_UP2 + 2 * FT


def build(nc, io):
    ctx = ExitStack()
    with ctx:
        def sem(name):
            return ctx.enter_context(nc.semaphore(name))

        arena_bytes = 212800
        base = (nc.sbuf_base + 31) // 32 * 32
        ctx.enter_context(nc.sbuf_tensor("arena", [P, arena_bytes // 4], F32))
        top = [0]

        def at(name, shape, dt, off):
            size = int(np.prod(shape[1:])) * (1 if dt == U8 else 4)
            assert off % 32 == 0 and off + size <= arena_bytes, (name, off, size)
            return nc.alloc_sbuf_tensor_at(name, shape, dt, offset=base + off), off + (size + 31) // 32 * 32

        def keep(name, shape, dt=F32):
            t, top[0] = at(name, shape, dt, top[0])
            return t

        hT = keep("hT", [P, KT, NT])
        xh = keep("xh", [P, KT, NT], F32R)
        xl = keep("xl", [P, KT, NT], F32R)
        rstd = keep("rstd", [P, NT])
        ssum = keep("ssum", [P, NT])
        wraw = keep("wraw", [P, SLOTS, BLOCK])
        wh = keep("wh", [P, SLOTS, BLOCK], F32R)
        wl = keep("wl", [P, SLOTS, BLOCK], F32R)
        vecs = keep("vecs", [P, NVEC])
        ones = keep("ones", [P, P])
        ident = keep("ident", [P, P])
        eps = keep("eps", [P, 1])
        sq = keep("sq", [P, NT])
        FREE = top[0]

        def region(start):
            cur = [start]

            def put(name, shape, dt=F32):
                t, cur[0] = at(name, shape, dt, cur[0])
                return t
            put.here = lambda: cur[0]
            return put

        put = region(FREE)
        ah = put("ah", [P, FT, NT], F32R)
        al = put("al", [P, FT, NT], F32R)
        zg = put("zg", [P, NT])
        sg = put("sg", [P, NT])
        zu = put("zu", [P, NT])
        put = region(FREE)
        oT = put("oT", [P, KT, SEQ])
        yah, _ = at("yah", [P, KT, SEQ], F32R, FREE)
        Y = put.here()
        yal = put("yal", [P, KT, SEQ], F32R)
        ybh = put("ybh", [P, KT, SEQ], F32R)
        ybl = put("ybl", [P, KT, SEQ], F32R)
        score = put("score", [P, sum(WIDTH)])
        DS = put.here()
        mput = region(put.here() - 32 * ((sum(WIDTH) * 4) // 32))
        mh = mput("mh", [P, KT, SEQ], F32R)
        ml = mput("ml", [P, KT, SEQ], F32R)
        mz, msg, ma = (mput(n, [P, SEQ]) for n in ("mz", "msg", "ma"))
        dput = region(DS)
        work = dput("work", [P, sum(WIDTH)])
        dqT = dput("dqT", [P, SEQ])
        dkT = dput("dkT", [P, NT])
        dvT = dput("dvT", [P, NT])
        dV = dput("dV", [P, QT + 1, DH])
        strip = dput("strip", [P, NT])
        logit = dput("logit", [P, 2, NT])
        pT = dput("pT", [P, 2, (QT + 1) * P])
        zr = dput("zr", [P, SEQ])
        sr = dput("sr", [P, SEQ])
        nmax = dput("nmax", [P, 2])
        rowsum = dput("rowsum", [P, 2])
        rinv = dput("rinv", [P, 2])
        gput = region(Y)
        blog = gput("blog", [P, GH, NT])
        qT = gput("qT", [P, SEQ])
        kT = gput("kT", [P, NT])
        vT = gput("vT", [P, 2, NT])
        V = gput("V", [P, QT + 1, DV])
        X = gput("X", [P, 2, SEQ])
        E = gput("E", [P, 2, SEQ])
        Dl = gput("Dl", [P, 2, SEQ])
        A = gput("A", [P, SEQ])
        S = gput("S", [P, 2, DV])
        lvlmask = gput("lvlmask", [P, len(LEVELS) + 1, P], U8)
        eb = gput("eb", [P, QT])
        ossq = gput("ossq", [P, QT])
        orms = gput("orms", [P, QT])
        orstd = gput("orstd", [P, QT])
        m8 = gput("m8", [P, QT, 8])
        iwq = gput("iwq", [P, QT, IH])
        triu = gput("triu", [P, P])
        qe = gput("qe", [P, SEQ])
        ke = gput("ke", [P, NT])
        kdT = gput("kdT", [P, QT, P])
        assert gput.here() <= DS - 4 * sum(WIDTH)
        iput = region(FREE)
        iq = iput("iq", [P, 4, SEQ])
        misc = iput("misc", [P, NT])
        iput = region(DS + (sum(WIDTH) * 4 + 31) // 32 * 32)
        on = iput("on", [P, QT, DV])
        ik2 = iput("ik2", [P, NT])
        zt = iput("zt", [P, NT])
        t1 = iput("t1", [P, 2, NT])
        chunk0 = iput("chunk0", [P, NT])
        wlr = iput("wlr", [P, GH * DK])
        relb = iput("relb", [BUCKETS, DH_HEADS])
        oneh = iput("oneh", [BUCKETS, LINE])
        line = iput("line", [DH_HEADS, LINE])
        final, _ = at("final", [P, KT, SEQ], F32, FREE)

        proj = ctx.enter_context(nc.psum_tensor("proj", [P, 2, 1024], F32))
        ps = ctx.enter_context(nc.psum_tensor("ps", [P, 2, 1024], F32))

        bias_line = nc.dram_tensor("bias_line", (DH_HEADS, LINE), F32)
        bias_strip = nc.dram_tensor("bias_strip", (DH_HEADS, P, NT), F32)

        def wide(r):
            return proj[:, r, :].rearrange("p (b n) -> p b n", b=2)[:, :, 0:HALF]

        def two(x):
            return x.rearrange("p (b n) -> p b n", b=2)

        def f(x):
            return x.bitcast(F32)

        consts = sem("consts")
        consts2 = sem("consts2")
        h_in = [sem(f"h_in{n}") for n in range(KT // 2)]
        w_in = [sem(f"w_in{s}") for s in range(SLOTS)]
        w_hi = sem("w_hi")
        w_lo = sem("w_lo")
        w_used = sem("w_used")
        evac = sem("evac")
        x_hi = sem("x_hi")
        x_lo = sem("x_lo")
        squared = sem("squared")
        ss_acc = sem("ss_acc")
        ss_sum = sem("ss_sum")
        rms_ok = sem("rms_ok")
        rstd_ok = sem("rstd_ok")
        setup = sem("setup")
        sig = sem("sig")
        gated = sem("gated")
        act_f = sem("act_f")
        act_hi = sem("act_hi")
        act_lo = sem("act_lo")
        iwT_mm = sem("iwT_mm")
        iw_ok = sem("iw_ok")
        ik2_in = sem("ik2_in")
        z_mm = sem("z_mm")
        lvl_ok = sem("lvl_ok")
        zb_ok = sem("zb_ok")
        softp = sem("softp")
        ls_ok = sem("ls_ok")
        b_ok = sem("b_ok")
        line_mm = sem("line_mm")
        line_ok = sem("line_ok")
        line_st = sem("line_st")
        s_mm = sem("s_mm")
        s_relu = sem("s_relu")
        s_acc = sem("s_acc")
        tk = sem("tk")
        mask_ok = sem("mask_ok")
        d_ok = sem("d_ok")
        e_ok = sem("e_ok")
        x_ok = sem("x_ok")
        g_mm = sem("g_mm")
        a_ok = sem("a_ok")
        vt_mm = sem("vt_mm")
        vt_ok = sem("vt_ok")
        de_ok = sem("de_ok")
        ex_ok = sem("ex_ok")
        qk_ok = sem("qk_ok")
        kd_mm = sem("kd_mm")
        kd_ok = sem("kd_ok")
        u_mm = sem("u_mm")
        s_ok = sem("s_ok")
        o_mm = sem("o_mm")
        oss_ok = sem("oss_ok")
        orms_ok = sem("orms_ok")
        orstd_ok = sem("orstd_ok")
        on_ok = sem("on_ok")
        ot_mm = sem("ot_mm")
        ot_ok = sem("ot_ok")
        strip_in = sem("strip_in")
        dv_mm = sem("dv_mm")
        dv_ok = sem("dv_ok")
        qk_mm = sem("qk_mm")
        lg_ok = sem("lg_ok")
        lm_ok = sem("lm_ok")
        p_ok = sem("p_ok")
        ri_ok = sem("ri_ok")
        pn_ok = sem("pn_ok")
        pt_mm = sem("pt_mm")
        pt_ok = sem("pt_ok")
        pv_mm = sem("pv_mm")
        yb_hi = sem("yb_hi")
        yb_lo = sem("yb_lo")
        r_sig = sem("r_sig")
        r_g = sem("r_g")
        ya_f = sem("ya_f")
        ya_hi = sem("ya_hi")
        ya_lo = sem("ya_lo")
        m_sig = sem("m_sig")
        m_sum = sem("m_sum")
        m_hi = sem("m_hi")
        m_lo = sem("m_lo")
        out_ok = sem("out_ok")
        out_st = sem("out_st")
        carried = sem("carried")

        def apart(eng):
            eng.sem_inc(carried, 1)

        block = ctx.enter_context(nc.Block())

        @block.sync
        def _(sp):
            def load(g, src, cols=BLOCK):
                slot = g % SLOTS
                if g >= SLOTS:
                    sp.wait_ge(w_lo, g - SLOTS + 1)
                sp.dma_start(wraw[:, slot, 0:cols], src).then_inc(w_in[slot], 16)

            def load_loop(g0, n, src):
                with sp.Fori(0, n) as i:
                    for j in range(4):
                        row = sp.snap(i * 4 + j)
                        free = sp.snap(i * 4 + (g0 + j - SLOTS + 1))
                        slot = (g0 + j) % SLOTS
                        sp.wait_ge(w_lo, free)
                        sp.dma_start(wraw[:, slot, :], src[row]).then_inc(w_in[slot], 16)

            def load_down(g0, src):
                with sp.Fori(0, KT) as m:
                    k = 0
                    row = sp.snap(m * 1)
                    for j, n in enumerate(DOWN_SPLIT):
                        free = sp.snap(m * 4 + (g0 + j - SLOTS + 1))
                        slot = (g0 + j) % SLOTS
                        sp.wait_ge(w_lo, free)
                        sp.dma_start(wraw[:, slot, 0:n * P], src[row][:, k * P:(k + n) * P])\
                          .then_inc(w_in[slot], 16)
                        k += n

            load(0, io["w_up1"][0])
            for n in range(KT // 2):
                sp.dma_start(hT[:, 2 * n:2 * n + 2, :], io["xT"][:, 2 * n:2 * n + 2, :]).then_inc(h_in[n], 16)
                if n < SLOTS - 1:
                    load(n + 1, io["w_up1"][n + 1])
            load_loop(SLOTS, 2 * FT // 4 - 1, io["w_up1"][SLOTS:])
            load_down(G_DOWN1, io["w_down1"])
            for j in range(5):
                load(G_IDX + j, io["w_mix"][j])
                if j == 3:
                    sp.wait_ge(w_used, G_IDX)
                    sp.dma_start(on[:, :, :].rearrange("p c n -> p (c n)"), io["lvlmask"]).then_inc(consts2, 16)
                    sp.dma_start(triu[:, :], io["triu"]).then_inc(consts2, 16)
                    sp.dma_start(chunk0[:, :], io["chunk0"]).then_inc(consts2, 16)
                    sp.dma_start(wlr[GLR_ROW:GLR_ROW + LOWRANK, :], io["w_lr"]).then_inc(consts2, 16)
                    sp.dma_start(relb[:, :], io["rel_bias"]).then_inc(consts2, 16)
                    sp.dma_start(oneh[:, :], io["oneh"]).then_inc(consts2, 16)
            load_loop(G_GLA, (G_UP2 - G_GLA) // 4, io["w_mix"][5:])
            load_loop(G_UP2, 2 * FT // 4, io["w_up2"])
            load_down(G_DOWN2, io["w_down2"])
            for m in range(KT):
                sp.wait_ge(out_ok, m + 1)
                sp.dma_start(io["outT"][m], final[:, m, :]).then_inc(out_st, 16)
            sp.wait_ge(out_st, 16 * KT)

        @block.gpsimd
        def _(pool):
            def lo(g, slot):
                pool.wait_ge(w_hi, g + 1)
                pool.tensor_tensor(wl[:, slot, :], wraw[:, slot, :], f(wh[:, slot, :]), ALU.subtract)\
                    .then_inc(w_lo, 1)

            def lo_loop(g0, n):
                with pool.Fori(0, n) as i:
                    for j in range(4):
                        lo(i * 4 + (g0 + j), (g0 + j) % SLOTS)

            pool.memset(ones[:, :], 1.0).then_inc(setup, 1)
            for g in range(SLOTS):
                lo(g, g)
            lo_loop(SLOTS, G_GLA // 4)
            for g in range(SLOTS + G_GLA // 4 * 4, G_GLA + SLOTS):
                lo(g, g % SLOTS)
            pool.memset(A[:, :], 0.0).then_inc(setup, 1)

            with pool.Fori(0, GH) as hd:
                g = hd * 4 + (G_GLA + SLOTS)

                def level(l):
                    m = LEVELS[l]
                    if l >= 2:
                        pool.wait_ge(g_mm, hd * 8 + (l - 1))
                    pool.wait_ge(e_ok, hd * 7 + (l + 1))
                    v = {n: x.rearrange("p (b two m) -> p b two m", two=2, m=m) for n, x in
                         (("q", qT[:, :]), ("k", kT[:, META:NT]), ("E", E[:, l % 2, :]), ("X", X[:, l % 2, :]))}
                    pool.tensor_tensor(v["X"][:, :, 1, :], v["q"][:, :, 1, :], v["E"][:, :, 1, :], ALU.mult)\
                        .then_inc(x_ok, 1)
                    pool.tensor_tensor(v["X"][:, :, 0, :], v["k"][:, :, 0, :], v["E"][:, :, 0, :], ALU.mult)\
                        .then_inc(x_ok, 1)

                lo(g, G_GLA % SLOTS)
                lo(g + 1, (G_GLA + 1) % SLOTS)
                for l in range(4):
                    level(l)
                lo(g + 2, (G_GLA + 2) % SLOTS)
                for l in range(4, 7):
                    level(l)
                lo(g + 3, (G_GLA + 3) % SLOTS)
                pool.wait_ge(ex_ok, hd * 3 + 1)
                pool.tensor_tensor(qe[:, :], qT[:, :], E[:, 1, :], ALU.mult).then_inc(qk_ok, 1)
                pool.wait_ge(ex_ok, hd * 3 + 2)
                pool.tensor_tensor(ke[:, :], kT[:, :], sq[:, :], ALU.mult).then_inc(qk_ok, 1)

            lo_loop(G_DSA + SLOTS, (G_END - G_DSA - SLOTS) // 4)

        @block.scalar
        def _(act):
            act.dma_start(vecs[:, :], io["vecs"]).then_inc(consts, 16)
            act.dma_start(ident[:, :], io["ident"]).then_inc(consts, 16)

            def hi(g, slot):
                lap = g // SLOTS if isinstance(g, int) else None
                act.wait_ge(w_in[slot], 16 * (lap + 1))
                if g >= SLOTS:
                    act.wait_ge(w_used, g - SLOTS + 1)
                act.activation(wh[:, slot, :], wraw[:, slot, :], ACT.Copy).then_inc(w_hi, 1)

            def hi_at(i, per, g0):
                if isinstance(i, int):
                    if i * per + g0 < G_END:
                        hi(i * per + g0, g0 % SLOTS)
                    return
                slot = g0 % SLOTS
                act.wait_ge(w_in[slot], i * (16 * per // SLOTS) + 16 * (g0 // SLOTS + 1))
                act.wait_ge(w_used, i * per + (g0 - SLOTS + 1))
                act.activation(wh[:, slot, :], wraw[:, slot, :], ACT.Copy).then_inc(w_hi, 1)

            def x_tile(n, m, lo_tok, gain):
                if gain is not None:
                    apart(act)
                    act.activation(xh[:, m, lo_tok:NT], hT[:, m, lo_tok:NT], ACT.Copy,
                                   scale=vecs[:, gain + m:gain + m + 1] if isinstance(m, int)
                                   else vecs[:, bass.ds(m + gain, 1)]).then_inc(x_hi, 1)
                act.wait_ge(ss_acc, m + (9 * n + 1))
                apart(act)
                act.activation(sq[:, lo_tok:NT], hT[:, m, lo_tok:NT], ACT.Square).then_inc(squared, 1)

            def rms(n, lo_tok):
                act.wait_ge(ss_sum, n + 1)
                if lo_tok == 0:
                    act.activation(two(sq[:, :]), ps[:, 0, :].rearrange("p (b n) -> p b n", b=2)[:, :, 0:HALF],
                                   ACT.Sqrt, bias=eps[:, :], scale=1.0 / D).then_inc(rms_ok, 1)
                else:
                    act.activation(sq[:, META:NT], ps[:, 0, 0:SEQ], ACT.Sqrt, bias=eps[:, :], scale=1.0 / D)\
                       .then_inc(rms_ok, 1)

            def up(i, n, g0, t0):
                for j in range(2):
                    ft = i * 2 + j
                    hi_at(i, 4, g0 + 2 * j + SLOTS)
                    act.wait_ge(evac, i * 4 + (t0 + 2 * j + 1))
                    act.activation(sg[:, lo_tok_of(n):NT], zg[:, lo_tok_of(n):NT], ACT.Sigmoid).then_inc(sig, 1)
                    act.wait_ge(act_f, i * 2 + (FT * n + j + 1))
                    apart(act)
                    act.activation(ah[:, ft, lo_tok_of(n):NT], zu[:, lo_tok_of(n):NT], ACT.Copy).then_inc(act_hi, 1)
                    hi_at(i, 4, g0 + 2 * j + 1 + SLOTS)

            def down(i, n, g0, t0, gain):
                for j in range(2):
                    for b in range(4):
                        hi_at(i, 8, g0 + 4 * j + b + SLOTS)
                    act.wait_ge(evac, i * 2 + (t0 + j + 1))
                    x_tile(n, i * 2 + j, lo_tok_of(n - 1), gain)

            def lo_tok_of(n):
                return 0 if n == 0 else META

            act.wait_ge(consts, 16 * 2)
            act.wait_ge(evac, 2)
            hi(0, 0)
            for m in range(KT):
                if m % 2 == 0:
                    act.wait_ge(h_in[m // 2], 16)
                x_tile(0, m, 0, V_FFN1)
                if m % 2 == 1 and m // 2 + 1 < SLOTS:
                    hi(m // 2 + 1, m // 2 + 1)
            rms(0, 0)
            with act.Fori(0, FT // 2) as i:
                up(i, 0, G_UP1, T_UP1)
            with act.Fori(0, KT // 2) as i:
                down(i, 1, G_DOWN1, T_DOWN1, V_MIX)
            rms(1, 0)

            for j in range(5):
                act.wait_ge(w_used, G_IDX + j + 1)
                hi_at(0, 4, G_IDX + j + SLOTS)
                if j == 0:
                    act.wait_ge(evac, T_IDX + 1)
                    act.dma_start(ik2[64:128, :], misc[0:64, :]).then_inc(ik2_in, 16)
            for h in range(GH):
                act.wait_ge(zb_ok, h + 1)
                act.activation(t1[:, 0, :], zt[:, :], ACT.Abs).then_inc(softp, 1)
                act.wait_ge(softp, 3 * h + 1)
                act.activation(t1[:, 0, :], t1[:, 0, :], ACT.Exp, scale=-1.0).then_inc(softp, 1)
                act.wait_ge(softp, 3 * h + 2)
                if h >= 1:
                    act.wait_ge(ls_ok, h)
                act.activation(t1[:, 1, :], t1[:, 0, :], ACT.Ln, bias=1.0).then_inc(softp, 1)
            for n in range(QT * IH):
                i = n // IH
                act.wait_ge(s_mm, n + 1)
                if n >= 2:
                    act.wait_ge(s_acc, n - 1)
                else:
                    act.wait_ge(ls_ok, GH)
                act.activation(t1[:, n % 2, 0:WIDTH[i]], ps[:, n % 2, 0:WIDTH[i]], ACT.Relu).then_inc(s_relu, 1)

            act.wait_ge(line_ok, 1)
            act.dma_start(bias_line.ap(), line[:, :]).then_inc(line_st, 16)
            act.wait_ge(line_st, 16)
            act.dma_start(bias_strip.ap(), bass.AP(bias_line, P - 1, [[LINE, DH_HEADS], [-1, P], [1, NT]]))\
               .then_inc(line_st, 16)

            with act.Fori(0, GH) as hd:
                def level(l):
                    act.wait_ge(d_ok, hd * 14 + (2 * l + 2))
                    if l >= 2:
                        act.wait_ge(x_ok, hd * 14 + 2 * (l - 1))
                    act.activation(E[:, l % 2, :], Dl[:, l % 2, :], ACT.Exp, scale=1.0 / TAU).then_inc(e_ok, 1)

                def copy_v(j):
                    act.wait_ge(vt_mm, hd * 2 + (j + 1))
                    act.activation(V[:, 1:QT + 1, j * P:(j + 1) * P],
                                   ps[:, 1, 0:QT * P].rearrange("p (c n) -> p c n", c=QT), ACT.Copy).then_inc(vt_ok, 1)
                    act.activation(V[0:META, 0, j * P:(j + 1) * P], ps[0:META, 1, 512:512 + P], ACT.Copy)\
                       .then_inc(vt_ok, 1)

                hi_at(hd, 4, G_GLA + SLOTS)
                hi_at(hd, 4, G_GLA + 1 + SLOTS)
                for l in range(4):
                    level(l)
                hi_at(hd, 4, G_GLA + 2 + SLOTS)
                for l in range(4, 7):
                    level(l)
                hi_at(hd, 4, G_GLA + 3 + SLOTS)
                copy_v(0)
                act.wait_ge(x_ok, hd * 14 + 12)
                apart(act)
                act.activation(E[:, 1, :], blog[:, hd, META:NT], ACT.Exp, scale=1.0 / TAU).then_inc(ex_ok, 1)
                act.wait_ge(de_ok, hd * 2 + 2)
                act.activation(sq[:, :], sq[:, :], ACT.Exp, scale=-1.0 / TAU).then_inc(ex_ok, 1)
                apart(act)
                act.activation(eb[:, :], blog[:, hd, META:NT].rearrange("p (c t) -> p c t", c=QT)[:, :, P - 1],
                               ACT.Exp, scale=1.0 / TAU).then_inc(ex_ok, 1)
                copy_v(1)
                act.wait_ge(kd_mm, hd + 1)
                act.activation(kdT[:, 1:QT, :], ps[:, 1, 0:(QT - 1) * P].rearrange("p (c n) -> p c n", c=QT - 1),
                               ACT.Copy).then_inc(kd_ok, 1)
                act.activation(kdT[0:META, 0, :], ps[0:META, 1, 512:512 + P], ACT.Copy).then_inc(kd_ok, 1)
                for c in range(QT):
                    act.wait_ge(o_mm, hd * 4 + (c // 2 * 2 + 2))
                    act.activation(Dl[:, 0, 0:DV], ps[:, 0, c * DV:(c + 1) * DV], ACT.Square,
                                   accum_out=ossq[:, c:c + 1]).then_inc(oss_ok, 1)
                    act.wait_ge(oss_ok, hd * 4 + (c + 1))
                act.activation(orms[:, :], ossq[:, :], ACT.Sqrt, bias=eps[:, :], scale=1.0 / DV).then_inc(orms_ok, 1)
                for j in range(2):
                    act.wait_ge(ot_mm, hd * 2 + (j + 1))
                    apart(act)
                    act.activation(oT[:, hd * 2 + j, :], ps[:, 1, j * SEQ:(j + 1) * SEQ], ACT.Copy,
                                   scale=vecs[:, V_GLA + j:V_GLA + j + 1]).then_inc(ot_ok, 1)

            act.wait_ge(line_st, 32)
            act.wait_ge(mask_ok, 1)
            act.dma_start(strip[:, :], bias_strip.ap()[0]).then_inc(strip_in, 16)
            with act.Fori(0, DH_HEADS) as h:
                def softmax(i):
                    w = WIDTH[i]
                    act.wait_ge(lm_ok, h * 4 + (i + 1))
                    act.activation(logit[:, i % 2, 0:w], logit[:, i % 2, 0:w], ACT.Exp, scale=-1.0,
                                   bias=nmax[:, i % 2:i % 2 + 1], accum_out=rowsum[:, i % 2:i % 2 + 1])\
                       .then_inc(p_ok, 1)

                def copy_p(i):
                    act.wait_ge(pt_mm, h * 4 + (i + 1))
                    act.activation(pT[:, i % 2, P:P + (i + 1) * P], ps[:, 1, 0:(i + 1) * P], ACT.Copy)\
                       .then_inc(pt_ok, 1)
                    act.activation(pT[0:META, i % 2, 0:P], ps[0:META, 1, 512:512 + P], ACT.Copy)\
                       .then_inc(pt_ok, 1)

                def y_high(i):
                    act.wait_ge(pv_mm, h * 4 + (i + 1))
                    apart(act)
                    act.activation(ybh[:, h, i * P:(i + 1) * P], ps[:, 0, 640:640 + P], ACT.Copy).then_inc(yb_hi, 1)

                hi_at(h, 4, G_DSA + SLOTS)
                hi_at(h, 4, G_DSA + 1 + SLOTS)
                hi_at(h, 4, G_DSA + 2 + SLOTS)
                act.wait_ge(dv_mm, h + 1)
                act.activation(dV[:, 1:QT + 1, :], ps[:, 1, 0:QT * P].rearrange("p (c n) -> p c n", c=QT), ACT.Copy)\
                   .then_inc(dv_ok, 1)
                act.activation(dV[0:META, 0, :], ps[0:META, 1, 512:512 + P], ACT.Copy).then_inc(dv_ok, 1)
                softmax(0)
                hi_at(h, 4, G_DSA + 3 + SLOTS)
                for i in range(QT):
                    if i + 1 < QT:
                        softmax(i + 1)
                    copy_p(i)
                    y_high(i)
                act.wait_ge(evac, h * 4 + (T_DSA + 4))
                act.activation(sr[:, :], zr[:, :], ACT.Sigmoid).then_inc(r_sig, 1)
                act.wait_ge(ya_f, h + 1)
                apart(act)
                act.activation(yah[:, h, :], zr[:, :], ACT.Copy).then_inc(ya_hi, 1)
                act.wait_ge(lg_ok, h * 4 + 4)
                act.dma_start(strip[:, :], bias_strip.ap()[(h + 1) % DH_HEADS]).then_inc(strip_in, 16)

            with act.Fori(0, KT) as m:
                hi_at(m, 4, G_MERGE + SLOTS)
                for j in range(2):
                    act.wait_ge(evac, m * 4 + (T_MERGE + 2 * j + 1))
                    act.activation(msg[:, :], mz[:, :], ACT.Sigmoid).then_inc(m_sig, 1)
                    if j == 0:
                        hi_at(m, 4, G_MERGE + 1 + SLOTS)
                        hi_at(m, 4, G_MERGE + 2 + SLOTS)
                    else:
                        hi_at(m, 4, G_MERGE + 3 + SLOTS)
                act.wait_ge(m_sum, m + 1)
                apart(act)
                act.activation(mh[:, m, :], ma[:, :], ACT.Copy).then_inc(m_hi, 1)

            with act.Fori(0, KT // 4) as i:
                for j in range(4):
                    hi_at(i, 4, G_OUT + j + SLOTS)
                    act.wait_ge(evac, i * 4 + (T_OUT + j + 1))
                    x_tile(2, i * 4 + j, META, V_FFN2)
            rms(2, META)
            with act.Fori(0, FT // 2) as i:
                up(i, 1, G_UP2, T_UP2)

            with act.Fori(0, KT // 2 - 1) as i:
                down(i, 3, G_DOWN2, T_DOWN2, None)
            down(KT // 2 - 1, 3, G_DOWN2, T_DOWN2, None)
            rms(3, META)

        @block.tensor
        def _(pe):
            def chunk_mm(r, slot, kts, k0, total, lhs_hi, lhs_lo, wide_tile, norm=None):
                for k in range(kts):
                    if norm is not None:
                        pe.wait_ge(x_lo, KT * norm + k + 1)
                    first, last = k0 + k == 0, k0 + k == total - 1
                    w_h = wh[:, slot, k * P:(k + 1) * P]
                    w_l = wl[:, slot, k * P:(k + 1) * P]
                    for n, (w, a) in enumerate(((w_h, lhs_hi), (w_h, lhs_lo), (w_l, lhs_hi))):
                        parts = ((0, 0), (HALF, 512)) if wide_tile else ((None, 0),)
                        for src, dst in parts:
                            size = HALF if wide_tile else SEQ
                            off = src if wide_tile else 0
                            mm = pe.matmul(proj[:, r, dst:dst + size], w, a(k0 + k, off, size),
                                           start=first and n == 0, stop=last and n == 2)
                return mm

            def xs(tok0):
                return (lambda k, off, size: xh[:, k, tok0 + off:tok0 + off + size],
                        lambda k, off, size: xl[:, k, tok0 + off:tok0 + off + size])

            def pair(hi_t, lo_t):
                return (lambda k, off, size: hi_t[:, k, off:off + size],
                        lambda k, off, size: lo_t[:, k, off:off + size])

            def tile8(i, t0, g0, src, wide_tile, per=4, norm=None):
                pe.wait_ge(evac, i * per + (t0 - 1))
                pe.wait_ge(w_lo, i * per + (g0 + 1))
                chunk_mm(t0 % 2, g0 % SLOTS, KT, 0, KT, *src, wide_tile, norm).then_inc(w_used, 1)

            def transpose(out, in_):
                return pe.transpose(out, in_, ident[:, :])

            def to_tokens(src, n_chunks, sem_):
                for c in range(n_chunks):
                    transpose(ps[:, 1, c * P:(c + 1) * P], src[:, META + c * P:META + (c + 1) * P])
                transpose(ps[0:META, 1, 512:512 + P], src[:, 0:META]).then_inc(sem_, 1)

            def norm_sum(n, tok0):
                pe.wait_ge(ss_acc, 9 * n + 9)
                if tok0 == 0:
                    pe.matmul(ps[:, 0, 0:HALF], ones[:, :], ssum[:, 0:HALF], start=True, stop=True)
                    pe.matmul(ps[:, 0, 512:512 + HALF], ones[:, :], ssum[:, HALF:NT], start=True, stop=True)\
                      .then_inc(ss_sum, 1)
                else:
                    pe.matmul(ps[:, 0, 0:SEQ], ones[:, :], ssum[:, META:NT], start=True, stop=True)\
                      .then_inc(ss_sum, 1)

            def up(n, g0, t0):
                tok0 = 0 if n == 0 else META
                tile8(0, t0, g0, xs(tok0), tok0 == 0, norm=2 * n)
                if n == 0:
                    pe.wait_ge(setup, 1)
                    pe.wait_ge(consts, 32)
                norm_sum(2 * n, tok0)
                for j in range(1, 4):
                    tile8(0, t0 + j, g0 + j, xs(tok0), tok0 == 0)
                with pe.Fori(0, FT // 2 - 1) as i:
                    for j in range(4, 8):
                        tile8(i, t0 + j, g0 + j, xs(tok0), tok0 == 0)

            def down(n, g0, t0):
                tok0 = 0 if n == 0 else META
                src = (lambda k, off, size: ah[:, k, tok0 + off:tok0 + off + size],
                       lambda k, off, size: al[:, k, tok0 + off:tok0 + off + size])
                with pe.Fori(0, KT // 2) as i:
                    for j in range(2):
                        pe.wait_ge(evac, i * 2 + (t0 + j - 1))
                        k = 0
                        for b, kts in enumerate(DOWN_SPLIT):
                            g = g0 + 4 * j + b
                            pe.wait_ge(w_lo, i * 8 + (g + 1))
                            pe.wait_ge(act_lo, FT * n + k + kts)
                            chunk_mm((t0 + j) % 2, g % SLOTS, kts, k, FT, *src, tok0 == 0).then_inc(w_used, 1)
                            k += kts

            up(0, G_UP1, T_UP1)
            down(0, G_DOWN1, T_DOWN1)

            def gate_z(h):
                if h >= 2:
                    pe.wait_ge(zb_ok, h - 1)
                elif h == 1:
                    pe.wait_ge(iw_ok, 1)
                w = wlr[GLR_ROW:GLR_ROW + LOWRANK, h * DK:(h + 1) * DK]
                x = misc[GLR_ROW:GLR_ROW + LOWRANK, :]
                pe.matmul(ps[:, h % 2, 0:HALF], w, x[:, 0:HALF], start=True, stop=True)
                pe.matmul(ps[:, h % 2, 512:512 + HALF], w, x[:, HALF:NT], start=True, stop=True).then_inc(z_mm, 1)

            tile8(0, T_IDX, G_IDX, xs(0), True, norm=1)
            norm_sum(1, 0)
            tile8(0, T_IDX + 1, G_IDX + 1, xs(META), False)
            pe.wait_ge(evac, T_IDX + 1)
            for i in range(QT):
                mm = transpose(ps[:, 1, i * P:(i + 1) * P], misc[:, META + i * P:META + (i + 1) * P])
            mm.then_inc(iwT_mm, 1)
            tile8(0, T_IDX + 2, G_IDX + 2, xs(META), False)
            pe.wait_ge(consts2, 16 * 6)
            gate_z(0)
            tile8(0, T_IDX + 3, G_IDX + 3, xs(META), False)
            gate_z(1)
            tile8(0, T_IDX + 4, G_IDX + 4, xs(META), False)
            gate_z(2)
            gate_z(3)
            pe.wait_ge(zb_ok, 3)
            pe.matmul(ps[0:DH_HEADS, 0, 0:512], relb[:, :], oneh[:, 0:512], start=True, stop=True)
            pe.matmul(ps[0:DH_HEADS, 0, 512:LINE], relb[:, :], oneh[:, 512:LINE], start=True, stop=True)\
              .then_inc(line_mm, 1)
            pe.wait_ge(ik2_in, 16)
            pe.wait_ge(evac, T_IDX + 5)
            for n in range(QT * IH):
                i, e = divmod(n, IH)
                lo_, keys = 64 * (e % 2), (misc if e % 2 == 0 else ik2)
                if n == 0:
                    pe.wait_ge(line_ok, 1)
                elif n == 1:
                    pe.wait_ge(zb_ok, GH)
                else:
                    pe.wait_ge(s_relu, n - 1)
                w = iq[lo_:lo_ + IDH, e // 2, i * P:(i + 1) * P]
                first = min(WIDTH[i], 512)
                mm = pe.matmul(ps[:, n % 2, 0:first], w, keys[lo_:lo_ + IDH, 0:first], start=True, stop=True)
                if WIDTH[i] > 512:
                    mm = pe.matmul(ps[:, n % 2, 512:NT], w, keys[lo_:lo_ + IDH, 512:NT], start=True, stop=True)
                mm.then_inc(s_mm, 1)
            pe.wait_ge(s_relu, QT * IH)

            with pe.Fori(0, GH) as hd:
                def level(l):
                    if l < len(LEVELS):
                        pe.wait_ge(x_ok, hd * 14 + (2 * l + 2))
                    if l >= 2:
                        pe.wait_ge(a_ok, hd * 8 + (l - 1))
                    for c in range(QT):
                        if l < len(LEVELS):
                            a = b = X[:, l % 2, c * P:(c + 1) * P]
                        else:
                            a, b = kT[:, META + c * P:META + (c + 1) * P], qT[:, c * P:(c + 1) * P]
                        o = (l % 2) * 512 + c * P
                        mm = pe.matmul(ps[:, 0, o:o + P], a, b, start=True, stop=True)
                    mm.then_inc(g_mm, 1)

                tile8(hd, T_GLA, G_GLA, xs(META), False)
                tile8(hd, T_GLA + 1, G_GLA + 1, xs(0), True)
                tile8(hd, T_GLA + 2, G_GLA + 2, xs(0), True)
                for l in range(3):
                    level(l)
                tile8(hd, T_GLA + 3, G_GLA + 3, xs(0), True)
                pe.wait_ge(evac, hd * 4 + (T_GLA + 3))
                to_tokens(vT[:, 0, :], QT, vt_mm)
                for l in range(3, 8):
                    level(l)
                pe.wait_ge(evac, hd * 4 + (T_GLA + 4))
                pe.wait_ge(vt_ok, hd * 4 + 2)
                to_tokens(vT[:, 1, :], QT, vt_mm)
                pe.wait_ge(vt_ok, hd * 4 + 4)
                pe.wait_ge(qk_ok, hd * 2 + 2)
                to_tokens(ke[:, :], QT - 1, kd_mm)
                pe.wait_ge(kd_ok, hd * 2 + 2)
                pe.matmul(ps[:, 1, 0:DV], kdT[0:META, 0, :], V[0:META, 0, :], start=True, stop=True)
                for c in range(1, QT):
                    mm = pe.matmul(ps[:, 1, c * DV:(c + 1) * DV], kdT[:, c, :], V[:, c, :], start=True, stop=True)
                mm.then_inc(u_mm, 1)
                pe.wait_ge(a_ok, hd * 8 + 8)
                for c in range(QT):
                    pe.wait_ge(s_ok, hd * 4 + (c + 1))
                    o = ps[:, 0, c * DV:(c + 1) * DV]
                    pe.matmul(o, A[:, c * P:(c + 1) * P], V[:, c + 1, :], start=True, stop=False)
                    pe.matmul(o, qe[:, c * P:(c + 1) * P], S[:, c % 2, :], start=False, stop=True).then_inc(o_mm, 1)
                pe.wait_ge(on_ok, hd * 4 + 4)
                for j in range(2):
                    for c in range(QT):
                        mm = transpose(ps[:, 1, j * SEQ + c * P:j * SEQ + (c + 1) * P], on[:, c, j * P:(j + 1) * P])
                    mm.then_inc(ot_mm, 1)

            with pe.Fori(0, DH_HEADS) as h:
                def logits(i):
                    if i >= 1:
                        pe.wait_ge(lg_ok, h * 4 + i)
                    w = dqT[:, i * P:(i + 1) * P]
                    first = min(WIDTH[i], 512)
                    if i == 3:
                        pe.wait_ge(yb_lo, h * 4 + 2)
                    mm = pe.matmul(ps[:, 0, 0:first], w, dkT[:, 0:first], start=True, stop=True)
                    if WIDTH[i] > 512:
                        mm = pe.matmul(ps[:, 0, 512:NT], w, dkT[:, 512:NT], start=True, stop=True)
                    mm.then_inc(qk_mm, 1)

                def attend(i):
                    pe.wait_ge(pn_ok, h * 4 + (i + 1))
                    if i == 0:
                        pe.wait_ge(dv_ok, h * 2 + 2)
                    to_tokens(logit[:, i % 2, :], i + 1, pt_mm)
                    pe.wait_ge(pt_ok, h * 8 + (2 * i + 2))
                    if i >= 1:
                        pe.wait_ge(yb_lo, h * 4 + i)
                    if i == 2:
                        pe.wait_ge(lg_ok, h * 4 + 4)
                    y = ps[:, 0, 640:640 + P]
                    pe.matmul(y, dV[0:META, 0, :], pT[0:META, i % 2, 0:P], start=True, stop=False)
                    for j in range(i + 1):
                        mm = pe.matmul(y, dV[:, j + 1, :], pT[:, i % 2, (j + 1) * P:(j + 2) * P],
                                       start=False, stop=j == i)
                    mm.then_inc(pv_mm, 1)

                tile8(h, T_DSA, G_DSA, xs(META), False)
                tile8(h, T_DSA + 1, G_DSA + 1, xs(0), True)
                tile8(h, T_DSA + 2, G_DSA + 2, xs(0), True)
                pe.wait_ge(evac, h * 4 + (T_DSA + 2))
                logits(0)
                pe.wait_ge(evac, h * 4 + (T_DSA + 3))
                to_tokens(dvT[:, :], QT, dv_mm)
                tile8(h, T_DSA + 3, G_DSA + 3, xs(META), False)
                for i in range(QT):
                    if i + 1 < QT:
                        logits(i + 1)
                    attend(i)

            pe.wait_ge(ya_lo, DH_HEADS)
            pe.wait_ge(yb_lo, DH_HEADS * QT)
            with pe.Fori(0, KT) as m:
                tile8(m, T_MERGE, G_MERGE, xs(META), False)
                tile8(m, T_MERGE + 1, G_MERGE + 1, pair(yah, yal), False)
                tile8(m, T_MERGE + 2, G_MERGE + 2, xs(META), False)
                tile8(m, T_MERGE + 3, G_MERGE + 3, pair(ybh, ybl), False)
            pe.wait_ge(m_lo, KT)
            with pe.Fori(0, KT // 4) as i:
                for j in range(4):
                    tile8(i, T_OUT + j, G_OUT + j, pair(mh, ml), False)
            up(1, G_UP2, T_UP2)
            down(1, G_DOWN2, T_DOWN2)
            norm_sum(3, META)

        @block.vector
        def _(dve):
            def col(c, m):
                return vecs[:, c + m:c + m + 1] if isinstance(m, int) else vecs[:, bass.ds(m + c, 1)]

            def x_tile(n, m, tok0, gain):
                dve.wait_ge(squared, m + (8 * n + 1))
                dve.wait_ge(ss_acc, m + (9 * n + 1))
                dve.tensor_tensor(ssum[:, tok0:NT], ssum[:, tok0:NT], sq[:, tok0:NT], ALU.add).then_inc(ss_acc, 1)
                if gain is not None:
                    dve.wait_ge(x_hi, m + (8 * n + 1))
                    dve.scalar_tensor_tensor(out=xl[:, m, tok0:NT], in0=hT[:, m, tok0:NT], scalar=col(gain, m),
                                             in1=f(xh[:, m, tok0:NT]), op0=ALU.mult, op1=ALU.subtract)\
                       .then_inc(x_lo, 1)

            def inv_rms(n, tok0):
                dve.wait_ge(rms_ok, n + 1)
                dve.reciprocal(rstd[:, tok0:NT], sq[:, tok0:NT]).then_inc(rstd_ok, 1)
                if n < 3:
                    dve.memset(ssum[:, :], 0.0).then_inc(ss_acc, 1)
                dve.wait_ge(rstd_ok, n + 1)

            def read_wide(dst, r, scale=None):
                return dve.tensor_tensor(two(dst), wide(r), two(rstd[:, :]), ALU.mult).then_inc(evac, 1)

            def read_seq(dst, r, scale=1.0):
                if scale == 1.0:
                    return dve.tensor_tensor(dst, proj[:, r, 0:SEQ], rstd[:, META:NT], ALU.mult).then_inc(evac, 1)
                return dve.scalar_tensor_tensor(out=dst, in0=proj[:, r, 0:SEQ], scalar=scale, in1=rstd[:, META:NT],
                                                op0=ALU.mult, op1=ALU.mult).then_inc(evac, 1)

            def up(n, g0, t0):
                tok0 = 0 if n == 0 else META
                with dve.Fori(0, FT // 2) as i:
                    for j in range(2):
                        for b, dst in enumerate((zg, zu)):
                            r = (t0 + 2 * j + b) % 2
                            dve.wait_ge(w_used, i * 4 + (g0 + 2 * j + b + 1))
                            if tok0 == 0:
                                read_wide(dst[:, :], r)
                            else:
                                read_seq(dst[:, META:NT], r)
                        dve.wait_ge(sig, i * 2 + (FT * n + j + 1))
                        dve.wait_ge(evac, i * 4 + (t0 + 2 * j + 2))
                        dve.tensor_tensor(zg[:, tok0:NT], zg[:, tok0:NT], sg[:, tok0:NT], ALU.mult).then_inc(gated, 1)
                        dve.wait_ge(gated, i * 2 + (FT * n + j + 1))
                        dve.tensor_tensor(zu[:, tok0:NT], zg[:, tok0:NT], zu[:, tok0:NT], ALU.mult).then_inc(act_f, 1)
                        dve.wait_ge(act_hi, i * 2 + (FT * n + j + 1))
                        dve.tensor_tensor(al[:, i * 2 + j, tok0:NT], zu[:, tok0:NT], f(ah[:, i * 2 + j, tok0:NT]),
                                          ALU.subtract).then_inc(act_lo, 1)
                        dve.wait_ge(act_lo, i * 2 + (FT * n + j + 1))

            def down(n, g0, t0, norm, gain):
                tok0 = 0 if n == 0 else META
                with dve.Fori(0, KT // 2) as i:
                    for j in range(2):
                        m, r = i * 2 + j, (t0 + j) % 2
                        dve.wait_ge(w_used, i * 8 + (g0 + 4 * j + 4))
                        if tok0 == 0:
                            h_, p_ = two(hT[:, m, :]), wide(r)
                        else:
                            h_, p_ = hT[:, m, META:NT], proj[:, r, 0:SEQ]
                        dve.scalar_tensor_tensor(out=h_, in0=p_, scalar=0.5, in1=h_, op0=ALU.mult, op1=ALU.add)\
                           .then_inc(evac, 1)
                        dve.wait_ge(evac, i * 2 + (t0 + j + 1))
                        x_tile(norm, m, tok0, gain)

            dve.memset(eps[:, :], EPS).then_inc(evac, 1)
            dve.memset(rstd[:, :], 0.0).then_inc(evac, 1)
            dve.memset(ssum[:, :], 0.0).then_inc(ss_acc, 1)
            dve.wait_ge(consts, 32)
            for m in range(KT):
                if m % 2 == 0:
                    dve.wait_ge(h_in[m // 2], 16)
                x_tile(0, m, 0, V_FFN1)
            inv_rms(0, 0)
            up(0, G_UP1, T_UP1)
            down(0, G_DOWN1, T_DOWN1, 1, V_MIX)
            inv_rms(1, 0)

            def log_decay(h):
                dve.wait_ge(z_mm, h + 1)
                dve.tensor_scalar(two(zt[:, :]), ps[:, h % 2, :].rearrange("p (b n) -> p b n", b=2)[:, :, 0:HALF],
                                  vecs[:, V_BLR + h:V_BLR + h + 1], None, ALU.add).then_inc(zb_ok, 1)
                dve.wait_ge(zb_ok, h + 1)
                dve.wait_ge(softp, 3 * h + 3)
                dve.scalar_tensor_tensor(out=zt[:, :], in0=zt[:, :], scalar=0.0, in1=t1[:, 1, :], op0=ALU.min,
                                         op1=ALU.subtract).then_inc(ls_ok, 1)
                dve.wait_ge(ls_ok, h + 1)
                dve.tensor_tensor_scan(blog[:, h, :], chunk0[:, :], zt[:, :], 0.0, ALU.mult, ALU.add).then_inc(b_ok, 1)
                dve.wait_ge(b_ok, h + 1)

            dve.wait_ge(w_used, G_IDX + 1)
            read_wide(misc[:, :], T_IDX % 2)
            dve.wait_ge(w_used, G_IDX + 2)
            read_seq(iq[:, 0, :], (T_IDX + 1) % 2)
            dve.wait_ge(iwT_mm, 1)
            dve.tensor_scalar(iwq[:, :, :], ps[:, 1, 0:SEQ].rearrange("p (i n) -> p i n", i=QT)[:, :, IW_ROW:IW_ROW + IH],
                              IH ** -0.5 * IDH ** -0.5, None, ALU.mult).then_inc(iw_ok, 1)
            dve.wait_ge(w_used, G_IDX + 3)
            read_seq(iq[:, 1, :], (T_IDX + 2) % 2)
            dve.wait_ge(consts2, 16 * 6)
            dve.tensor_copy(lvlmask[:, :, :].rearrange("p l n -> p (l n)"), on[:, :, :].rearrange("p c n -> p (c n)"))\
               .then_inc(lvl_ok, 1)
            log_decay(0)
            dve.wait_ge(w_used, G_IDX + 4)
            read_seq(iq[:, 2, :], (T_IDX + 3) % 2)
            log_decay(1)
            dve.wait_ge(w_used, G_IDX + 5)
            read_seq(iq[:, 3, :], (T_IDX + 4) % 2)
            log_decay(2)
            log_decay(3)
            dve.wait_ge(line_mm, 1)
            dve.tensor_copy(line[:, :], ps[0:DH_HEADS, 0, 0:LINE]).then_inc(line_ok, 1)
            dve.wait_ge(iw_ok, 1)
            for n in range(QT * IH):
                i, e = divmod(n, IH)
                s_i = score[:, COL[i]:COL[i] + WIDTH[i]]
                dve.wait_ge(s_relu, n + 1)
                if e == 0:
                    dve.tensor_scalar(s_i, t1[:, n % 2, 0:WIDTH[i]], iwq[:, i, e:e + 1], 0.0, ALU.mult, ALU.add)\
                       .then_inc(s_acc, 1)
                else:
                    dve.wait_ge(s_acc, n)
                    dve.scalar_tensor_tensor(out=s_i, in0=t1[:, n % 2, 0:WIDTH[i]], scalar=iwq[:, i, e:e + 1], in1=s_i,
                                             op0=ALU.mult, op1=ALU.add).then_inc(s_acc, 1)
            dve.wait_ge(s_acc, QT * IH)
            for i in range(QT):
                last = score[:, COL[i] + WIDTH[i] - P:COL[i] + WIDTH[i]]
                dve.tensor_tensor(last, last, triu[:, :], ALU.min).then_inc(tk, 1)
            dve.wait_ge(tk, QT)
            dve.tensor_copy(work[:, :], score[:, :]).then_inc(tk, 1)
            dve.wait_ge(setup, 2)
            dve.wait_ge(lvl_ok, 1)

            ROUNDS = TOPK // 8 // GH
            with dve.Fori(0, GH) as hd:
                def top_rounds(i):
                    w_i = work[:, COL[i]:COL[i] + WIDTH[i]]
                    for n in range(ROUNDS):
                        at_ = QT + 1 + 2 * (i * ROUNDS + n)
                        dve.wait_ge(tk, hd * (2 * QT * ROUNDS) + at_)
                        apart(dve)
                        dve.max(m8[:, i, :], w_i).then_inc(tk, 1)
                        dve.wait_ge(tk, hd * (2 * QT * ROUNDS) + (at_ + 1))
                        apart(dve)
                        dve.match_replace(w_i, m8[:, i, :], w_i, NEG).then_inc(tk, 1)

                def expo(l):
                    m = LEVELS[l]
                    if l >= 2:
                        dve.wait_ge(e_ok, hd * 7 + (l - 1))
                    b = blog[:, hd, META:NT].rearrange("p (b two m) -> p b two m", two=2, m=m)
                    d = Dl[:, l % 2, :].rearrange("p (b two m) -> p b two m", two=2, m=m)
                    ref = b[:, :, 0, m - 1:m].to_broadcast([P, SEQ // (2 * m), m])
                    dve.tensor_tensor(d[:, :, 1, :], b[:, :, 1, :], ref, ALU.subtract).then_inc(d_ok, 1)
                    dve.tensor_tensor(d[:, :, 0, :], ref, b[:, :, 0, :], ALU.subtract).then_inc(d_ok, 1)

                def merge_level(l):
                    dve.wait_ge(g_mm, hd * 8 + (l + 1))
                    o = (l % 2) * 512
                    apart(dve)
                    if l >= 1:
                        dve.wait_ge(a_ok, hd * 8 + l)
                        apart(dve)
                    dve.copy_predicated(A[:, :].rearrange("p (c t) -> p c t", c=QT),
                                        lvlmask[:, l, :].unsqueeze(1).to_broadcast([P, QT, P]),
                                        ps[:, 0, o:o + SEQ].rearrange("p (c t) -> p c t", c=QT)).then_inc(a_ok, 1)

                dve.wait_ge(w_used, hd * 4 + (G_GLA + 1))
                read_seq(qT[:, :], T_GLA % 2, DK ** -0.5)
                dve.wait_ge(w_used, hd * 4 + (G_GLA + 2))
                read_wide(kT[:, :], (T_GLA + 1) % 2)
                expo(0)
                expo(1)
                top_rounds(0)
                expo(2)
                top_rounds(1)
                expo(3)
                dve.wait_ge(w_used, hd * 4 + (G_GLA + 3))
                read_wide(vT[:, 0, :], (T_GLA + 2) % 2)
                merge_level(0)
                expo(4)
                merge_level(1)
                expo(5)
                merge_level(2)
                expo(6)
                for n, (src, size) in enumerate(((blog[:, hd, META:NT], P), (blog[:, hd, 0:META], META))):
                    b = src.rearrange("p (c t) -> p c t", t=size)
                    d = (sq[:, META:NT] if n == 0 else sq[:, 0:META]).rearrange("p (c t) -> p c t", t=size)
                    nch = QT if n == 0 else 1
                    dve.tensor_tensor(d, b, b[:, :, size - 1:size].to_broadcast([P, nch, size]), ALU.subtract)\
                       .then_inc(de_ok, 1)
                top_rounds(2)
                dve.wait_ge(w_used, hd * 4 + (G_GLA + 4))
                read_wide(vT[:, 1, :], (T_GLA + 3) % 2)
                for l in range(3, 8):
                    merge_level(l)
                top_rounds(3)
                dve.wait_ge(u_mm, hd + 1)
                dve.tensor_copy(S[:, 0, :], ps[:, 1, 0:DV]).then_inc(s_ok, 1)
                dve.wait_ge(ex_ok, hd * 3 + 3)
                for c in range(1, QT):
                    dve.wait_ge(s_ok, hd * 4 + c)
                    if c >= 2:
                        dve.wait_ge(o_mm, hd * 4 + (c - 1))
                    dve.scalar_tensor_tensor(out=S[:, c % 2, :], in0=S[:, (c - 1) % 2, :], scalar=eb[:, c - 1:c],
                                             in1=ps[:, 1, c * DV:(c + 1) * DV], op0=ALU.mult, op1=ALU.add)\
                       .then_inc(s_ok, 1)
                dve.wait_ge(orms_ok, hd + 1)
                dve.reciprocal(orstd[:, :], orms[:, :]).then_inc(orstd_ok, 1)
                dve.wait_ge(orstd_ok, hd + 1)
                for c in range(QT):
                    dve.tensor_scalar(on[:, c, :], ps[:, 0, c * DV:(c + 1) * DV], orstd[:, c:c + 1], None, ALU.mult)\
                       .then_inc(on_ok, 1)

            dve.wait_ge(tk, QT + 1 + 2 * QT * (TOPK // 8))
            dve.tensor_tensor(score[:, :], work[:, :], score[:, :], ALU.is_equal).then_inc(tk, 1)
            dve.wait_ge(tk, QT + 2 + 2 * QT * (TOPK // 8))
            dve.wait_ge(ot_ok, 2 * GH)
            dve.tensor_scalar(score[:, :], score[:, :], MASKED, None, ALU.mult).then_inc(mask_ok, 1)
            dve.wait_ge(mask_ok, 1)

            with dve.Fori(0, DH_HEADS) as h:
                def masked(i):
                    w, b = WIDTH[i], i % 2
                    dve.wait_ge(qk_mm, h * 4 + (i + 1))
                    if i >= 2:
                        dve.wait_ge(pt_mm, h * 4 + (i - 1))
                    dve.tensor_tensor(logit[:, b, 0:w], ps[:, 0, 0:w], strip[:, NT - w:NT], ALU.add).then_inc(lg_ok, 1)
                    dve.wait_ge(lg_ok, h * 4 + (i + 1))
                    apart(dve)
                    dve.tensor_tensor_reduce(logit[:, b, 0:w], logit[:, b, 0:w], score[:, COL[i]:COL[i] + w], -1.0,
                                             3.0e38, ALU.add, ALU.min, nmax[:, b:b + 1]).then_inc(lm_ok, 1)

                def normalise(i):
                    w, b = WIDTH[i], i % 2
                    dve.wait_ge(p_ok, h * 4 + (i + 1))
                    dve.reciprocal(rinv[:, b:b + 1], rowsum[:, b:b + 1]).then_inc(ri_ok, 1)
                    dve.wait_ge(ri_ok, h * 4 + (i + 1))
                    dve.tensor_scalar(logit[:, b, 0:w], logit[:, b, 0:w], rinv[:, b:b + 1], None, ALU.mult)\
                       .then_inc(pn_ok, 1)

                def y_low(i):
                    dve.wait_ge(yb_hi, h * 4 + (i + 1))
                    dve.tensor_tensor(ybl[:, h, i * P:(i + 1) * P], ps[:, 0, 640:640 + P],
                                      f(ybh[:, h, i * P:(i + 1) * P]), ALU.subtract).then_inc(yb_lo, 1)

                dve.wait_ge(w_used, h * 4 + (G_DSA + 1))
                read_seq(dqT[:, :], T_DSA % 2, DH ** -0.5)
                dve.wait_ge(w_used, h * 4 + (G_DSA + 2))
                read_wide(dkT[:, :], (T_DSA + 1) % 2)
                dve.wait_ge(w_used, h * 4 + (G_DSA + 3))
                read_wide(dvT[:, :], (T_DSA + 2) % 2)
                dve.wait_ge(strip_in, h * 16 + 16)
                masked(0)
                normalise(0)
                dve.wait_ge(w_used, h * 4 + (G_DSA + 4))
                read_seq(zr[:, :], (T_DSA + 3) % 2)
                for i in range(QT):
                    if i + 1 < QT:
                        masked(i + 1)
                        normalise(i + 1)
                    y_low(i)
                dve.wait_ge(r_sig, h + 1)
                dve.tensor_tensor(sr[:, :], zr[:, :], sr[:, :], ALU.mult).then_inc(r_g, 1)
                dve.wait_ge(r_g, h + 1)
                dve.tensor_tensor(zr[:, :], sr[:, :], oT[:, h, :], ALU.mult).then_inc(ya_f, 1)
                dve.wait_ge(ya_hi, h + 1)
                dve.tensor_tensor(yal[:, h, :], zr[:, :], f(yah[:, h, :]), ALU.subtract).then_inc(ya_lo, 1)

            dve.wait_ge(strip_in, 16 * (DH_HEADS + 1))
            with dve.Fori(0, KT) as m:
                dve.wait_ge(w_used, m * 4 + (G_MERGE + 1))
                read_seq(mz[:, :], T_MERGE % 2)
                dve.wait_ge(w_used, m * 4 + (G_MERGE + 2))
                dve.wait_ge(m_sig, m * 2 + 1)
                dve.tensor_tensor(ma[:, :], proj[:, (T_MERGE + 1) % 2, 0:SEQ], msg[:, :], ALU.mult).then_inc(evac, 1)
                dve.wait_ge(w_used, m * 4 + (G_MERGE + 3))
                read_seq(mz[:, :], (T_MERGE + 2) % 2)
                dve.wait_ge(w_used, m * 4 + (G_MERGE + 4))
                dve.wait_ge(m_sig, m * 2 + 2)
                dve.tensor_tensor(mz[:, :], proj[:, (T_MERGE + 3) % 2, 0:SEQ], msg[:, :], ALU.mult).then_inc(evac, 1)
                dve.wait_ge(evac, m * 4 + (T_MERGE + 4))
                dve.tensor_tensor(ma[:, :], ma[:, :], mz[:, :], ALU.add).then_inc(m_sum, 1)
                dve.wait_ge(m_hi, m + 1)
                dve.tensor_tensor(ml[:, m, :], ma[:, :], f(mh[:, m, :]), ALU.subtract).then_inc(m_lo, 1)

            with dve.Fori(0, KT // 4) as i:
                for j in range(4):
                    m = i * 4 + j
                    dve.wait_ge(w_used, i * 4 + (G_OUT + j + 1))
                    dve.tensor_tensor(hT[:, m, META:NT], proj[:, (T_OUT + j) % 2, 0:SEQ], hT[:, m, META:NT], ALU.add)\
                       .then_inc(evac, 1)
                    dve.wait_ge(evac, i * 4 + (T_OUT + j + 1))
                    x_tile(2, m, META, V_FFN2)
            inv_rms(2, META)
            up(1, G_UP2, T_UP2)
            down(1, G_DOWN2, T_DOWN2, 3, None)
            inv_rms(3, META)
            for m in range(KT):
                dve.scalar_tensor_tensor(out=final[:, m, :], in0=hT[:, m, META:NT], scalar=col(V_FINAL, m),
                                         in1=rstd[:, META:NT], op0=ALU.mult, op1=ALU.mult).then_inc(out_ok, 1)


def rel_bucket(dist):
    n = np.maximum(dist, 0)
    exact = BUCKETS // 2
    nf = np.maximum(n, exact).astype(np.float32)
    large = exact + (np.log(nf / np.float32(exact)) / np.float32(math.log(MAX_DIST / exact))
                     * np.float32(BUCKETS - exact)).astype(np.int32)
    return np.where(n < exact, n, np.minimum(large, BUCKETS - 1))


def constants():
    p, t = np.arange(P)[:, None], np.arange(P)[None, :]
    masks = []
    for m in LEVELS:
        same = p // (2 * m) == t // (2 * m)
        masks.append(same & (p // m % 2 == 0) & (t // m % 2 == 1))
    masks.append(p == t)
    bucket = rel_bucket(NT - 1 - np.arange(LINE))
    chunk0 = np.ones((P, NT), np.float32)
    chunk0[:, [0] + [META + P * c for c in range(QT)]] = 0.0
    return {
        "ident": np.eye(P, dtype=np.float32),
        "lvlmask": np.stack(masks, 1).astype(np.float32).reshape(P, -1),
        "triu": np.where(t <= p, -NEG, NEG).astype(np.float32),
        "chunk0": chunk0,
        "oneh": (np.arange(BUCKETS)[:, None] == bucket[None, :]).astype(np.float32),
    }


def feature_tiles(w, cols=None):
    k, m = w.shape
    return np.ascontiguousarray(w.reshape(k // P, P, m // P, P).transpose(2, 1, 0, 3).reshape(m // P, P, k))


def lay_out(inputs):
    g = {n: np.asarray(a) for n, a in inputs.items()}
    w_in = g["w_in"][0]
    sizes = (GH * DK, GH * DK, GH * DV, GH * DV, LOWRANK, D, D, D, IH * IDH, IDH, IH, D, D)
    cuts = np.cumsum((0,) + sizes)
    gq, gk, gv, gr, glr, dq, dk, dv, iq, ik, iw, ga, gb = (w_in[:, a:b] for a, b in zip(cuts[:-1], cuts[1:]))
    misc = np.zeros((D, P), np.float32)
    misc[:, 0:IDH], misc[:, GLR_ROW:GLR_ROW + LOWRANK], misc[:, IW_ROW:IW_ROW + IH] = ik, glr, iw
    order = [misc, iq]
    for h in range(GH):
        order += [gq[:, h * DK:(h + 1) * DK], gk[:, h * DK:(h + 1) * DK], gv[:, h * DV:(h + 1) * DV]]
    for h in range(DH_HEADS):
        order += [x[:, h * P:(h + 1) * P] for x in (dq, dk, dv, gr)]
    for m in range(KT):
        order += [x[:, m * P:(m + 1) * P] for x in (ga, g["w_up_a"][0], gb, g["w_up_b"][0])]
    order.append(g["w_out"][0])
    out = {"w_mix": feature_tiles(np.concatenate(order, axis=1))}
    for n in (1, 2):
        gate, up = g[f"ffn{n}_w_gate"][0], g[f"ffn{n}_w_up"][0]
        both = np.stack([gate.reshape(D, FT, P), up.reshape(D, FT, P)], axis=2).reshape(D, 2 * DFF)
        out[f"w_up{n}"] = feature_tiles(both)
        out[f"w_down{n}"] = feature_tiles(g[f"ffn{n}_w_down"][0])
    tokens = np.concatenate([g["meta_tokens"], g["x"][0]], axis=0)
    out["xT"] = np.ascontiguousarray(tokens.T.reshape(KT, P, NT).transpose(1, 0, 2))
    vectors = [g["norm_ffn1"][0], g["norm_mix"][0], g["norm_ffn2"][0], g["norm_final"], g["gla_norm"][0],
               g["gla_b_lr"][0]]
    out["vecs"] = np.ascontiguousarray(np.concatenate(vectors).reshape(NVEC, P).T)
    out["w_lr"] = np.ascontiguousarray(g["gla_w_lr"][0])
    out["rel_bias"] = np.ascontiguousarray(g["rel_bias"])
    return {**out, **constants()}


def kernel(**inputs):
    import concourse.bacc as bacc
    from concourse.bass_utils import run_bass_kernel_spmd

    arrays = lay_out(inputs)
    nc = bacc.Bacc("TRN2", target_bir_lowering=False, num_devices=1)
    io = {n: nc.dram_tensor(f"in_{n}", a.shape, mybir.dt.from_np(a.dtype), kind="ExternalInput").ap()
          for n, a in arrays.items()}
    io["outT"] = nc.dram_tensor("outT", (KT, P, SEQ), F32, kind="ExternalOutput").ap()
    build(nc, io)
    r = run_bass_kernel_spmd(nc, [{f"in_{n}": a for n, a in arrays.items()}], core_ids=[0])
    got = r.results[0]["outT"]
    return np.ascontiguousarray(got.reshape(D, SEQ).T.reshape(1, SEQ, D))
```

```python
import math
from contextlib import ExitStack

import numpy as np

import concourse.bass as bass
from concourse import mybir

F32 = mybir.dt.float32
F32R = mybir.dt.float32r
U8 = mybir.dt.uint8
ACT = mybir.ActivationFunctionType
ALU = mybir.AluOpType
AX = mybir.AxisListType

P = 128
D = 1024
KT = D // P
SEQ = 512
META = 16
NT = SEQ + META
HALF = NT // 2
DFF = 2816
FT = DFF // P
DOWN_SPLIT = (6, 6, 5, 5)
EPS = 1e-6
GH, DK, DV = 4, 128, 256
LOWRANK = 16
TAU = 16.0
DH_HEADS, DH = 8, 128
IH, IDH = 8, 64
TOPK = min(256, SEQ // 4)
BUCKETS, MAX_DIST = 32, 128
QT = SEQ // P
LEVELS = (64, 32, 16, 8, 4, 2, 1)
NEG = -3.0e38
MASKED = -1.0e30
GLR_ROW, IW_ROW = 64, 96
WIDTH = [META + P * (i + 1) for i in range(QT)]
COL = [sum(WIDTH[:i]) for i in range(QT)]
LINE = NT + P
SLOTS = 4
BLOCK = KT * P

V_FFN1, V_MIX, V_FFN2, V_FINAL, V_GLA, V_BLR = 0, 8, 16, 24, 32, 34
NVEC = V_BLR + GH

G_UP1 = 0
G_DOWN1 = G_UP1 + 2 * FT
G_IDX = G_DOWN1 + 4 * KT
G_GLA = G_IDX + 5
G_DSA = G_GLA + 4 * GH
G_MERGE = G_DSA + 4 * DH_HEADS
G_OUT = G_MERGE + 4 * KT
G_UP2 = G_OUT + KT
G_DOWN2 = G_UP2 + 2 * FT
G_END = G_DOWN2 + 4 * KT
T_UP1 = 2
T_DOWN1 = T_UP1 + 2 * FT
T_IDX = T_DOWN1 + KT
T_GLA = T_IDX + 5
T_DSA = T_GLA + 4 * GH
T_MERGE = T_DSA + 4 * DH_HEADS
T_OUT = T_MERGE + 4 * KT
T_UP2 = T_OUT + KT
T_DOWN2 = T_UP2 + 2 * FT


def build(nc, io):
    ctx = ExitStack()
    with ctx:
        def sem(name):
            return ctx.enter_context(nc.semaphore(name))

        arena_bytes = 212800
        base = (nc.sbuf_base + 31) // 32 * 32
        ctx.enter_context(nc.sbuf_tensor("arena", [P, arena_bytes // 4], F32))
        top = [0]

        def at(name, shape, dt, off):
            size = int(np.prod(shape[1:])) * (1 if dt == U8 else 4)
            assert off % 32 == 0 and off + size <= arena_bytes, (name, off, size)
            return nc.alloc_sbuf_tensor_at(name, shape, dt, offset=base + off), off + (size + 31) // 32 * 32

        def keep(name, shape, dt=F32):
            t, top[0] = at(name, shape, dt, top[0])
            return t

        hT = keep("hT", [P, KT, NT])
        xh = keep("xh", [P, KT, NT], F32R)
        xl = keep("xl", [P, KT, NT], F32R)
        rstd = keep("rstd", [P, NT])
        ssum = keep("ssum", [P, NT])
        wraw = keep("wraw", [P, SLOTS, BLOCK])
        wh = keep("wh", [P, SLOTS, BLOCK], F32R)
        wl = keep("wl", [P, SLOTS, BLOCK], F32R)
        vecs = keep("vecs", [P, NVEC])
        ones = keep("ones", [P, P])
        ident = keep("ident", [P, P])
        eps = keep("eps", [P, 1])
        sq = keep("sq", [P, NT])
        FREE = top[0]

        def region(start):
            cur = [start]

            def put(name, shape, dt=F32):
                t, cur[0] = at(name, shape, dt, cur[0])
                return t
            put.here = lambda: cur[0]
            return put

        put = region(FREE)
        ah = put("ah", [P, FT, NT], F32R)
        al = put("al", [P, FT, NT], F32R)
        zg = put("zg", [P, NT])
        sg = put("sg", [P, NT])
        zu = put("zu", [P, NT])
        put = region(FREE)
        oT = put("oT", [P, KT, SEQ])
        yah, _ = at("yah", [P, KT, SEQ], F32R, FREE)
        Y = put.here()
        yal = put("yal", [P, KT, SEQ], F32R)
        ybh = put("ybh", [P, KT, SEQ], F32R)
        ybl = put("ybl", [P, KT, SEQ], F32R)
        score = put("score", [P, sum(WIDTH)])
        DS = put.here()
        dput = region(DS)
        work = dput("work", [P, sum(WIDTH)])
        pT, _ = at("pT", [P, 2, (QT + 1) * P], F32, DS)
        dqT = dput("dqT", [P, SEQ])
        dkT = dput("dkT", [P, NT])
        dvT = dput("dvT", [P, NT])
        dV = dput("dV", [P, QT + 1, DH])
        strip = dput("strip", [P, NT])
        logit = dput("logit", [P, 2, NT])
        zr = dput("zr", [P, SEQ])
        sr = dput("sr", [P, SEQ])
        nmax = dput("nmax", [P, 2])
        rowsum = dput("rowsum", [P, 2])
        rinv = dput("rinv", [P, 2])
        on = dput("on", [P, QT, DV])
        mput = region(DS - 4 * sum(WIDTH))
        mh = mput("mh", [P, KT, SEQ], F32R)
        ml = mput("ml", [P, KT, SEQ], F32R)
        assert mput.here() >= dput.here() - 4 * QT * DV - 32, "the first gates come before the last head is done"
        sga, sgb, ma = (mput(n, [P, SEQ]) for n in ("sga", "sgb", "ma"))
        gput = region(Y)
        blog = gput("blog", [P, GH, NT])
        qT = gput("qT", [P, SEQ])
        kT = gput("kT", [P, NT])
        vT = gput("vT", [P, 2, NT])
        V = gput("V", [P, QT + 1, DV])
        x_at = gput.here()
        X = gput("X", [P, 2, SEQ])
        E = gput("E", [P, 2, SEQ])
        Dl = gput("Dl", [P, 2, SEQ])
        A = gput("A", [P, SEQ])
        S = gput("S", [P, QT, DV])
        sp, _ = at("sp", [P, GH, NT], F32, x_at)
        lvlmask = gput("lvlmask", [P, len(LEVELS) + 1, P], U8)
        eb = gput("eb", [P, QT])
        ossq = gput("ossq", [P, QT])
        orms = gput("orms", [P, QT])
        orstd = gput("orstd", [P, QT])
        m8 = gput("m8", [P, QT, 8])
        iwq = gput("iwq", [P, QT, IH])
        triu = gput("triu", [P, P])
        qe = gput("qe", [P, SEQ])
        ke = gput("ke", [P, NT])
        kdT = gput("kdT", [P, QT, P])
        assert gput.here() <= DS - 4 * sum(WIDTH)
        iput = region(FREE)
        iq = iput("iq", [P, 4, SEQ])
        misc = iput("misc", [P, NT])
        iput = region(DS + (sum(WIDTH) * 4 + 31) // 32 * 32)
        ik2 = iput("ik2", [P, NT])
        t1 = iput("t1", [P, 2, NT])
        chunk0 = iput("chunk0", [P, NT])
        wlr = iput("wlr", [P, GH * DK])
        relb = iput("relb", [BUCKETS, DH_HEADS])
        oneh = iput("oneh", [BUCKETS, LINE])
        line = iput("line", [DH_HEADS, LINE])
        final, _ = at("final", [P, KT, SEQ], F32, FREE)

        proj = ctx.enter_context(nc.psum_tensor("proj", [P, 2, 1024], F32))
        ps = ctx.enter_context(nc.psum_tensor("ps", [P, 2, 1024], F32))

        bias_line = nc.dram_tensor("bias_line", (DH_HEADS, LINE), F32)
        bias_strip = nc.dram_tensor("bias_strip", (DH_HEADS, P, NT), F32)

        def wide(r):
            return proj[:, r, :].rearrange("p (b n) -> p b n", b=2)[:, :, 0:HALF]

        def two(x):
            return x.rearrange("p (b n) -> p b n", b=2)

        def f(x):
            return x.bitcast(F32)

        consts = sem("consts")
        consts2 = sem("consts2")
        h_in = [sem(f"h_in{n}") for n in range(KT // 2)]
        w_in = [sem(f"w_in{s}") for s in range(SLOTS)]
        w_hi = sem("w_hi")
        w_lo = sem("w_lo")
        w_used = sem("w_used")
        evac = sem("evac")
        x_hi = sem("x_hi")
        x_lo = sem("x_lo")
        squared = sem("squared")
        ss_acc = sem("ss_acc")
        ss_sum = sem("ss_sum")
        rms_ok = sem("rms_ok")
        rstd_ok = sem("rstd_ok")
        setup = sem("setup")
        sig = sem("sig")
        gated = sem("gated")
        act_f = sem("act_f")
        act_hi = sem("act_hi")
        act_lo = sem("act_lo")
        iwT_mm = sem("iwT_mm")
        iw_ok = sem("iw_ok")
        ik2_in = sem("ik2_in")
        z_mm = sem("z_mm")
        lvl_ok = sem("lvl_ok")
        zb_ok = sem("zb_ok")
        softp = sem("softp")
        ls_ok = sem("ls_ok")
        b_ok = sem("b_ok")
        line_mm = sem("line_mm")
        line_ok = sem("line_ok")
        line_st = sem("line_st")
        s_mm = sem("s_mm")
        s_relu = sem("s_relu")
        s_acc = sem("s_acc")
        tk = sem("tk")
        mask_ok = sem("mask_ok")
        d_ok = sem("d_ok")
        e_ok = sem("e_ok")
        x_ok = sem("x_ok")
        g_mm = sem("g_mm")
        a_ok = sem("a_ok")
        vt_mm = sem("vt_mm")
        vt_ok = sem("vt_ok")
        de_ok = sem("de_ok")
        ex_ok = sem("ex_ok")
        qk_ok = sem("qk_ok")
        kd_mm = sem("kd_mm")
        kd_ok = sem("kd_ok")
        u_mm = sem("u_mm")
        s_ok = sem("s_ok")
        o_mm = sem("o_mm")
        oss_ok = sem("oss_ok")
        orms_ok = sem("orms_ok")
        orstd_ok = sem("orstd_ok")
        on_ok = sem("on_ok")
        ot_mm = sem("ot_mm")
        ot_ok = sem("ot_ok")
        strip_in = sem("strip_in")
        dv_mm = sem("dv_mm")
        dv_ok = sem("dv_ok")
        qk_mm = sem("qk_mm")
        lg_ok = sem("lg_ok")
        lm_ok = sem("lm_ok")
        p_ok = sem("p_ok")
        ri_ok = sem("ri_ok")
        pn_ok = sem("pn_ok")
        pt_mm = sem("pt_mm")
        pt_ok = sem("pt_ok")
        pv_mm = sem("pv_mm")
        yb_hi = sem("yb_hi")
        yb_lo = sem("yb_lo")
        r_sig = sem("r_sig")
        r_g = sem("r_g")
        ya_f = sem("ya_f")
        ya_hi = sem("ya_hi")
        ya_lo = sem("ya_lo")
        m_sig = sem("m_sig")
        m_sum = sem("m_sum")
        m_hi = sem("m_hi")
        m_lo = sem("m_lo")
        out_ok = sem("out_ok")
        out_st = sem("out_st")
        carried = sem("carried")

        def apart(eng):
            eng.sem_inc(carried, 1)

        block = ctx.enter_context(nc.Block())

        @block.sync
        def _(sp):
            def load(g, src, cols=BLOCK):
                slot = g % SLOTS
                if g >= SLOTS:
                    sp.wait_ge(w_lo, g - SLOTS + 1)
                sp.dma_start(wraw[:, slot, 0:cols], src).then_inc(w_in[slot], 16)

            def load_loop(g0, n, src):
                with sp.Fori(0, n) as i:
                    for j in range(4):
                        row = sp.snap(i * 4 + j)
                        free = sp.snap(i * 4 + (g0 + j - SLOTS + 1))
                        slot = (g0 + j) % SLOTS
                        sp.wait_ge(w_lo, free)
                        sp.dma_start(wraw[:, slot, :], src[row]).then_inc(w_in[slot], 16)

            def load_down(g0, src):
                with sp.Fori(0, KT) as m:
                    k = 0
                    row = sp.snap(m * 1)
                    for j, n in enumerate(DOWN_SPLIT):
                        free = sp.snap(m * 4 + (g0 + j - SLOTS + 1))
                        slot = (g0 + j) % SLOTS
                        sp.wait_ge(w_lo, free)
                        sp.dma_start(wraw[:, slot, 0:n * P], src[row][:, k * P:(k + n) * P])\
                          .then_inc(w_in[slot], 16)
                        k += n

            load(0, io["w_up1"][0])
            for n in range(KT // 2):
                sp.dma_start(hT[:, 2 * n:2 * n + 2, :], io["xT"][:, 2 * n:2 * n + 2, :]).then_inc(h_in[n], 16)
                if n < SLOTS - 1:
                    load(n + 1, io["w_up1"][n + 1])
            load_loop(SLOTS, 2 * FT // 4 - 1, io["w_up1"][SLOTS:])
            load_down(G_DOWN1, io["w_down1"])
            for j in range(5):
                load(G_IDX + j, io["w_mix"][j])
                if j == 3:
                    sp.wait_ge(w_used, G_IDX)
                    sp.dma_start(on[:, :, :].rearrange("p c n -> p (c n)"), io["lvlmask"]).then_inc(consts2, 16)
                    sp.dma_start(triu[:, :], io["triu"]).then_inc(consts2, 16)
                    sp.dma_start(chunk0[:, :], io["chunk0"]).then_inc(consts2, 16)
                    sp.dma_start(wlr[GLR_ROW:GLR_ROW + LOWRANK, :], io["w_lr"]).then_inc(consts2, 16)
                    sp.dma_start(relb[:, :], io["rel_bias"]).then_inc(consts2, 16)
                    sp.dma_start(oneh[:, :], io["oneh"]).then_inc(consts2, 16)
            load_loop(G_GLA, (G_UP2 - G_GLA) // 4, io["w_mix"][5:])
            load_loop(G_UP2, 2 * FT // 4, io["w_up2"])
            load_down(G_DOWN2, io["w_down2"])
            for m in range(KT):
                sp.wait_ge(out_ok, m + 1)
                sp.dma_start(io["outT"][m], final[:, m, :]).then_inc(out_st, 16)
            sp.wait_ge(out_st, 16 * KT)

        @block.gpsimd
        def _(pool):
            def lo(g, slot):
                pool.wait_ge(w_hi, g + 1)
                pool.tensor_tensor(wl[:, slot, :], wraw[:, slot, :], f(wh[:, slot, :]), ALU.subtract)\
                    .then_inc(w_lo, 1)

            def lo_loop(g0, n):
                with pool.Fori(0, n) as i:
                    for j in range(4):
                        lo(i * 4 + (g0 + j), (g0 + j) % SLOTS)

            pool.memset(ones[:, :], 1.0).then_inc(setup, 1)
            for g in range(SLOTS):
                lo(g, g)
            lo_loop(SLOTS, G_GLA // 4 + 1)
            for g in range(2 * SLOTS + G_GLA // 4 * 4, G_GLA + 2 * SLOTS):
                lo(g, g % SLOTS)
            pool.memset(A[:, :], 0.0).then_inc(setup, 1)

            with pool.Fori(0, GH) as hd:
                def level(l):
                    m = LEVELS[l]
                    if l >= 2:
                        pool.wait_ge(g_mm, hd * 8 + (l - 1))
                    pool.wait_ge(e_ok, hd * 7 + (l + 1))
                    v = {n: x.rearrange("p (b two m) -> p b two m", two=2, m=m) for n, x in
                         (("q", qT[:, :]), ("k", kT[:, META:NT]), ("E", E[:, l % 2, :]), ("X", X[:, l % 2, :]))}
                    pool.tensor_tensor(v["X"][:, :, 1, :], v["q"][:, :, 1, :], v["E"][:, :, 1, :], ALU.mult)\
                        .then_inc(x_ok, 1)
                    pool.tensor_tensor(v["X"][:, :, 0, :], v["k"][:, :, 0, :], v["E"][:, :, 0, :], ALU.mult)\
                        .then_inc(x_ok, 1)

                pool.wait_ge(evac, hd * 4 + (T_GLA + 4))
                for l in range(len(LEVELS)):
                    level(l)
                pool.wait_ge(ex_ok, hd * 3 + 1)
                pool.tensor_tensor(qe[:, :], qT[:, :], E[:, 1, :], ALU.mult).then_inc(qk_ok, 1)
                pool.wait_ge(ex_ok, hd * 3 + 2)
                pool.tensor_tensor(ke[:, :], kT[:, :], sq[:, :], ALU.mult).then_inc(qk_ok, 1)
                for j in range(4):
                    lo(hd * 4 + (G_GLA + 2 * SLOTS + j), (G_GLA + j) % SLOTS)

            lo_loop(G_DSA + 2 * SLOTS, (G_END - G_DSA - 2 * SLOTS) // 4)

        @block.scalar
        def _(act):
            act.dma_start(vecs[:, :], io["vecs"]).then_inc(consts, 16)
            act.dma_start(ident[:, :], io["ident"]).then_inc(consts, 16)

            def hi(g, slot):
                lap = g // SLOTS if isinstance(g, int) else None
                act.wait_ge(w_in[slot], 16 * (lap + 1))
                if g >= SLOTS:
                    act.wait_ge(w_used, g - SLOTS + 1)
                act.activation(wh[:, slot, :], wraw[:, slot, :], ACT.Copy).then_inc(w_hi, 1)

            def hi_at(i, per, g0):
                if isinstance(i, int):
                    if i * per + g0 < G_END:
                        hi(i * per + g0, g0 % SLOTS)
                    return
                slot = g0 % SLOTS
                act.wait_ge(w_in[slot], i * (16 * per // SLOTS) + 16 * (g0 // SLOTS + 1))
                act.wait_ge(w_used, i * per + (g0 - SLOTS + 1))
                act.activation(wh[:, slot, :], wraw[:, slot, :], ACT.Copy).then_inc(w_hi, 1)

            def x_tile(n, m, lo_tok, gain):
                if gain is not None:
                    apart(act)
                    act.activation(xh[:, m, lo_tok:NT], hT[:, m, lo_tok:NT], ACT.Copy,
                                   scale=vecs[:, gain + m:gain + m + 1] if isinstance(m, int)
                                   else vecs[:, bass.ds(m + gain, 1)]).then_inc(x_hi, 1)
                act.wait_ge(ss_acc, m + (9 * n + 1))
                apart(act)
                act.activation(sq[:, lo_tok:NT], hT[:, m, lo_tok:NT], ACT.Square).then_inc(squared, 1)

            def rms(n, lo_tok):
                act.wait_ge(ss_sum, n + 1)
                if lo_tok == 0:
                    act.activation(two(sq[:, :]), ps[:, 0, :].rearrange("p (b n) -> p b n", b=2)[:, :, 0:HALF],
                                   ACT.Sqrt, bias=eps[:, :], scale=1.0 / D).then_inc(rms_ok, 1)
                else:
                    act.activation(sq[:, META:NT], ps[:, 0, 0:SEQ], ACT.Sqrt, bias=eps[:, :], scale=1.0 / D)\
                       .then_inc(rms_ok, 1)

            def up(i, n, g0, t0):
                for j in range(2):
                    ft = i * 2 + j
                    hi_at(i, 4, g0 + 2 * j + SLOTS)
                    act.wait_ge(evac, i * 4 + (t0 + 2 * j + 1))
                    act.activation(sg[:, lo_tok_of(n):NT], zg[:, lo_tok_of(n):NT], ACT.Sigmoid).then_inc(sig, 1)
                    act.wait_ge(act_f, i * 2 + (FT * n + j + 1))
                    apart(act)
                    act.activation(ah[:, ft, lo_tok_of(n):NT], zu[:, lo_tok_of(n):NT], ACT.Copy).then_inc(act_hi, 1)
                    hi_at(i, 4, g0 + 2 * j + 1 + SLOTS)

            def down(i, n, g0, t0, gain):
                for j in range(2):
                    for b in range(4):
                        hi_at(i, 8, g0 + 4 * j + b + SLOTS)
                    act.wait_ge(evac, i * 2 + (t0 + j + 1))
                    x_tile(n, i * 2 + j, lo_tok_of(n - 1), gain)

            def lo_tok_of(n):
                return 0 if n == 0 else META

            act.wait_ge(consts, 16 * 2)
            act.wait_ge(evac, 2)
            hi(0, 0)
            for m in range(KT):
                if m % 2 == 0:
                    act.wait_ge(h_in[m // 2], 16)
                x_tile(0, m, 0, V_FFN1)
                if m % 2 == 1 and m // 2 + 1 < SLOTS:
                    hi(m // 2 + 1, m // 2 + 1)
            rms(0, 0)
            with act.Fori(0, FT // 2) as i:
                up(i, 0, G_UP1, T_UP1)
            with act.Fori(0, KT // 2) as i:
                down(i, 1, G_DOWN1, T_DOWN1, V_MIX)
            rms(1, 0)

            def hi_next(j):
                hi_at(0, 4, G_IDX + j + SLOTS)

            hi_next(0)
            act.wait_ge(evac, T_IDX + 1)
            act.dma_start(ik2[64:128, :], misc[0:64, :]).then_inc(ik2_in, 16)
            for j in range(1, 4):
                hi_next(j)
            act.wait_ge(zb_ok, GH)
            act.activation(sp[:, :, :], blog[:, :, :], ACT.Abs).then_inc(softp, 1)
            act.wait_ge(softp, 1)
            act.activation(sp[:, :, :], sp[:, :, :], ACT.Exp, scale=-1.0).then_inc(softp, 1)
            act.wait_ge(softp, 2)
            act.activation(sp[:, :, :], sp[:, :, :], ACT.Ln, bias=1.0).then_inc(softp, 1)
            hi_next(4)
            act.wait_ge(line_ok, 1)
            act.dma_start(bias_line.ap(), line[:, :]).then_inc(line_st, 16)
            for i in range(QT):
                hi_next(5 + i)
                for n in range(i * IH, (i + 1) * IH):
                    act.wait_ge(s_mm, n + 1)
                    if n >= 2:
                        act.wait_ge(s_acc, n - 1)
                    act.activation(t1[:, n % 2, 0:WIDTH[i]], ps[:, n % 2, 0:WIDTH[i]], ACT.Relu).then_inc(s_relu, 1)
                if i == 1:
                    act.wait_ge(line_st, 16)
                    act.dma_start(bias_strip.ap(), bass.AP(bias_line, P - 1, [[LINE, DH_HEADS], [-1, P], [1, NT]]))\
                       .then_inc(line_st, 16)
            act.wait_ge(line_st, 32)
            act.dma_start(strip[:, :], bias_strip.ap()[0]).then_inc(strip_in, 16)

            def level(hd, l):
                act.wait_ge(d_ok, hd * 14 + (2 * l + 2))
                if l >= 2:
                    act.wait_ge(x_ok, hd * 14 + 2 * (l - 1))
                act.activation(E[:, l % 2, :], Dl[:, l % 2, :], ACT.Exp, scale=1.0 / TAU).then_inc(e_ok, 1)

            level(0, 0)
            level(0, 1)

            def gla_head(hd, last=False):
                def copy_v(j):
                    act.wait_ge(vt_mm, hd * 2 + (j + 1))
                    act.activation(V[:, 1:QT + 1, j * P:(j + 1) * P],
                                   ps[:, 1, 0:QT * P].rearrange("p (c n) -> p c n", c=QT), ACT.Copy).then_inc(vt_ok, 1)
                    act.activation(V[0:META, 0, j * P:(j + 1) * P], ps[0:META, 1, 512:512 + P], ACT.Copy)\
                       .then_inc(vt_ok, 1)

                level(hd, 2)
                level(hd, 3)
                copy_v(0)
                level(hd, 4)
                copy_v(1)
                for l in range(5, 7):
                    level(hd, l)
                hi_at(hd, 4, G_GLA + 2 * SLOTS)
                act.wait_ge(x_ok, hd * 14 + 12)
                apart(act)
                act.activation(E[:, 1, :], blog[:, hd, META:NT], ACT.Exp, scale=1.0 / TAU).then_inc(ex_ok, 1)
                act.wait_ge(de_ok, hd * 2 + 2)
                act.activation(sq[:, :], sq[:, :], ACT.Exp, scale=-1.0 / TAU).then_inc(ex_ok, 1)
                apart(act)
                act.activation(eb[:, :], blog[:, hd, META:NT].rearrange("p (c t) -> p c t", c=QT)[:, :, P - 1],
                               ACT.Exp, scale=1.0 / TAU).then_inc(ex_ok, 1)
                act.wait_ge(kd_mm, hd + 1)
                act.activation(kdT[:, 1:QT, :], ps[:, 1, 0:(QT - 1) * P].rearrange("p (c n) -> p c n", c=QT - 1),
                               ACT.Copy).then_inc(kd_ok, 1)
                act.activation(kdT[0:META, 0, :], ps[0:META, 1, 512:512 + P], ACT.Copy).then_inc(kd_ok, 1)
                hi_at(hd, 4, G_GLA + 2 * SLOTS + 1)
                if not last:
                    act.wait_ge(qk_ok, hd * 2 + 2)
                    level(hd + 1, 0)
                    level(hd + 1, 1)
                hi_at(hd, 4, G_GLA + 2 * SLOTS + 2)
                for c in range(QT):
                    act.wait_ge(o_mm, hd * 4 + (c // 2 * 2 + 2))
                    act.activation(sq[:, 0:DV], ps[:, 0, c * DV:(c + 1) * DV], ACT.Square,
                                   accum_out=ossq[:, c:c + 1]).then_inc(oss_ok, 1)
                    act.wait_ge(oss_ok, hd * 4 + (c + 1))
                act.activation(orms[:, :], ossq[:, :], ACT.Sqrt, bias=eps[:, :], scale=1.0 / DV).then_inc(orms_ok, 1)
                hi_at(hd, 4, G_GLA + 2 * SLOTS + 3)
                for j in range(2):
                    act.wait_ge(ot_mm, hd * 2 + (j + 1))
                    apart(act)
                    act.activation(oT[:, hd * 2 + j, :], ps[:, 1, j * SEQ:(j + 1) * SEQ], ACT.Copy,
                                   scale=vecs[:, V_GLA + j:V_GLA + j + 1]).then_inc(ot_ok, 1)

            with act.Fori(0, GH - 1) as hd:
                gla_head(hd)
            gla_head(GH - 1, last=True)

            def dsa_head(h, last=False):
                def softmax(i):
                    w = WIDTH[i]
                    act.wait_ge(lm_ok, h * 4 + (i + 1))
                    act.activation(logit[:, i % 2, 0:w], logit[:, i % 2, 0:w], ACT.Exp, scale=-1.0,
                                   bias=nmax[:, i % 2:i % 2 + 1], accum_out=rowsum[:, i % 2:i % 2 + 1])\
                       .then_inc(p_ok, 1)

                def copy_p(i):
                    act.wait_ge(pt_mm, h * 4 + (i + 1))
                    act.activation(pT[:, i % 2, P:P + (i + 1) * P], ps[:, 1, 0:(i + 1) * P], ACT.Copy)\
                       .then_inc(pt_ok, 1)
                    act.activation(pT[0:META, i % 2, 0:P], ps[0:META, 1, 512:512 + P], ACT.Copy)\
                       .then_inc(pt_ok, 1)

                def y_high(i):
                    act.wait_ge(pv_mm, h * 4 + (i + 1))
                    apart(act)
                    act.activation(ybh[:, h, i * P:(i + 1) * P], ps[:, 0, 640:640 + P], ACT.Copy).then_inc(yb_hi, 1)

                def next_hi(j):
                    hi_at(h, 4, G_DSA + 2 * SLOTS + j)

                act.wait_ge(dv_mm, h + 1)
                act.activation(dV[:, 1:QT + 1, :], ps[:, 1, 0:QT * P].rearrange("p (c n) -> p c n", c=QT), ACT.Copy)\
                   .then_inc(dv_ok, 1)
                act.activation(dV[0:META, 0, :], ps[0:META, 1, 512:512 + P], ACT.Copy).then_inc(dv_ok, 1)
                softmax(0)
                softmax(1)
                next_hi(0)
                copy_p(0)
                y_high(0)
                copy_p(1)
                softmax(2)
                softmax(3)
                if not last:
                    act.dma_start(strip[:, :], bias_strip.ap()[h + 1]).then_inc(strip_in, 16)
                act.activation(sr[:, :], zr[:, :], ACT.Sigmoid).then_inc(r_sig, 1)
                if not last:
                    next_hi(1)
                y_high(1)
                act.wait_ge(ya_f, h + 1)
                apart(act)
                act.activation(yah[:, h, :], zr[:, :], ACT.Copy).then_inc(ya_hi, 1)
                copy_p(2)
                next_hi(1 if last else 2)
                y_high(2)
                copy_p(3)
                if not last:
                    next_hi(3)
                y_high(3)

            with act.Fori(0, DH_HEADS - 1) as h:
                dsa_head(h)
            dsa_head(DH_HEADS - 1, last=True)

            def merge(m, first=False):
                for j, gate in enumerate((sga, sgb)):
                    act.wait_ge(evac, m * 4 + (T_MERGE + j + 1))
                    act.activation(gate[:, :], gate[:, :], ACT.Sigmoid).then_inc(m_sig, 1)
                    if not first:
                        hi_at(m, 4, G_MERGE + j + SLOTS)
                hi_at(m, 4, G_MERGE + 2 + SLOTS)
                hi_at(m, 4, G_MERGE + 3 + SLOTS)
                act.wait_ge(m_sum, m + 1)
                apart(act)
                act.activation(mh[:, m, :], ma[:, :], ACT.Copy).then_inc(m_hi, 1)

            merge(0, first=True)
            with act.Fori(0, KT - 1) as m:
                merge(m + 1)

            with act.Fori(0, KT // 4) as i:
                for j in range(4):
                    hi_at(i, 4, G_OUT + j + SLOTS)
                    act.wait_ge(evac, i * 4 + (T_OUT + j + 1))
                    x_tile(2, i * 4 + j, META, V_FFN2)
            rms(2, META)
            with act.Fori(0, FT // 2) as i:
                up(i, 1, G_UP2, T_UP2)

            with act.Fori(0, KT // 2 - 1) as i:
                down(i, 3, G_DOWN2, T_DOWN2, None)
            down(KT // 2 - 1, 3, G_DOWN2, T_DOWN2, None)
            rms(3, META)

        @block.tensor
        def _(pe):
            def chunk_mm(r, slot, kts, k0, total, lhs_hi, lhs_lo, wide_tile, come=None):
                for k in range(kts):
                    if come is not None:
                        pe.wait_ge(come[0], come[1] + k + 1)
                    first, last = k0 + k == 0, k0 + k == total - 1
                    w_h = wh[:, slot, k * P:(k + 1) * P]
                    w_l = wl[:, slot, k * P:(k + 1) * P]
                    for n, (w, a) in enumerate(((w_h, lhs_hi), (w_h, lhs_lo), (w_l, lhs_hi))):
                        parts = ((0, 0), (HALF, 512)) if wide_tile else ((None, 0),)
                        for src, dst in parts:
                            size = HALF if wide_tile else SEQ
                            off = src if wide_tile else 0
                            mm = pe.matmul(proj[:, r, dst:dst + size], w, a(k0 + k, off, size),
                                           start=first and n == 0, stop=last and n == 2)
                return mm

            def xs(tok0):
                return (lambda k, off, size: xh[:, k, tok0 + off:tok0 + off + size],
                        lambda k, off, size: xl[:, k, tok0 + off:tok0 + off + size])

            def pair(hi_t, lo_t):
                return (lambda k, off, size: hi_t[:, k, off:off + size],
                        lambda k, off, size: lo_t[:, k, off:off + size])

            def tile8(i, t0, g0, src, wide_tile, per=4, come=None):
                pe.wait_ge(evac, i * per + (t0 - 1))
                pe.wait_ge(w_lo, i * per + (g0 + 1))
                chunk_mm(t0 % 2, g0 % SLOTS, KT, 0, KT, *src, wide_tile, come).then_inc(w_used, 1)

            def transpose(out, in_):
                return pe.transpose(out, in_, ident[:, :])

            def to_tokens(src, n_chunks, sem_):
                for c in range(n_chunks):
                    transpose(ps[:, 1, c * P:(c + 1) * P], src[:, META + c * P:META + (c + 1) * P])
                transpose(ps[0:META, 1, 512:512 + P], src[:, 0:META]).then_inc(sem_, 1)

            def norm_sum(n, tok0):
                pe.wait_ge(ss_acc, 9 * n + 9)
                if tok0 == 0:
                    pe.matmul(ps[:, 0, 0:HALF], ones[:, :], ssum[:, 0:HALF], start=True, stop=True)
                    pe.matmul(ps[:, 0, 512:512 + HALF], ones[:, :], ssum[:, HALF:NT], start=True, stop=True)\
                      .then_inc(ss_sum, 1)
                else:
                    pe.matmul(ps[:, 0, 0:SEQ], ones[:, :], ssum[:, META:NT], start=True, stop=True)\
                      .then_inc(ss_sum, 1)

            def up(n, g0, t0):
                tok0 = 0 if n == 0 else META
                tile8(0, t0, g0, xs(tok0), tok0 == 0, come=(x_lo, 2 * n * KT))
                if n == 0:
                    pe.wait_ge(setup, 1)
                    pe.wait_ge(consts, 32)
                norm_sum(2 * n, tok0)
                for j in range(1, 4):
                    tile8(0, t0 + j, g0 + j, xs(tok0), tok0 == 0)
                with pe.Fori(0, FT // 2 - 1) as i:
                    for j in range(4, 8):
                        tile8(i, t0 + j, g0 + j, xs(tok0), tok0 == 0)

            def down(n, g0, t0):
                tok0 = 0 if n == 0 else META
                src = (lambda k, off, size: ah[:, k, tok0 + off:tok0 + off + size],
                       lambda k, off, size: al[:, k, tok0 + off:tok0 + off + size])
                with pe.Fori(0, KT // 2) as i:
                    for j in range(2):
                        pe.wait_ge(evac, i * 2 + (t0 + j - 1))
                        k = 0
                        for b, kts in enumerate(DOWN_SPLIT):
                            g = g0 + 4 * j + b
                            pe.wait_ge(w_lo, i * 8 + (g + 1))
                            pe.wait_ge(act_lo, FT * n + k + kts)
                            chunk_mm((t0 + j) % 2, g % SLOTS, kts, k, FT, *src, tok0 == 0).then_inc(w_used, 1)
                            k += kts

            up(0, G_UP1, T_UP1)
            down(0, G_DOWN1, T_DOWN1)

            def gate_z(h):
                if h >= 2:
                    pe.wait_ge(zb_ok, h - 1)
                elif h == 1:
                    pe.wait_ge(iw_ok, 1)
                w = wlr[GLR_ROW:GLR_ROW + LOWRANK, h * DK:(h + 1) * DK]
                x = misc[GLR_ROW:GLR_ROW + LOWRANK, :]
                pe.matmul(ps[:, h % 2, 0:HALF], w, x[:, 0:HALF], start=True, stop=True)
                pe.matmul(ps[:, h % 2, 512:512 + HALF], w, x[:, HALF:NT], start=True, stop=True).then_inc(z_mm, 1)

            tile8(0, T_IDX, G_IDX, xs(0), True, come=(x_lo, KT))
            norm_sum(1, 0)
            tile8(0, T_IDX + 1, G_IDX + 1, xs(META), False)
            pe.wait_ge(evac, T_IDX + 1)
            for i in range(QT):
                mm = transpose(ps[:, 1, i * P:(i + 1) * P], misc[:, META + i * P:META + (i + 1) * P])
            mm.then_inc(iwT_mm, 1)
            pe.wait_ge(consts2, 16 * 6)
            gate_z(0)
            tile8(0, T_IDX + 2, G_IDX + 2, xs(META), False)
            gate_z(1)
            gate_z(2)
            tile8(0, T_IDX + 3, G_IDX + 3, xs(META), False)
            gate_z(3)
            tile8(0, T_IDX + 4, G_IDX + 4, xs(META), False)
            pe.wait_ge(zb_ok, 3)
            pe.matmul(ps[0:DH_HEADS, 0, 0:512], relb[:, :], oneh[:, 0:512], start=True, stop=True)
            pe.matmul(ps[0:DH_HEADS, 0, 512:LINE], relb[:, :], oneh[:, 512:LINE], start=True, stop=True)\
              .then_inc(line_mm, 1)
            for i in range(QT):
                tile8(0, T_GLA + i, G_GLA + i, xs(META if i == 0 else 0), i > 0)
                if i == 0:
                    pe.wait_ge(ik2_in, 16)
                for e in range(IH):
                    n = i * IH + e
                    lo_, keys = 64 * (e % 2), (misc if e % 2 == 0 else ik2)
                    if n == 0:
                        pe.wait_ge(line_ok, 1)
                    elif n == 1:
                        pe.wait_ge(zb_ok, GH)
                    else:
                        pe.wait_ge(s_relu, n - 1)
                    w = iq[lo_:lo_ + IDH, e // 2, i * P:(i + 1) * P]
                    first = min(WIDTH[i], 512)
                    mm = pe.matmul(ps[:, n % 2, 0:first], w, keys[lo_:lo_ + IDH, 0:first], start=True, stop=True)
                    if WIDTH[i] > 512:
                        mm = pe.matmul(ps[:, n % 2, 512:NT], w, keys[lo_:lo_ + IDH, 512:NT], start=True, stop=True)
                    mm.then_inc(s_mm, 1)
            pe.wait_ge(s_relu, QT * IH)

            def gla_head(hd, last=False):
                def level(l):
                    if l < len(LEVELS):
                        pe.wait_ge(x_ok, hd * 14 + (2 * l + 2))
                    if l >= 2:
                        pe.wait_ge(a_ok, hd * 8 + (l - 1))
                    for c in range(QT):
                        if l < len(LEVELS):
                            a = b = X[:, l % 2, c * P:(c + 1) * P]
                        else:
                            a, b = kT[:, META + c * P:META + (c + 1) * P], qT[:, c * P:(c + 1) * P]
                        o = (l % 2) * 512 + c * P
                        mm = pe.matmul(ps[:, 0, o:o + P], a, b, start=True, stop=True)
                    mm.then_inc(g_mm, 1)

                def values(j):
                    if j == 1:
                        pe.wait_ge(vt_ok, hd * 4 + 2)
                    to_tokens(vT[:, j, :], QT, vt_mm)

                def ahead(j):
                    all_tokens = j in (1, 2) if last else j in (0, 1, 3)
                    tile8(hd, T_GLA + 4 + j, G_GLA + 4 + j, xs(0 if all_tokens else META), all_tokens)

                level(0)
                level(1)
                level(2)
                values(0)
                level(3)
                values(1)
                level(4)
                ahead(0)
                level(5)
                level(6)
                level(7)
                pe.wait_ge(vt_ok, hd * 4 + 4)
                pe.wait_ge(qk_ok, hd * 2 + 2)
                to_tokens(ke[:, :], QT - 1, kd_mm)
                ahead(1)
                pe.wait_ge(kd_ok, hd * 2 + 2)
                pe.matmul(ps[:, 1, 0:DV], kdT[0:META, 0, :], V[0:META, 0, :], start=True, stop=True)
                for c in range(1, QT):
                    mm = pe.matmul(ps[:, 1, c * DV:(c + 1) * DV], kdT[:, c, :], V[:, c, :], start=True, stop=True)
                mm.then_inc(u_mm, 1)
                ahead(2)
                pe.wait_ge(a_ok, hd * 8 + 8)
                for c in range(QT):
                    pe.wait_ge(s_ok, hd * 4 + (c + 1))
                    o = ps[:, 0, c * DV:(c + 1) * DV]
                    pe.matmul(o, A[:, c * P:(c + 1) * P], V[:, c + 1, :], start=True, stop=False)
                    pe.matmul(o, qe[:, c * P:(c + 1) * P], S[:, c, :], start=False, stop=True).then_inc(o_mm, 1)
                ahead(3)
                pe.wait_ge(on_ok, hd * 4 + 4)
                for j in range(2):
                    for c in range(QT):
                        mm = transpose(ps[:, 1, j * SEQ + c * P:j * SEQ + (c + 1) * P], on[:, c, j * P:(j + 1) * P])
                    mm.then_inc(ot_mm, 1)

            with pe.Fori(0, GH - 1) as hd:
                gla_head(hd)
            gla_head(GH - 1, last=True)

            def dsa_head(h, last=False):
                def logits(i):
                    if i >= 1:
                        pe.wait_ge(lg_ok, h * 4 + i)
                    w = dqT[:, i * P:(i + 1) * P]
                    first = min(WIDTH[i], 512)
                    if WIDTH[i] > 512:
                        pe.wait_ge(yb_lo, h * 4 + 1)
                    mm = pe.matmul(ps[:, 0, 0:first], w, dkT[:, 0:first], start=True, stop=True)
                    if WIDTH[i] > 512:
                        mm = pe.matmul(ps[:, 0, 512:NT], w, dkT[:, 512:NT], start=True, stop=True)
                    mm.then_inc(qk_mm, 1)

                def turn(i):
                    pe.wait_ge(pn_ok, h * 4 + (i + 1))
                    to_tokens(logit[:, i % 2, :], i + 1, pt_mm)

                def attend(i):
                    pe.wait_ge(pt_ok, h * 8 + (2 * i + 2))
                    if i == 1:
                        pe.wait_ge(lg_ok, h * 4 + 4)
                    elif i >= 2:
                        pe.wait_ge(yb_lo, h * 4 + i)
                    y = ps[:, 0, 640:640 + P]
                    pe.matmul(y, dV[0:META, 0, :], pT[0:META, i % 2, 0:P], start=True, stop=False)
                    for j in range(i + 1):
                        mm = pe.matmul(y, dV[:, j + 1, :], pT[:, i % 2, (j + 1) * P:(j + 2) * P],
                                       start=False, stop=j == i)
                    mm.then_inc(pv_mm, 1)

                def ahead(j):
                    all_tokens = not last and j in (0, 2)
                    tile8(h, T_DSA + 4 + j, G_DSA + 4 + j, xs(0 if all_tokens else META), all_tokens)

                logits(0)
                to_tokens(dvT[:, :], QT, dv_mm)
                logits(1)
                ahead(0)
                pe.wait_ge(dv_ok, h * 2 + 2)
                turn(0)
                logits(2)
                attend(0)
                turn(1)
                logits(3)
                if not last:
                    ahead(1)
                attend(1)
                turn(2)
                ahead(1 if last else 2)
                attend(2)
                turn(3)
                if not last:
                    ahead(3)
                attend(3)

            pe.wait_ge(ot_ok, 2 * GH)
            with pe.Fori(0, DH_HEADS - 1) as h:
                dsa_head(h)
            dsa_head(DH_HEADS - 1, last=True)

            pe.wait_ge(ya_lo, DH_HEADS)
            tile8(0, T_MERGE + 2, G_MERGE + 2, pair(yah, yal), False)
            pe.wait_ge(yb_lo, DH_HEADS * QT)
            tile8(0, T_MERGE + 3, G_MERGE + 3, pair(ybh, ybl), False)
            with pe.Fori(0, KT - 1) as m:
                tile8(m, T_MERGE + 4, G_MERGE + 4, xs(META), False)
                tile8(m, T_MERGE + 5, G_MERGE + 5, xs(META), False)
                tile8(m, T_MERGE + 6, G_MERGE + 6, pair(yah, yal), False)
                tile8(m, T_MERGE + 7, G_MERGE + 7, pair(ybh, ybl), False)
            tile8(0, T_OUT, G_OUT, pair(mh, ml), False, come=(m_lo, 0))
            for j in range(1, KT):
                tile8(0, T_OUT + j, G_OUT + j, pair(mh, ml), False)
            up(1, G_UP2, T_UP2)
            down(1, G_DOWN2, T_DOWN2)
            norm_sum(3, META)

        @block.vector
        def _(dve):
            def col(c, m):
                return vecs[:, c + m:c + m + 1] if isinstance(m, int) else vecs[:, bass.ds(m + c, 1)]

            def x_tile(n, m, tok0, gain):
                dve.wait_ge(squared, m + (8 * n + 1))
                dve.wait_ge(ss_acc, m + (9 * n + 1))
                dve.tensor_tensor(ssum[:, tok0:NT], ssum[:, tok0:NT], sq[:, tok0:NT], ALU.add).then_inc(ss_acc, 1)
                if gain is not None:
                    dve.wait_ge(x_hi, m + (8 * n + 1))
                    dve.scalar_tensor_tensor(out=xl[:, m, tok0:NT], in0=hT[:, m, tok0:NT], scalar=col(gain, m),
                                             in1=f(xh[:, m, tok0:NT]), op0=ALU.mult, op1=ALU.subtract)\
                       .then_inc(x_lo, 1)

            def inv_rms(n, tok0):
                dve.wait_ge(rms_ok, n + 1)
                dve.reciprocal(rstd[:, tok0:NT], sq[:, tok0:NT]).then_inc(rstd_ok, 1)
                if n < 3:
                    dve.memset(ssum[:, :], 0.0).then_inc(ss_acc, 1)
                dve.wait_ge(rstd_ok, n + 1)

            def read_wide(dst, r, scale=None):
                return dve.tensor_tensor(two(dst), wide(r), two(rstd[:, :]), ALU.mult).then_inc(evac, 1)

            def read_seq(dst, r, scale=1.0):
                if scale == 1.0:
                    return dve.tensor_tensor(dst, proj[:, r, 0:SEQ], rstd[:, META:NT], ALU.mult).then_inc(evac, 1)
                return dve.scalar_tensor_tensor(out=dst, in0=proj[:, r, 0:SEQ], scalar=scale, in1=rstd[:, META:NT],
                                                op0=ALU.mult, op1=ALU.mult).then_inc(evac, 1)

            def up(n, g0, t0):
                tok0 = 0 if n == 0 else META
                with dve.Fori(0, FT // 2) as i:
                    for j in range(2):
                        for b, dst in enumerate((zg, zu)):
                            r = (t0 + 2 * j + b) % 2
                            dve.wait_ge(w_used, i * 4 + (g0 + 2 * j + b + 1))
                            if tok0 == 0:
                                read_wide(dst[:, :], r)
                            else:
                                read_seq(dst[:, META:NT], r)
                        dve.wait_ge(sig, i * 2 + (FT * n + j + 1))
                        dve.wait_ge(evac, i * 4 + (t0 + 2 * j + 2))
                        dve.tensor_tensor(zg[:, tok0:NT], zg[:, tok0:NT], sg[:, tok0:NT], ALU.mult).then_inc(gated, 1)
                        dve.wait_ge(gated, i * 2 + (FT * n + j + 1))
                        dve.tensor_tensor(zu[:, tok0:NT], zg[:, tok0:NT], zu[:, tok0:NT], ALU.mult).then_inc(act_f, 1)
                        dve.wait_ge(act_hi, i * 2 + (FT * n + j + 1))
                        dve.tensor_tensor(al[:, i * 2 + j, tok0:NT], zu[:, tok0:NT], f(ah[:, i * 2 + j, tok0:NT]),
                                          ALU.subtract).then_inc(act_lo, 1)
                        dve.wait_ge(act_lo, i * 2 + (FT * n + j + 1))

            def down(n, g0, t0, norm, gain):
                tok0 = 0 if n == 0 else META
                with dve.Fori(0, KT // 2) as i:
                    for j in range(2):
                        m, r = i * 2 + j, (t0 + j) % 2
                        dve.wait_ge(w_used, i * 8 + (g0 + 4 * j + 4))
                        if tok0 == 0:
                            h_, p_ = two(hT[:, m, :]), wide(r)
                        else:
                            h_, p_ = hT[:, m, META:NT], proj[:, r, 0:SEQ]
                        dve.scalar_tensor_tensor(out=h_, in0=p_, scalar=0.5, in1=h_, op0=ALU.mult, op1=ALU.add)\
                           .then_inc(evac, 1)
                        dve.wait_ge(evac, i * 2 + (t0 + j + 1))
                        x_tile(norm, m, tok0, gain)

            dve.memset(eps[:, :], EPS).then_inc(evac, 1)
            dve.memset(rstd[:, :], 0.0).then_inc(evac, 1)
            dve.memset(ssum[:, :], 0.0).then_inc(ss_acc, 1)
            dve.wait_ge(consts, 32)
            for m in range(KT):
                if m % 2 == 0:
                    dve.wait_ge(h_in[m // 2], 16)
                x_tile(0, m, 0, V_FFN1)
            inv_rms(0, 0)
            up(0, G_UP1, T_UP1)
            down(0, G_DOWN1, T_DOWN1, 1, V_MIX)
            inv_rms(1, 0)

            def gate_bias(h):
                dve.wait_ge(z_mm, h + 1)
                apart(dve)
                dve.tensor_scalar(two(blog[:, h, :]), ps[:, h % 2, :].rearrange("p (b n) -> p b n", b=2)[:, :, 0:HALF],
                                  vecs[:, V_BLR + h:V_BLR + h + 1], None, ALU.add).then_inc(zb_ok, 1)

            def index_scores(i):
                s_i = score[:, COL[i]:COL[i] + WIDTH[i]]
                for e in range(IH):
                    n = i * IH + e
                    dve.wait_ge(s_relu, n + 1)
                    if e == 0:
                        dve.tensor_scalar(s_i, t1[:, n % 2, 0:WIDTH[i]], iwq[:, i, e:e + 1], 0.0, ALU.mult, ALU.add)\
                           .then_inc(s_acc, 1)
                    else:
                        dve.wait_ge(s_acc, n)
                        dve.scalar_tensor_tensor(out=s_i, in0=t1[:, n % 2, 0:WIDTH[i]], scalar=iwq[:, i, e:e + 1],
                                                 in1=s_i, op0=ALU.mult, op1=ALU.add).then_inc(s_acc, 1)

            dve.wait_ge(w_used, G_IDX + 1)
            read_wide(misc[:, :], T_IDX % 2)
            dve.wait_ge(w_used, G_IDX + 2)
            read_seq(iq[:, 0, :], (T_IDX + 1) % 2)
            dve.wait_ge(iwT_mm, 1)
            dve.tensor_scalar(iwq[:, :, :], ps[:, 1, 0:SEQ].rearrange("p (i n) -> p i n", i=QT)[:, :, IW_ROW:IW_ROW + IH],
                              IH ** -0.5 * IDH ** -0.5, None, ALU.mult).then_inc(iw_ok, 1)
            gate_bias(0)
            dve.wait_ge(consts2, 16 * 6)
            dve.tensor_copy(lvlmask[:, :, :].rearrange("p l n -> p (l n)"), on[:, :, :].rearrange("p c n -> p (c n)"))\
               .then_inc(lvl_ok, 1)
            dve.wait_ge(w_used, G_IDX + 3)
            read_seq(iq[:, 1, :], (T_IDX + 2) % 2)
            gate_bias(1)
            gate_bias(2)
            dve.wait_ge(w_used, G_IDX + 4)
            read_seq(iq[:, 2, :], (T_IDX + 3) % 2)
            gate_bias(3)
            dve.wait_ge(w_used, G_IDX + 5)
            read_seq(iq[:, 3, :], (T_IDX + 4) % 2)
            dve.wait_ge(line_mm, 1)
            dve.tensor_copy(line[:, :], ps[0:DH_HEADS, 0, 0:LINE]).then_inc(line_ok, 1)
            dve.wait_ge(softp, 3)
            dve.wait_ge(zb_ok, GH)
            dve.scalar_tensor_tensor(out=sp[:, :, :], in0=blog[:, :, :], scalar=0.0, in1=sp[:, :, :], op0=ALU.min,
                                     op1=ALU.subtract).then_inc(ls_ok, 1)
            dve.wait_ge(ls_ok, 1)
            for h in range(GH):
                dve.tensor_tensor_scan(blog[:, h, :], chunk0[:, :], sp[:, h, :], 0.0, ALU.mult, ALU.add).then_inc(b_ok, 1)
            dve.wait_ge(iw_ok, 1)
            for i in range(QT):
                dve.wait_ge(w_used, G_GLA + i + 1)
                if i == 0:
                    read_seq(qT[:, :], T_GLA % 2, DK ** -0.5)
                else:
                    read_wide(kT[:, :] if i == 1 else vT[:, i - 2, :], (T_GLA + i) % 2)
                index_scores(i)
            dve.wait_ge(s_acc, QT * IH)
            for i in range(QT):
                last_keys = score[:, COL[i] + WIDTH[i] - P:COL[i] + WIDTH[i]]
                dve.tensor_tensor(last_keys, last_keys, triu[:, :], ALU.min).then_inc(tk, 1)
            dve.wait_ge(tk, QT)
            dve.tensor_copy(work[:, :], score[:, :]).then_inc(tk, 1)
            dve.wait_ge(setup, 2)
            dve.wait_ge(lvl_ok, 1)
            dve.wait_ge(b_ok, GH)

            ROUNDS = TOPK // 8 // GH

            def expo(hd, l):
                m = LEVELS[l]
                if l >= 2:
                    dve.wait_ge(e_ok, hd * 7 + (l - 1))
                b = blog[:, hd, META:NT].rearrange("p (b two m) -> p b two m", two=2, m=m)
                d = Dl[:, l % 2, :].rearrange("p (b two m) -> p b two m", two=2, m=m)
                ref = b[:, :, 0, m - 1:m].to_broadcast([P, SEQ // (2 * m), m])
                dve.tensor_tensor(d[:, :, 1, :], b[:, :, 1, :], ref, ALU.subtract).then_inc(d_ok, 1)
                dve.tensor_tensor(d[:, :, 0, :], ref, b[:, :, 0, :], ALU.subtract).then_inc(d_ok, 1)

            expo(0, 0)
            expo(0, 1)

            def gla_head(hd, last=False):
                def top_rounds(i):
                    w_i = work[:, COL[i]:COL[i] + WIDTH[i]]
                    turn = TURNS.index(i)
                    for n in range(ROUNDS):
                        at_ = QT + 1 + 2 * (turn * ROUNDS + n)
                        dve.wait_ge(tk, hd * (2 * QT * ROUNDS) + at_)
                        apart(dve)
                        dve.max(m8[:, i, :], w_i).then_inc(tk, 1)
                        dve.wait_ge(tk, hd * (2 * QT * ROUNDS) + (at_ + 1))
                        apart(dve)
                        dve.match_replace(w_i, m8[:, i, :], w_i, NEG).then_inc(tk, 1)

                def merge_level(l):
                    dve.wait_ge(g_mm, hd * 8 + (l + 1))
                    o = (l % 2) * 512
                    apart(dve)
                    if l >= 1:
                        dve.wait_ge(a_ok, hd * 8 + l)
                        apart(dve)
                    dve.copy_predicated(A[:, :].rearrange("p (c t) -> p c t", c=QT),
                                        lvlmask[:, l, :].unsqueeze(1).to_broadcast([P, QT, P]),
                                        ps[:, 0, o:o + SEQ].rearrange("p (c t) -> p c t", c=QT)).then_inc(a_ok, 1)

                def read_ahead(j):
                    dve.wait_ge(w_used, hd * 4 + (G_GLA + 4 + j + 1))
                    r = (T_GLA + j) % 2
                    if last:
                        if j in (1, 2):
                            read_wide((dkT if j == 1 else dvT)[:, :], r)
                        elif j == 0:
                            read_seq(dqT[:, :], r, DH ** -0.5)
                        else:
                            read_seq(zr[:, :], r)
                    elif j == 2:
                        dve.wait_ge(qk_ok, hd * 2 + 2)
                        read_seq(qT[:, :], r, DK ** -0.5)
                    else:
                        read_wide(kT[:, :] if j == 3 else vT[:, j, :], r)

                TURNS = (1, 3, 2, 0)
                expo(hd, 2)
                merge_level(0)
                expo(hd, 3)
                merge_level(1)
                expo(hd, 4)
                merge_level(2)
                expo(hd, 5)
                merge_level(3)
                expo(hd, 6)
                merge_level(4)
                for n, (src, size) in enumerate(((blog[:, hd, META:NT], P), (blog[:, hd, 0:META], META))):
                    b = src.rearrange("p (c t) -> p c t", t=size)
                    d = (sq[:, META:NT] if n == 0 else sq[:, 0:META]).rearrange("p (c t) -> p c t", t=size)
                    nch = QT if n == 0 else 1
                    dve.tensor_tensor(d, b, b[:, :, size - 1:size].to_broadcast([P, nch, size]), ALU.subtract)\
                       .then_inc(de_ok, 1)
                top_rounds(1)
                for l in range(5, 8):
                    merge_level(l)
                read_ahead(0)
                top_rounds(3)
                dve.wait_ge(u_mm, hd + 1)
                dve.tensor_copy(S[:, 0, :], ps[:, 1, 0:DV]).then_inc(s_ok, 1)
                dve.wait_ge(ex_ok, hd * 3 + 3)
                for c in range(1, QT):
                    dve.wait_ge(s_ok, hd * 4 + c)
                    dve.scalar_tensor_tensor(out=S[:, c, :], in0=S[:, c - 1, :], scalar=eb[:, c - 1:c],
                                             in1=ps[:, 1, c * DV:(c + 1) * DV], op0=ALU.mult, op1=ALU.add)\
                       .then_inc(s_ok, 1)
                read_ahead(1)
                if not last:
                    expo(hd + 1, 0)
                    expo(hd + 1, 1)
                top_rounds(2)
                read_ahead(2)
                dve.wait_ge(orms_ok, hd + 1)
                dve.reciprocal(orstd[:, :], orms[:, :]).then_inc(orstd_ok, 1)
                dve.wait_ge(orstd_ok, hd + 1)
                for c in range(QT):
                    dve.tensor_scalar(on[:, c, :], ps[:, 0, c * DV:(c + 1) * DV], orstd[:, c:c + 1], None, ALU.mult)\
                       .then_inc(on_ok, 1)
                top_rounds(0)
                read_ahead(3)

            with dve.Fori(0, GH - 1) as hd:
                gla_head(hd)
            gla_head(GH - 1, last=True)

            dve.wait_ge(tk, QT + 1 + 2 * QT * (TOPK // 8))
            dve.tensor_tensor(score[:, :], work[:, :], score[:, :], ALU.is_equal).then_inc(tk, 1)
            dve.wait_ge(tk, QT + 2 + 2 * QT * (TOPK // 8))
            dve.wait_ge(ot_ok, 2 * GH)
            dve.tensor_scalar(score[:, :], score[:, :], MASKED, None, ALU.mult).then_inc(mask_ok, 1)
            dve.wait_ge(mask_ok, 1)

            def dsa_head(h, last=False):
                def masked(i):
                    w, b = WIDTH[i], i % 2
                    dve.wait_ge(qk_mm, h * 4 + (i + 1))
                    if i >= 2:
                        dve.wait_ge(pt_mm, h * 4 + (i - 1))
                    dve.tensor_tensor(logit[:, b, 0:w], ps[:, 0, 0:w], strip[:, NT - w:NT], ALU.add).then_inc(lg_ok, 1)
                    dve.wait_ge(lg_ok, h * 4 + (i + 1))
                    apart(dve)
                    dve.tensor_tensor_reduce(logit[:, b, 0:w], logit[:, b, 0:w], score[:, COL[i]:COL[i] + w], -1.0,
                                             3.0e38, ALU.add, ALU.min, nmax[:, b:b + 1]).then_inc(lm_ok, 1)

                def normalise(i):
                    w, b = WIDTH[i], i % 2
                    dve.wait_ge(p_ok, h * 4 + (i + 1))
                    dve.reciprocal(rinv[:, b:b + 1], rowsum[:, b:b + 1]).then_inc(ri_ok, 1)
                    dve.wait_ge(ri_ok, h * 4 + (i + 1))
                    dve.tensor_scalar(logit[:, b, 0:w], logit[:, b, 0:w], rinv[:, b:b + 1], None, ALU.mult)\
                       .then_inc(pn_ok, 1)

                def y_low(i):
                    dve.wait_ge(yb_hi, h * 4 + (i + 1))
                    dve.tensor_tensor(ybl[:, h, i * P:(i + 1) * P], ps[:, 0, 640:640 + P],
                                      f(ybh[:, h, i * P:(i + 1) * P]), ALU.subtract).then_inc(yb_lo, 1)

                def read_ahead(j):
                    dve.wait_ge(w_used, h * 4 + (G_DSA + 4 + j + 1))
                    r = (T_DSA + j) % 2
                    if j in (0, 2):
                        read_wide((dvT if j == 0 else dkT)[:, :], r)
                    elif j == 1:
                        read_seq(dqT[:, :], r, DH ** -0.5)
                    else:
                        read_seq(zr[:, :], r)

                def read_gate(j):
                    dve.wait_ge(w_used, G_MERGE + j + 1)
                    read_seq((sga, sgb)[j][:, :], (T_MERGE + j) % 2)

                dve.wait_ge(strip_in, h * 16 + 16)
                masked(0)
                normalise(0)
                masked(1)
                normalise(1)
                read_gate(0) if last else read_ahead(0)
                masked(2)
                y_low(0)
                normalise(2)
                masked(3)
                normalise(3)
                dve.wait_ge(r_sig, h + 1)
                dve.tensor_tensor(sr[:, :], zr[:, :], sr[:, :], ALU.mult).then_inc(r_g, 1)
                dve.wait_ge(r_g, h + 1)
                dve.tensor_tensor(zr[:, :], sr[:, :], oT[:, h, :], ALU.mult).then_inc(ya_f, 1)
                if not last:
                    read_ahead(1)
                y_low(1)
                dve.wait_ge(ya_hi, h + 1)
                dve.tensor_tensor(yal[:, h, :], zr[:, :], f(yah[:, h, :]), ALU.subtract).then_inc(ya_lo, 1)
                read_gate(1) if last else read_ahead(2)
                y_low(2)
                if not last:
                    dve.wait_ge(ya_lo, h + 1)
                    read_ahead(3)
                y_low(3)

            with dve.Fori(0, DH_HEADS - 1) as h:
                dsa_head(h)
            dsa_head(DH_HEADS - 1, last=True)

            def merge(m, first=False):
                if not first:
                    for j, gate in enumerate((sga, sgb)):
                        dve.wait_ge(w_used, m * 4 + (G_MERGE + j + 1))
                        read_seq(gate[:, :], (T_MERGE + j) % 2)
                dve.wait_ge(w_used, m * 4 + (G_MERGE + 3))
                dve.wait_ge(m_sig, m * 2 + 1)
                dve.tensor_tensor(ma[:, :], proj[:, (T_MERGE + 2) % 2, 0:SEQ], sga[:, :], ALU.mult).then_inc(evac, 1)
                dve.wait_ge(w_used, m * 4 + (G_MERGE + 4))
                dve.wait_ge(m_sig, m * 2 + 2)
                dve.tensor_tensor(sgb[:, :], proj[:, (T_MERGE + 3) % 2, 0:SEQ], sgb[:, :], ALU.mult).then_inc(evac, 1)
                dve.wait_ge(evac, m * 4 + (T_MERGE + 4))
                dve.tensor_tensor(ma[:, :], ma[:, :], sgb[:, :], ALU.add).then_inc(m_sum, 1)
                dve.wait_ge(m_hi, m + 1)
                dve.tensor_tensor(ml[:, m, :], ma[:, :], f(mh[:, m, :]), ALU.subtract).then_inc(m_lo, 1)

            merge(0, first=True)
            with dve.Fori(0, KT - 1) as m:
                merge(m + 1)

            with dve.Fori(0, KT // 4) as i:
                for j in range(4):
                    m = i * 4 + j
                    dve.wait_ge(w_used, i * 4 + (G_OUT + j + 1))
                    dve.tensor_tensor(hT[:, m, META:NT], proj[:, (T_OUT + j) % 2, 0:SEQ], hT[:, m, META:NT], ALU.add)\
                       .then_inc(evac, 1)
                    dve.wait_ge(evac, i * 4 + (T_OUT + j + 1))
                    x_tile(2, m, META, V_FFN2)
            inv_rms(2, META)
            up(1, G_UP2, T_UP2)
            down(1, G_DOWN2, T_DOWN2, 3, None)
            inv_rms(3, META)
            for m in range(KT):
                dve.scalar_tensor_tensor(out=final[:, m, :], in0=hT[:, m, META:NT], scalar=col(V_FINAL, m),
                                         in1=rstd[:, META:NT], op0=ALU.mult, op1=ALU.mult).then_inc(out_ok, 1)


def rel_bucket(dist):
    n = np.maximum(dist, 0)
    exact = BUCKETS // 2
    nf = np.maximum(n, exact).astype(np.float32)
    large = exact + (np.log(nf / np.float32(exact)) / np.float32(math.log(MAX_DIST / exact))
                     * np.float32(BUCKETS - exact)).astype(np.int32)
    return np.where(n < exact, n, np.minimum(large, BUCKETS - 1))


def constants():
    p, t = np.arange(P)[:, None], np.arange(P)[None, :]
    masks = []
    for m in LEVELS:
        same = p // (2 * m) == t // (2 * m)
        masks.append(same & (p // m % 2 == 0) & (t // m % 2 == 1))
    masks.append(p == t)
    bucket = rel_bucket(NT - 1 - np.arange(LINE))
    chunk0 = np.ones((P, NT), np.float32)
    chunk0[:, [0] + [META + P * c for c in range(QT)]] = 0.0
    return {
        "ident": np.eye(P, dtype=np.float32),
        "lvlmask": np.stack(masks, 1).astype(np.float32).reshape(P, -1),
        "triu": np.where(t <= p, -NEG, NEG).astype(np.float32),
        "chunk0": chunk0,
        "oneh": (np.arange(BUCKETS)[:, None] == bucket[None, :]).astype(np.float32),
    }


def feature_tiles(w, cols=None):
    k, m = w.shape
    return np.ascontiguousarray(w.reshape(k // P, P, m // P, P).transpose(2, 1, 0, 3).reshape(m // P, P, k))


def lay_out(inputs):
    g = {n: np.asarray(a) for n, a in inputs.items()}
    w_in = g["w_in"][0]
    sizes = (GH * DK, GH * DK, GH * DV, GH * DV, LOWRANK, D, D, D, IH * IDH, IDH, IH, D, D)
    cuts = np.cumsum((0,) + sizes)
    gq, gk, gv, gr, glr, dq, dk, dv, iq, ik, iw, ga, gb = (w_in[:, a:b] for a, b in zip(cuts[:-1], cuts[1:]))
    misc = np.zeros((D, P), np.float32)
    misc[:, 0:IDH], misc[:, GLR_ROW:GLR_ROW + LOWRANK], misc[:, IW_ROW:IW_ROW + IH] = ik, glr, iw
    order = [misc, iq]
    for h in range(GH):
        q_k = [gq[:, h * DK:(h + 1) * DK], gk[:, h * DK:(h + 1) * DK]]
        v = [gv[:, h * DV:(h + 1) * DV]]
        order += q_k + v if h == 0 else v + q_k
    for h in range(DH_HEADS):
        order += [x[:, h * P:(h + 1) * P] for x in ((dq, dk, dv, gr) if h == 0 else (dv, dq, dk, gr))]
    for m in range(KT):
        order += [x[:, m * P:(m + 1) * P] for x in (ga, gb, g["w_up_a"][0], g["w_up_b"][0])]
    order.append(g["w_out"][0])
    out = {"w_mix": feature_tiles(np.concatenate(order, axis=1))}
    for n in (1, 2):
        gate, up = g[f"ffn{n}_w_gate"][0], g[f"ffn{n}_w_up"][0]
        both = np.stack([gate.reshape(D, FT, P), up.reshape(D, FT, P)], axis=2).reshape(D, 2 * DFF)
        out[f"w_up{n}"] = feature_tiles(both)
        out[f"w_down{n}"] = feature_tiles(g[f"ffn{n}_w_down"][0])
    tokens = np.concatenate([g["meta_tokens"], g["x"][0]], axis=0)
    out["xT"] = np.ascontiguousarray(tokens.T.reshape(KT, P, NT).transpose(1, 0, 2))
    vectors = [g["norm_ffn1"][0], g["norm_mix"][0], g["norm_ffn2"][0], g["norm_final"], g["gla_norm"][0],
               g["gla_b_lr"][0]]
    out["vecs"] = np.ascontiguousarray(np.concatenate(vectors).reshape(NVEC, P).T)
    out["w_lr"] = np.ascontiguousarray(g["gla_w_lr"][0])
    out["rel_bias"] = np.ascontiguousarray(g["rel_bias"])
    return {**out, **constants()}


def kernel(**inputs):
    import concourse.bacc as bacc
    from concourse.bass_utils import run_bass_kernel_spmd

    arrays = lay_out(inputs)
    nc = bacc.Bacc("TRN2", target_bir_lowering=False, num_devices=1)
    io = {n: nc.dram_tensor(f"in_{n}", a.shape, mybir.dt.from_np(a.dtype), kind="ExternalInput").ap()
          for n, a in arrays.items()}
    io["outT"] = nc.dram_tensor("outT", (KT, P, SEQ), F32, kind="ExternalOutput").ap()
    build(nc, io)
    r = run_bass_kernel_spmd(nc, [{f"in_{n}": a for n, a in arrays.items()}], core_ids=[0])
    got = r.results[0]["outT"]
    return np.ascontiguousarray(got.reshape(D, SEQ).T.reshape(1, SEQ, D))
```

```python
import math
from contextlib import ExitStack

import numpy as np

import concourse.bass as bass
from concourse import mybir

F32 = mybir.dt.float32
F32R = mybir.dt.float32r
U8 = mybir.dt.uint8
ACT = mybir.ActivationFunctionType
ALU = mybir.AluOpType

P = 128
D = 1024
KT = D // P
SEQ = 512
META = 16
NT = SEQ + META
HALF = NT // 2
DFF = 2816
FT = DFF // P
DOWN_SPLIT = (6, 6, 5, 5)
EPS = 1e-6
GH, DK, DV = 4, 128, 256
LOWRANK = 16
TAU = 16.0
DH_HEADS, DH = 8, 128
IH, IDH = 8, 64
TOPK = min(256, SEQ // 4)
BUCKETS, MAX_DIST = 32, 128
QT = SEQ // P
LEVELS = (64, 32, 16, 8, 4, 2, 1)
DIAG = len(LEVELS)
ORDER = (0, 1, 2, 3, 4, DIAG, 5, 6)
NEG = -3.0e38
MASKED = -1.0e30
GLR_ROW, IW_ROW = 64, 96
WIDTH = [META + P * (i + 1) for i in range(QT)]
COL = [sum(WIDTH[:i]) for i in range(QT)]
LINE = NT + P
SLOTS = 4
BLOCK = KT * P

V_FFN1, V_MIX, V_FFN2, V_FINAL, V_GLA, V_BLR = 0, 8, 16, 24, 32, 34
NVEC = V_BLR + GH

G_UP1 = 0
G_DOWN1 = G_UP1 + 2 * FT
G_IDX = G_DOWN1 + 4 * KT
G_GLA = G_IDX + 5
G_DSA = G_GLA + 4 * GH
G_MERGE = G_DSA + 4 * DH_HEADS
G_OUT = G_MERGE + 4 * KT
G_UP2 = G_OUT + KT
G_DOWN2 = G_UP2 + 2 * FT
G_END = G_DOWN2 + 4 * KT
T_UP1 = 2
T_DOWN1 = T_UP1 + 2 * FT
T_IDX = T_DOWN1 + KT
T_GLA = T_IDX + 5
T_DSA = T_GLA + 4 * GH
T_MERGE = T_DSA + 4 * DH_HEADS
T_OUT = T_MERGE + 4 * KT
T_UP2 = T_OUT + KT
T_DOWN2 = T_UP2 + 2 * FT


def build(nc, io):
    ctx = ExitStack()
    with ctx:
        def sem(name):
            return ctx.enter_context(nc.semaphore(name))

        arena_bytes = 212800
        base = (nc.sbuf_base + 31) // 32 * 32
        ctx.enter_context(nc.sbuf_tensor("arena", [P, arena_bytes // 4], F32))
        top = [0]

        def at(name, shape, dt, off):
            size = int(np.prod(shape[1:])) * (1 if dt == U8 else 4)
            assert off % 32 == 0 and off + size <= arena_bytes, (name, off, size)
            return nc.alloc_sbuf_tensor_at(name, shape, dt, offset=base + off), off + (size + 31) // 32 * 32

        def keep(name, shape, dt=F32):
            t, top[0] = at(name, shape, dt, top[0])
            return t

        hT = keep("hT", [P, KT, NT])
        xh = keep("xh", [P, KT, NT], F32R)
        xl = keep("xl", [P, KT, NT], F32R)
        rstd = keep("rstd", [P, NT])
        ssum = keep("ssum", [P, NT])
        wraw = keep("wraw", [P, SLOTS, BLOCK])
        wh = keep("wh", [P, SLOTS, BLOCK], F32R)
        wl = keep("wl", [P, SLOTS, BLOCK], F32R)
        vecs = keep("vecs", [P, NVEC])
        ones = keep("ones", [P, P])
        ident = keep("ident", [P, P])
        eps = keep("eps", [P, 1])
        sq = keep("sq", [P, NT])
        FREE = top[0]

        def region(start):
            cur = [start]

            def put(name, shape, dt=F32):
                t, cur[0] = at(name, shape, dt, cur[0])
                return t
            put.here = lambda: cur[0]
            return put

        put = region(FREE)
        ah = put("ah", [P, FT, NT], F32R)
        al = put("al", [P, FT, NT], F32R)
        zg = put("zg", [P, NT])
        sg = put("sg", [P, NT])
        zu = put("zu", [P, NT])
        put = region(FREE)
        oT = put("oT", [P, KT, SEQ])
        yah, _ = at("yah", [P, KT, SEQ], F32R, FREE)
        Y = put.here()
        yal = put("yal", [P, KT, SEQ], F32R)
        ybh = put("ybh", [P, KT, SEQ], F32R)
        ybl = put("ybl", [P, KT, SEQ], F32R)
        score = put("score", [P, sum(WIDTH)])
        DS = put.here()
        dput = region(DS)
        work = dput("work", [P, sum(WIDTH)])
        pT, _ = at("pT", [P, 2, (QT + 1) * P], F32, DS)
        dqT = dput("dqT", [P, SEQ])
        dkT = dput("dkT", [P, NT])
        dvT = dput("dvT", [P, NT])
        dV = dput("dV", [P, QT + 1, DH])
        strip = dput("strip", [P, NT])
        logit = dput("logit", [P, 2, NT])
        zr = dput("zr", [P, SEQ])
        sr = dput("sr", [P, SEQ])
        nmax = dput("nmax", [P, 2])
        rowsum = dput("rowsum", [P, 2])
        rinv = dput("rinv", [P, 2])
        on = dput("on", [P, QT, DV])
        mput = region(DS - 4 * sum(WIDTH))
        mh = mput("mh", [P, KT, SEQ], F32R)
        ml = mput("ml", [P, KT, SEQ], F32R)
        assert mput.here() >= dput.here() - 4 * QT * DV - 32, "the first gates come before the last head is done"
        sga, sgb, ma = (mput(n, [P, SEQ]) for n in ("sga", "sgb", "ma"))
        gput = region(Y)
        blog = gput("blog", [P, GH, NT])
        qT = gput("qT", [P, SEQ])
        kT = gput("kT", [P, NT])
        vT = gput("vT", [P, 2, NT])
        V = gput("V", [P, QT + 1, DV])
        x_at = gput.here()
        X = gput("X", [P, 2, SEQ])
        E = gput("E", [P, 2, SEQ])
        Dl = gput("Dl", [P, 2, SEQ])
        A = gput("A", [P, SEQ])
        S = gput("S", [P, QT, DV])
        sp, _ = at("sp", [P, GH, NT], F32, x_at)
        lvlmask = gput("lvlmask", [P, len(LEVELS) + 1, P], U8)
        eb = gput("eb", [P, QT])
        ossq = gput("ossq", [P, QT])
        orms = gput("orms", [P, QT])
        orstd = gput("orstd", [P, QT])
        m8 = gput("m8", [P, QT, 8])
        iwq = gput("iwq", [P, QT, IH])
        triu = gput("triu", [P, P])
        qe = gput("qe", [P, SEQ])
        ke = gput("ke", [P, NT])
        kdT = gput("kdT", [P, QT, P])
        assert gput.here() <= DS - 4 * sum(WIDTH)
        iput = region(FREE)
        iq = iput("iq", [P, 4, SEQ])
        misc = iput("misc", [P, NT])
        iput = region(DS + (sum(WIDTH) * 4 + 31) // 32 * 32)
        ik2 = iput("ik2", [P, NT])
        t1 = iput("t1", [P, 2, NT])
        chunk0 = iput("chunk0", [P, NT])
        wlr = iput("wlr", [P, GH * DK])
        relb = iput("relb", [BUCKETS, DH_HEADS])
        oneh = iput("oneh", [BUCKETS, LINE])
        line = iput("line", [DH_HEADS, LINE])
        final, _ = at("final", [P, KT, SEQ], F32, FREE)

        proj = ctx.enter_context(nc.psum_tensor("proj", [P, 2, 1024], F32))
        ps = ctx.enter_context(nc.psum_tensor("ps", [P, 2, 1024], F32))

        bias_line = nc.dram_tensor("bias_line", (DH_HEADS, LINE), F32)
        bias_strip = nc.dram_tensor("bias_strip", (DH_HEADS, P, NT), F32)

        def wide(r):
            return proj[:, r, :].rearrange("p (b n) -> p b n", b=2)[:, :, 0:HALF]

        def squares(n, m):
            return zu if n == 0 and m % 2 else sq

        def two(x):
            return x.rearrange("p (b n) -> p b n", b=2)

        def f(x):
            return x.bitcast(F32)

        consts = sem("consts")
        consts2 = sem("consts2")
        h_in = [sem(f"h_in{n}") for n in range(KT // 2)]
        w_in = [sem(f"w_in{s}") for s in range(SLOTS)]
        w_hi = sem("w_hi")
        w_lo = sem("w_lo")
        w_used = sem("w_used")
        evac = sem("evac")
        x_hi = sem("x_hi")
        x_lo = sem("x_lo")
        squared = sem("squared")
        ss_acc = sem("ss_acc")
        ss_sum = sem("ss_sum")
        rms_ok = sem("rms_ok")
        rstd_ok = sem("rstd_ok")
        setup = sem("setup")
        sig = sem("sig")
        gated = sem("gated")
        act_f = sem("act_f")
        act_hi = sem("act_hi")
        act_lo = sem("act_lo")
        iwT_mm = sem("iwT_mm")
        iw_ok = sem("iw_ok")
        ik2_in = sem("ik2_in")
        z_mm = sem("z_mm")
        lvl_ok = sem("lvl_ok")
        zb_ok = sem("zb_ok")
        softp = sem("softp")
        ls_ok = sem("ls_ok")
        b_ok = sem("b_ok")
        line_mm = sem("line_mm")
        line_ok = sem("line_ok")
        line_st = sem("line_st")
        s_mm = sem("s_mm")
        s_relu = sem("s_relu")
        s_acc = sem("s_acc")
        tk = sem("tk")
        mask_ok = sem("mask_ok")
        d_ok = sem("d_ok")
        e_ok = sem("e_ok")
        x_ok = sem("x_ok")
        g_mm = sem("g_mm")
        a_ok = sem("a_ok")
        vt_mm = sem("vt_mm")
        vt_ok = sem("vt_ok")
        de_ok = sem("de_ok")
        ex_ok = sem("ex_ok")
        qk_ok = sem("qk_ok")
        kd_mm = sem("kd_mm")
        kd_ok = sem("kd_ok")
        u_mm = sem("u_mm")
        s_ok = sem("s_ok")
        o_mm = sem("o_mm")
        oss_ok = sem("oss_ok")
        orms_ok = sem("orms_ok")
        orstd_ok = sem("orstd_ok")
        on_ok = sem("on_ok")
        ot_mm = sem("ot_mm")
        ot_ok = sem("ot_ok")
        strip_in = sem("strip_in")
        dv_mm = sem("dv_mm")
        dv_ok = sem("dv_ok")
        qk_mm = sem("qk_mm")
        lg_ok = sem("lg_ok")
        lm_ok = sem("lm_ok")
        p_ok = sem("p_ok")
        ri_ok = sem("ri_ok")
        pn_ok = sem("pn_ok")
        pt_mm = sem("pt_mm")
        pt_ok = sem("pt_ok")
        pv_mm = sem("pv_mm")
        yb_hi = sem("yb_hi")
        yb_lo = sem("yb_lo")
        r_sig = sem("r_sig")
        r_g = sem("r_g")
        ya_f = sem("ya_f")
        ya_hi = sem("ya_hi")
        ya_lo = sem("ya_lo")
        m_sig = sem("m_sig")
        m_sum = sem("m_sum")
        m_hi = sem("m_hi")
        m_lo = sem("m_lo")
        out_ok = sem("out_ok")
        out_st = sem("out_st")
        carried = sem("carried")

        def apart(eng):
            eng.sem_inc(carried, 1)

        block = ctx.enter_context(nc.Block())

        @block.sync
        def _(sp):
            def load(g, src, cols=BLOCK):
                slot = g % SLOTS
                if g >= SLOTS:
                    sp.wait_ge(w_lo, g - SLOTS + 1)
                sp.dma_start(wraw[:, slot, 0:cols], src).then_inc(w_in[slot], 16)

            def load_loop(g0, n, src):
                with sp.Fori(0, n) as i:
                    for j in range(4):
                        row = sp.snap(i * 4 + j)
                        free = sp.snap(i * 4 + (g0 + j - SLOTS + 1))
                        slot = (g0 + j) % SLOTS
                        sp.wait_ge(w_lo, free)
                        sp.dma_start(wraw[:, slot, :], src[row]).then_inc(w_in[slot], 16)

            def load_down(g0, src):
                with sp.Fori(0, KT) as m:
                    k = 0
                    row = sp.snap(m * 1)
                    for j, n in enumerate(DOWN_SPLIT):
                        free = sp.snap(m * 4 + (g0 + j - SLOTS + 1))
                        slot = (g0 + j) % SLOTS
                        sp.wait_ge(w_lo, free)
                        sp.dma_start(wraw[:, slot, 0:n * P], src[row][:, k * P:(k + n) * P])\
                          .then_inc(w_in[slot], 16)
                        k += n

            load(0, io["w_up1"][0])
            for n in range(KT // 2):
                sp.dma_start(hT[:, 2 * n:2 * n + 2, :], io["xT"][:, 2 * n:2 * n + 2, :]).then_inc(h_in[n], 16)
                if n < SLOTS - 1:
                    load(n + 1, io["w_up1"][n + 1])
            load_loop(SLOTS, 2 * FT // 4 - 1, io["w_up1"][SLOTS:])
            load_down(G_DOWN1, io["w_down1"])
            for j in range(5):
                load(G_IDX + j, io["w_mix"][j])
                if j == 3:
                    sp.wait_ge(w_used, G_IDX)
                    sp.dma_start(on[:, :, :].rearrange("p c n -> p (c n)"), io["lvlmask"]).then_inc(consts2, 16)
                    sp.dma_start(triu[:, :], io["triu"]).then_inc(consts2, 16)
                    sp.dma_start(chunk0[:, :], io["chunk0"]).then_inc(consts2, 16)
                    sp.dma_start(wlr[GLR_ROW:GLR_ROW + LOWRANK, :], io["w_lr"]).then_inc(consts2, 16)
                    sp.dma_start(relb[:, :], io["rel_bias"]).then_inc(consts2, 16)
                    sp.dma_start(oneh[:, :], io["oneh"]).then_inc(consts2, 16)
            load_loop(G_GLA, (G_UP2 - G_GLA) // 4, io["w_mix"][5:])
            load_loop(G_UP2, 2 * FT // 4, io["w_up2"])
            load_down(G_DOWN2, io["w_down2"])
            for m in range(KT):
                sp.wait_ge(out_ok, m + 1)
                sp.dma_start(io["outT"][m], final[:, m, :]).then_inc(out_st, 16)
            sp.wait_ge(out_st, 16 * KT)

        @block.gpsimd
        def _(pool):
            def lo(g, slot):
                pool.wait_ge(w_hi, g + 1)
                pool.tensor_tensor(wl[:, slot, :], wraw[:, slot, :], f(wh[:, slot, :]), ALU.subtract)\
                    .then_inc(w_lo, 1)

            def lo_loop(g0, n):
                with pool.Fori(0, n) as i:
                    for j in range(4):
                        lo(i * 4 + (g0 + j), (g0 + j) % SLOTS)

            pool.memset(ones[:, :], 1.0).then_inc(setup, 1)
            for g in range(SLOTS):
                lo(g, g)
            lo_loop(SLOTS, G_GLA // 4 + 1)
            for g in range(2 * SLOTS + G_GLA // 4 * 4, G_GLA + 2 * SLOTS - 1):
                lo(g, g % SLOTS)
            pool.memset(A[:, :], 0.0).then_inc(setup, 1)

            def level(hd, l):
                m = LEVELS[l]
                if l >= 2:
                    pool.wait_ge(g_mm, hd * 8 + (l - 1))
                pool.wait_ge(e_ok, hd * 7 + (l + 1))
                v = {n: x.rearrange("p (b two m) -> p b two m", two=2, m=m) for n, x in
                     (("q", qT[:, :]), ("k", kT[:, META:NT]), ("E", E[:, l % 2, :]), ("X", X[:, l % 2, :]))}
                pool.tensor_tensor(v["X"][:, :, 1, :], v["q"][:, :, 1, :], v["E"][:, :, 1, :], ALU.mult)\
                    .then_inc(x_ok, 1)
                pool.tensor_tensor(v["X"][:, :, 0, :], v["k"][:, :, 0, :], v["E"][:, :, 0, :], ALU.mult)\
                    .then_inc(x_ok, 1)

            def first_levels(hd):
                pool.wait_ge(evac, hd * 4 + (T_GLA + 3))
                level(hd, 0)
                level(hd, 1)

            def gla_head(hd, last=False):
                for l in range(2, 5):
                    level(hd, l)
                pool.wait_ge(ex_ok, hd * 3 + 1)
                pool.tensor_tensor(ke[:, :], kT[:, :], sq[:, :], ALU.mult).then_inc(qk_ok, 1)
                level(hd, 5)
                level(hd, 6)
                pool.wait_ge(ex_ok, hd * 3 + 2)
                pool.tensor_tensor(qe[:, :], qT[:, :], E[:, 1, :], ALU.mult).then_inc(qk_ok, 1)
                for j in range(-1, 3):
                    lo(hd * 4 + (G_GLA + 2 * SLOTS + j), (G_GLA + j) % SLOTS)
                if not last:
                    first_levels(hd + 1)

            first_levels(0)
            with pool.Fori(0, GH - 1) as hd:
                gla_head(hd)
            gla_head(GH - 1, last=True)
            lo(G_DSA + 2 * SLOTS - 1, (G_DSA - 1) % SLOTS)
            lo_loop(G_DSA + 2 * SLOTS, (G_END - G_DSA - 2 * SLOTS) // 4)

        @block.scalar
        def _(act):
            act.dma_start(vecs[:, :], io["vecs"]).then_inc(consts, 16)
            act.dma_start(ident[:, :], io["ident"]).then_inc(consts, 16)

            def first_token(n):
                return 0 if n == 0 else META

            def hi(g, slot):
                act.wait_ge(w_in[slot], 16 * (g // SLOTS + 1))
                if g >= SLOTS:
                    act.wait_ge(w_used, g - SLOTS + 1)
                act.activation(wh[:, slot, :], wraw[:, slot, :], ACT.Copy).then_inc(w_hi, 1)

            def hi_at(i, per, g0):
                if isinstance(i, int):
                    if i * per + g0 < G_END:
                        hi(i * per + g0, g0 % SLOTS)
                    return
                slot = g0 % SLOTS
                act.wait_ge(w_in[slot], i * (16 * per // SLOTS) + 16 * (g0 // SLOTS + 1))
                act.wait_ge(w_used, i * per + (g0 - SLOTS + 1))
                act.activation(wh[:, slot, :], wraw[:, slot, :], ACT.Copy).then_inc(w_hi, 1)

            def gained(m, tok0, gain):
                apart(act)
                act.activation(xh[:, m, tok0:NT], hT[:, m, tok0:NT], ACT.Copy,
                               scale=vecs[:, gain + m:gain + m + 1] if isinstance(m, int)
                               else vecs[:, bass.ds(m + gain, 1)]).then_inc(x_hi, 1)

            def square(n, m, tok0):
                if n == 0:
                    if m >= 2:
                        act.wait_ge(ss_acc, m)
                else:
                    act.wait_ge(ss_acc, m + (9 * n + 1))
                    apart(act)
                act.activation(squares(n, m)[:, tok0:NT], hT[:, m, tok0:NT], ACT.Square).then_inc(squared, 1)

            def x_tile(n, m, tok0, gain):
                if gain is not None:
                    gained(m, tok0, gain)
                square(n, m, tok0)

            def rms(n, tok0):
                act.wait_ge(ss_sum, n + 1)
                if tok0 == 0:
                    act.activation(two(sq[:, :]), ps[:, 0, :].rearrange("p (b n) -> p b n", b=2)[:, :, 0:HALF],
                                   ACT.Sqrt, bias=eps[:, :], scale=1.0 / D).then_inc(rms_ok, 1)
                else:
                    act.activation(sq[:, META:NT], ps[:, 0, 0:SEQ], ACT.Sqrt, bias=eps[:, :], scale=1.0 / D)\
                       .then_inc(rms_ok, 1)

            def up(i, n, g0, t0):
                for j in range(2):
                    ft = i * 2 + j
                    hi_at(i, 4, g0 + 2 * j + SLOTS)
                    act.wait_ge(evac, i * 4 + (t0 + 2 * j + 1))
                    act.activation(sg[:, first_token(n):NT], zg[:, first_token(n):NT], ACT.Sigmoid).then_inc(sig, 1)
                    act.wait_ge(act_f, i * 2 + (FT * n + j + 1))
                    apart(act)
                    act.activation(ah[:, ft, first_token(n):NT], zu[:, first_token(n):NT], ACT.Copy).then_inc(act_hi, 1)
                    hi_at(i, 4, g0 + 2 * j + 1 + SLOTS)

            def down(i, n, g0, t0, gain):
                for j in range(2):
                    for b in range(4):
                        hi_at(i, 8, g0 + 4 * j + b + SLOTS)
                    act.wait_ge(evac, i * 2 + (t0 + j + 1))
                    x_tile(n, i * 2 + j, first_token(n - 1), gain)

            act.wait_ge(evac, 1)
            act.activation(sg[:, 0:1], eps[:, :], ACT.Sqrt)
            hi(0, 0)
            act.wait_ge(consts, 16 * 2)
            act.wait_ge(evac, 2)
            for m in range(KT):
                if m % 2 == 0:
                    act.wait_ge(h_in[m // 2], 16)
                gained(m, 0, V_FFN1)
                if m == 4:
                    hi(1, 1)
            for m in range(KT):
                square(0, m, 0)
                if m in (1, 5):
                    hi(2 + m // 4, 2 + m // 4)
            rms(0, 0)
            with act.Fori(0, FT // 2) as i:
                up(i, 0, G_UP1, T_UP1)
            with act.Fori(0, KT // 2) as i:
                down(i, 1, G_DOWN1, T_DOWN1, V_MIX)
            rms(1, 0)

            def hi_next(j):
                hi_at(0, 4, G_IDX + j + SLOTS)

            hi_next(0)
            act.wait_ge(evac, T_IDX + 1)
            act.dma_start(ik2[64:128, :], misc[0:64, :]).then_inc(ik2_in, 16)
            for j in range(1, 4):
                hi_next(j)
            act.wait_ge(zb_ok, GH)
            act.activation(sp[:, :, :], blog[:, :, :], ACT.Abs).then_inc(softp, 1)
            act.wait_ge(softp, 1)
            act.activation(sp[:, :, :], sp[:, :, :], ACT.Exp, scale=-1.0).then_inc(softp, 1)
            act.wait_ge(softp, 2)
            act.activation(sp[:, :, :], sp[:, :, :], ACT.Ln, bias=1.0).then_inc(softp, 1)
            hi_next(4)
            act.wait_ge(line_ok, 1)
            act.dma_start(bias_line.ap(), line[:, :]).then_inc(line_st, 16)
            def level(hd, l):
                act.wait_ge(d_ok, hd * 14 + (2 * l + 2))
                if l >= 2:
                    act.wait_ge(x_ok, hd * 14 + 2 * (l - 1))
                act.activation(E[:, l % 2, :], Dl[:, l % 2, :], ACT.Exp, scale=1.0 / TAU).then_inc(e_ok, 1)

            for i in range(QT):
                if i == 3:
                    level(0, 2)
                hi_next(5 + i)
                for n in range(i * IH, (i + 1) * IH):
                    act.wait_ge(s_mm, n + 1)
                    if n >= 2:
                        act.wait_ge(s_acc, n - 1)
                    act.activation(t1[:, n % 2, 0:WIDTH[i]], ps[:, n % 2, 0:WIDTH[i]], ACT.Relu).then_inc(s_relu, 1)
                if i == 1:
                    level(0, 0)
                    level(0, 1)
                    act.wait_ge(line_st, 16)
                    act.dma_start(bias_strip.ap(), bass.AP(bias_line, P - 1, [[LINE, DH_HEADS], [-1, P], [1, NT]]))\
                       .then_inc(line_st, 16)
            act.wait_ge(line_st, 32)
            act.dma_start(strip[:, :], bias_strip.ap()[0]).then_inc(strip_in, 16)

            def gla_head(hd, last=False):
                def copy_v(j):
                    act.wait_ge(vt_mm, hd * 2 + (j + 1))
                    act.activation(V[:, 1:QT + 1, j * P:(j + 1) * P],
                                   ps[:, 1, 0:QT * P].rearrange("p (c n) -> p c n", c=QT), ACT.Copy).then_inc(vt_ok, 1)
                    act.activation(V[0:META, 0, j * P:(j + 1) * P], ps[0:META, 1, 512:512 + P], ACT.Copy)\
                       .then_inc(vt_ok, 1)

                level(hd, 3)
                copy_v(0)
                level(hd, 4)
                act.wait_ge(de_ok, hd * 2 + 2)
                act.activation(sq[:, :], sq[:, :], ACT.Exp, scale=-1.0 / TAU).then_inc(ex_ok, 1)
                level(hd, 5)
                level(hd, 6)
                hi_at(hd, 4, G_GLA + 2 * SLOTS)
                copy_v(1)
                act.wait_ge(x_ok, hd * 14 + 12)
                apart(act)
                act.activation(E[:, 1, :], blog[:, hd, META:NT], ACT.Exp, scale=1.0 / TAU).then_inc(ex_ok, 1)
                apart(act)
                act.activation(eb[:, :], blog[:, hd, META:NT].rearrange("p (c t) -> p c t", c=QT)[:, :, P - 1],
                               ACT.Exp, scale=1.0 / TAU).then_inc(ex_ok, 1)
                act.wait_ge(kd_mm, hd + 1)
                act.activation(kdT[:, 1:QT, :], ps[:, 1, 0:(QT - 1) * P].rearrange("p (c n) -> p c n", c=QT - 1),
                               ACT.Copy).then_inc(kd_ok, 1)
                act.activation(kdT[0:META, 0, :], ps[0:META, 1, 512:512 + P], ACT.Copy).then_inc(kd_ok, 1)
                hi_at(hd, 4, G_GLA + 2 * SLOTS + 1)
                if not last:
                    act.wait_ge(qk_ok, hd * 2 + 2)
                    level(hd + 1, 0)
                    level(hd + 1, 1)
                hi_at(hd, 4, G_GLA + 2 * SLOTS + 2)
                for c in range(QT):
                    act.wait_ge(o_mm, hd * 4 + (c // 2 * 2 + 2))
                    act.activation(sq[:, 0:DV], ps[:, 0, c * DV:(c + 1) * DV], ACT.Square,
                                   accum_out=ossq[:, c:c + 1]).then_inc(oss_ok, 1)
                    act.wait_ge(oss_ok, hd * 4 + (c + 1))
                act.activation(orms[:, :], ossq[:, :], ACT.Sqrt, bias=eps[:, :], scale=1.0 / DV).then_inc(orms_ok, 1)
                if not last:
                    level(hd + 1, 2)
                hi_at(hd, 4, G_GLA + 2 * SLOTS + 3)
                for j in range(2):
                    act.wait_ge(ot_mm, hd * 2 + (j + 1))
                    apart(act)
                    act.activation(oT[:, hd * 2 + j, :], ps[:, 1, j * SEQ:(j + 1) * SEQ], ACT.Copy,
                                   scale=vecs[:, V_GLA + j:V_GLA + j + 1]).then_inc(ot_ok, 1)

            with act.Fori(0, GH - 1) as hd:
                gla_head(hd)
            gla_head(GH - 1, last=True)

            def dsa_head(h, last=False):
                def softmax(i):
                    w = WIDTH[i]
                    act.wait_ge(lm_ok, h * 4 + (i + 1))
                    act.activation(logit[:, i % 2, 0:w], logit[:, i % 2, 0:w], ACT.Exp, scale=-1.0,
                                   bias=nmax[:, i % 2:i % 2 + 1], accum_out=rowsum[:, i % 2:i % 2 + 1])\
                       .then_inc(p_ok, 1)

                def copy_p(i):
                    act.wait_ge(pt_mm, h * 4 + (i + 1))
                    act.activation(pT[:, i % 2, P:P + (i + 1) * P], ps[:, 1, 0:(i + 1) * P], ACT.Copy)\
                       .then_inc(pt_ok, 1)
                    act.activation(pT[0:META, i % 2, 0:P], ps[0:META, 1, 512:512 + P], ACT.Copy)\
                       .then_inc(pt_ok, 1)

                def y_high(i):
                    act.wait_ge(pv_mm, h * 4 + (i + 1))
                    apart(act)
                    act.activation(ybh[:, h, i * P:(i + 1) * P], ps[:, 0, 640:640 + P], ACT.Copy).then_inc(yb_hi, 1)

                def next_hi(j):
                    hi_at(h, 4, G_DSA + 2 * SLOTS + j)

                act.wait_ge(evac, h * 4 + (T_DSA + 4))
                act.activation(sr[:, :], zr[:, :], ACT.Sigmoid).then_inc(r_sig, 1)
                act.wait_ge(dv_mm, h + 1)
                act.activation(dV[:, 1:QT + 1, :], ps[:, 1, 0:QT * P].rearrange("p (c n) -> p c n", c=QT), ACT.Copy)\
                   .then_inc(dv_ok, 1)
                act.activation(dV[0:META, 0, :], ps[0:META, 1, 512:512 + P], ACT.Copy).then_inc(dv_ok, 1)
                softmax(0)
                softmax(1)
                copy_p(0)
                y_high(0)
                copy_p(1)
                next_hi(0)
                softmax(2)
                softmax(3)
                if not last:
                    act.dma_start(strip[:, :], bias_strip.ap()[h + 1]).then_inc(strip_in, 16)
                act.wait_ge(ya_f, h + 1)
                apart(act)
                act.activation(yah[:, h, :], zr[:, :], ACT.Copy).then_inc(ya_hi, 1)
                next_hi(1)
                y_high(1)
                copy_p(2)
                if not last:
                    next_hi(2)
                y_high(2)
                copy_p(3)
                if not last:
                    next_hi(3)
                y_high(3)

            with act.Fori(0, DH_HEADS - 1) as h:
                dsa_head(h)
            dsa_head(DH_HEADS - 1, last=True)

            def merge(m, first=False):
                for j, gate in enumerate((sga, sgb)):
                    act.wait_ge(evac, m * 4 + (T_MERGE + j + 1))
                    act.activation(gate[:, :], gate[:, :], ACT.Sigmoid).then_inc(m_sig, 1)
                    if not first:
                        hi_at(m, 4, G_MERGE + j + SLOTS)
                hi_at(m, 4, G_MERGE + 2 + SLOTS)
                hi_at(m, 4, G_MERGE + 3 + SLOTS)
                act.wait_ge(m_sum, m + 1)
                apart(act)
                act.activation(mh[:, m, :], ma[:, :], ACT.Copy).then_inc(m_hi, 1)

            merge(0, first=True)
            with act.Fori(0, KT - 1) as m:
                merge(m + 1)

            with act.Fori(0, KT // 4) as i:
                for j in range(4):
                    hi_at(i, 4, G_OUT + j + SLOTS)
                    act.wait_ge(evac, i * 4 + (T_OUT + j + 1))
                    x_tile(2, i * 4 + j, META, V_FFN2)
            rms(2, META)
            with act.Fori(0, FT // 2) as i:
                up(i, 1, G_UP2, T_UP2)

            act.wait_ge(evac, T_DOWN2)
            act.activation(sg[:, 0:1], eps[:, :], ACT.Sqrt)
            with act.Fori(0, KT // 2 - 1) as i:
                down(i, 3, G_DOWN2, T_DOWN2, None)
            down(KT // 2 - 1, 3, G_DOWN2, T_DOWN2, None)
            rms(3, META)

        @block.tensor
        def _(pe):
            def chunk_mm(r, slot, kts, k0, total, x_high, x_low, all_tokens, come=None):
                for k in range(kts):
                    if come is not None:
                        pe.wait_ge(come[0], come[1] + k + 1)
                    first, last = k0 + k == 0, k0 + k == total - 1
                    w_h = wh[:, slot, k * P:(k + 1) * P]
                    w_l = wl[:, slot, k * P:(k + 1) * P]
                    for n, (w, a) in enumerate(((w_h, x_high), (w_h, x_low), (w_l, x_high))):
                        for off, bank, size in ((0, 0, HALF), (HALF, 512, HALF)) if all_tokens else ((0, 0, SEQ),):
                            mm = pe.matmul(proj[:, r, bank:bank + size], w, a(k0 + k, off, size),
                                           start=first and n == 0, stop=last and n == 2)
                return mm

            def xs(tok0):
                return (lambda k, off, size: xh[:, k, tok0 + off:tok0 + off + size],
                        lambda k, off, size: xl[:, k, tok0 + off:tok0 + off + size])

            def pair(hi_t, lo_t):
                return (lambda k, off, size: hi_t[:, k, off:off + size],
                        lambda k, off, size: lo_t[:, k, off:off + size])

            def tile8(i, t0, g0, src, all_tokens, per=4, come=None):
                pe.wait_ge(evac, i * per + (t0 - 1))
                pe.wait_ge(w_lo, i * per + (g0 + 1))
                chunk_mm(t0 % 2, g0 % SLOTS, KT, 0, KT, *src, all_tokens, come).then_inc(w_used, 1)

            def transpose(out, in_):
                return pe.transpose(out, in_, ident[:, :])

            def to_tokens(src, n_chunks, sem_):
                for c in range(n_chunks):
                    transpose(ps[:, 1, c * P:(c + 1) * P], src[:, META + c * P:META + (c + 1) * P])
                transpose(ps[0:META, 1, 512:512 + P], src[:, 0:META]).then_inc(sem_, 1)

            def norm_sum(n, tok0):
                pe.wait_ge(ss_acc, 9 * n + 9)
                if tok0 == 0:
                    pe.matmul(ps[:, 0, 0:HALF], ones[:, :], ssum[:, 0:HALF], start=True, stop=True)
                    pe.matmul(ps[:, 0, 512:512 + HALF], ones[:, :], ssum[:, HALF:NT], start=True, stop=True)\
                      .then_inc(ss_sum, 1)
                else:
                    pe.matmul(ps[:, 0, 0:SEQ], ones[:, :], ssum[:, META:NT], start=True, stop=True)\
                      .then_inc(ss_sum, 1)

            def up(n, g0, t0):
                tok0 = 0 if n == 0 else META
                tile8(0, t0, g0, xs(tok0), tok0 == 0, come=(x_lo, 2 * n * KT))
                if n == 0:
                    tile8(0, t0 + 1, g0 + 1, xs(tok0), True)
                    pe.wait_ge(setup, 1)
                    pe.wait_ge(consts, 32)
                norm_sum(2 * n, tok0)
                for j in range(2 - n, 4):
                    tile8(0, t0 + j, g0 + j, xs(tok0), tok0 == 0)
                with pe.Fori(0, FT // 2 - 1) as i:
                    for j in range(4, 8):
                        tile8(i, t0 + j, g0 + j, xs(tok0), tok0 == 0)

            def down(n, g0, t0):
                tok0 = 0 if n == 0 else META
                src = (lambda k, off, size: ah[:, k, tok0 + off:tok0 + off + size],
                       lambda k, off, size: al[:, k, tok0 + off:tok0 + off + size])
                with pe.Fori(0, KT // 2) as i:
                    for j in range(2):
                        pe.wait_ge(evac, i * 2 + (t0 + j - 1))
                        k = 0
                        for b, kts in enumerate(DOWN_SPLIT):
                            g = g0 + 4 * j + b
                            pe.wait_ge(w_lo, i * 8 + (g + 1))
                            pe.wait_ge(act_lo, FT * n + k + kts)
                            chunk_mm((t0 + j) % 2, g % SLOTS, kts, k, FT, *src, tok0 == 0).then_inc(w_used, 1)
                            k += kts

            up(0, G_UP1, T_UP1)
            down(0, G_DOWN1, T_DOWN1)

            def gate_z(h):
                if h >= 2:
                    pe.wait_ge(zb_ok, h - 1)
                elif h == 1:
                    pe.wait_ge(iw_ok, 1)
                w = wlr[GLR_ROW:GLR_ROW + LOWRANK, h * DK:(h + 1) * DK]
                x = misc[GLR_ROW:GLR_ROW + LOWRANK, :]
                pe.matmul(ps[:, h % 2, 0:HALF], w, x[:, 0:HALF], start=True, stop=True)
                pe.matmul(ps[:, h % 2, 512:512 + HALF], w, x[:, HALF:NT], start=True, stop=True).then_inc(z_mm, 1)

            tile8(0, T_IDX, G_IDX, xs(0), True, come=(x_lo, KT))
            norm_sum(1, 0)
            tile8(0, T_IDX + 1, G_IDX + 1, xs(META), False)
            pe.wait_ge(evac, T_IDX + 1)
            for i in range(QT):
                mm = transpose(ps[:, 1, i * P:(i + 1) * P], misc[:, META + i * P:META + (i + 1) * P])
            mm.then_inc(iwT_mm, 1)
            pe.wait_ge(consts2, 16 * 6)
            gate_z(0)
            tile8(0, T_IDX + 2, G_IDX + 2, xs(META), False)
            gate_z(1)
            gate_z(2)
            tile8(0, T_IDX + 3, G_IDX + 3, xs(META), False)
            gate_z(3)
            tile8(0, T_IDX + 4, G_IDX + 4, xs(META), False)
            pe.wait_ge(zb_ok, 3)
            pe.matmul(ps[0:DH_HEADS, 0, 0:512], relb[:, :], oneh[:, 0:512], start=True, stop=True)
            pe.matmul(ps[0:DH_HEADS, 0, 512:LINE], relb[:, :], oneh[:, 512:LINE], start=True, stop=True)\
              .then_inc(line_mm, 1)
            for i in range(QT):
                tile8(0, T_GLA + i, G_GLA + i, xs(META if i == 1 else 0), i != 1)
                if i == 0:
                    pe.wait_ge(ik2_in, 16)
                for e in range(IH):
                    n = i * IH + e
                    lo_, keys = 64 * (e % 2), (misc if e % 2 == 0 else ik2)
                    if n == 0:
                        pe.wait_ge(line_ok, 1)
                    elif n == 1:
                        pe.wait_ge(zb_ok, GH)
                    else:
                        pe.wait_ge(s_relu, n - 1)
                    w = iq[lo_:lo_ + IDH, e // 2, i * P:(i + 1) * P]
                    first = min(WIDTH[i], 512)
                    mm = pe.matmul(ps[:, n % 2, 0:first], w, keys[lo_:lo_ + IDH, 0:first], start=True, stop=True)
                    if WIDTH[i] > 512:
                        mm = pe.matmul(ps[:, n % 2, 512:NT], w, keys[lo_:lo_ + IDH, 512:NT], start=True, stop=True)
                    mm.then_inc(s_mm, 1)
            pe.wait_ge(s_relu, QT * IH)

            def gla_head(hd, first=False, last=False):
                def level(l, hd=hd):
                    turn = ORDER.index(l)
                    if l != DIAG:
                        pe.wait_ge(x_ok, hd * 14 + (2 * l + 2))
                    if turn >= 2:
                        pe.wait_ge(a_ok, hd * 8 + (turn - 1))
                    for c in range(QT):
                        if l != DIAG:
                            a = X[:, l % 2, c * P:(c + 1) * P]
                            b = a.rearrange("p (b two m) -> p b two m", two=2, m=LEVELS[l])[:, :, 1, :]
                            o, size = (turn % 2) * 512 + c * P // 2, P // 2
                        else:
                            a, b = kT[:, META + c * P:META + (c + 1) * P], qT[:, c * P:(c + 1) * P]
                            o, size = (turn % 2) * 512 + c * P, P
                        mm = pe.matmul(ps[:, 0, o:o + size], a, b, start=True, stop=True)
                    mm.then_inc(g_mm, 1)

                def values(j):
                    if j == 1:
                        pe.wait_ge(vt_ok, hd * 4 + 2)
                    to_tokens(vT[:, j, :], QT, vt_mm)

                def ahead(j):
                    all_tokens = j in (1, 2) if last else j != 1
                    tile8(hd, T_GLA + 4 + j, G_GLA + 4 + j, xs(0 if all_tokens else META), all_tokens)

                if first:
                    level(0)
                    level(1)
                values(0)
                level(2)
                ahead(0)
                level(3)
                level(4)
                values(1)
                level(DIAG)
                level(5)
                level(6)
                pe.wait_ge(vt_ok, hd * 4 + 4)
                pe.wait_ge(qk_ok, hd * 2 + 1)
                to_tokens(ke[:, :], QT - 1, kd_mm)
                ahead(1)
                pe.wait_ge(kd_ok, hd * 2 + 2)
                pe.matmul(ps[:, 1, 0:DV], kdT[0:META, 0, :], V[0:META, 0, :], start=True, stop=True)
                for c in range(1, QT):
                    mm = pe.matmul(ps[:, 1, c * DV:(c + 1) * DV], kdT[:, c, :], V[:, c, :], start=True, stop=True)
                mm.then_inc(u_mm, 1)
                ahead(2)
                pe.wait_ge(a_ok, hd * 8 + 8)
                pe.wait_ge(qk_ok, hd * 2 + 2)
                for c in range(QT):
                    pe.wait_ge(s_ok, hd * 4 + (c + 1))
                    o = ps[:, 0, c * DV:(c + 1) * DV]
                    pe.matmul(o, A[:, c * P:(c + 1) * P], V[:, c + 1, :], start=True, stop=False)
                    pe.matmul(o, qe[:, c * P:(c + 1) * P], S[:, c, :], start=False, stop=True).then_inc(o_mm, 1)
                ahead(3)
                pe.wait_ge(on_ok, hd * 4 + 4)
                for j in range(2):
                    for c in range(QT):
                        mm = transpose(ps[:, 1, j * SEQ + c * P:j * SEQ + (c + 1) * P], on[:, c, j * P:(j + 1) * P])
                    mm.then_inc(ot_mm, 1)
                if not last:
                    level(0, hd + 1)
                    level(1, hd + 1)
                    pe.wait_ge(ot_ok, hd * 2 + 2)

            gla_head(0, first=True)
            with pe.Fori(0, GH - 2) as hd:
                gla_head(hd + 1)
            gla_head(GH - 1, last=True)

            def dsa_head(h, first=False, last=False):
                def logits(i, h=h):
                    if i == 0:
                        pe.wait_ge(evac, h * 4 + (T_DSA + 3))
                    else:
                        pe.wait_ge(lg_ok, h * 4 + i)
                    w = dqT[:, i * P:(i + 1) * P]
                    bank = min(WIDTH[i], 512)
                    mm = pe.matmul(ps[:, 0, 0:bank], w, dkT[:, 0:bank], start=True, stop=True)
                    if WIDTH[i] > 512:
                        pe.wait_ge(yb_lo, h * 4 + 1)
                        mm = pe.matmul(ps[:, 0, 512:NT], w, dkT[:, 512:NT], start=True, stop=True)
                    mm.then_inc(qk_mm, 1)

                def turn(i):
                    pe.wait_ge(pn_ok, h * 4 + (i + 1))
                    to_tokens(logit[:, i % 2, :], i + 1, pt_mm)

                def attend(i):
                    pe.wait_ge(pt_ok, h * 8 + (2 * i + 2))
                    if i == 1:
                        pe.wait_ge(lg_ok, h * 4 + 4)
                    elif i >= 2:
                        pe.wait_ge(yb_lo, h * 4 + i)
                    y = ps[:, 0, 640:640 + P]
                    pe.matmul(y, dV[0:META, 0, :], pT[0:META, i % 2, 0:P], start=True, stop=False)
                    for j in range(i + 1):
                        mm = pe.matmul(y, dV[:, j + 1, :], pT[:, i % 2, (j + 1) * P:(j + 2) * P],
                                       start=False, stop=j == i)
                    mm.then_inc(pv_mm, 1)

                def ahead(j):
                    all_tokens = not last and j in (0, 2)
                    tile8(h, T_DSA + 4 + j, G_DSA + 4 + j, xs(0 if all_tokens else META), all_tokens)

                if first:
                    logits(0)
                    pe.wait_ge(ot_ok, 2 * GH)
                to_tokens(dvT[:, :], QT, dv_mm)
                logits(1)
                ahead(0)
                pe.wait_ge(dv_ok, h * 2 + 2)
                turn(0)
                logits(2)
                attend(0)
                turn(1)
                logits(3)
                ahead(1)
                attend(1)
                turn(2)
                if last:
                    pe.wait_ge(ya_lo, DH_HEADS)
                    tile8(0, T_MERGE + 2, G_MERGE + 2, pair(yah, yal), False)
                else:
                    ahead(2)
                attend(2)
                turn(3)
                if not last:
                    ahead(3)
                    logits(0, h + 1)
                attend(3)

            dsa_head(0, first=True)
            with pe.Fori(0, DH_HEADS - 2) as h:
                dsa_head(h + 1)
            dsa_head(DH_HEADS - 1, last=True)

            pe.wait_ge(yb_lo, DH_HEADS * QT)
            tile8(0, T_MERGE + 3, G_MERGE + 3, pair(ybh, ybl), False)
            with pe.Fori(0, KT - 1) as m:
                tile8(m, T_MERGE + 4, G_MERGE + 4, xs(META), False)
                tile8(m, T_MERGE + 5, G_MERGE + 5, xs(META), False)
                tile8(m, T_MERGE + 6, G_MERGE + 6, pair(yah, yal), False)
                tile8(m, T_MERGE + 7, G_MERGE + 7, pair(ybh, ybl), False)
            tile8(0, T_OUT, G_OUT, pair(mh, ml), False, come=(m_lo, 0))
            for j in range(1, KT):
                tile8(0, T_OUT + j, G_OUT + j, pair(mh, ml), False)
            up(1, G_UP2, T_UP2)
            down(1, G_DOWN2, T_DOWN2)
            norm_sum(3, META)

        @block.vector
        def _(dve):
            def col(c, m):
                return vecs[:, c + m:c + m + 1] if isinstance(m, int) else vecs[:, bass.ds(m + c, 1)]

            def add_square(n, m, tok0):
                dve.wait_ge(squared, m + (8 * n + 1))
                dve.wait_ge(ss_acc, m + (9 * n + 1))
                dve.tensor_tensor(ssum[:, tok0:NT], ssum[:, tok0:NT], squares(n, m)[:, tok0:NT], ALU.add)\
                   .then_inc(ss_acc, 1)

            def x_low(n, m, tok0, gain):
                dve.wait_ge(x_hi, m + (8 * n + 1))
                dve.scalar_tensor_tensor(out=xl[:, m, tok0:NT], in0=hT[:, m, tok0:NT], scalar=col(gain, m),
                                         in1=f(xh[:, m, tok0:NT]), op0=ALU.mult, op1=ALU.subtract)\
                   .then_inc(x_lo, 1)

            def x_tile(n, m, tok0, gain):
                if gain is not None:
                    x_low(n, m, tok0, gain)
                add_square(n, m, tok0)

            def inv_rms(n, tok0):
                dve.wait_ge(rms_ok, n + 1)
                dve.reciprocal(rstd[:, tok0:NT], sq[:, tok0:NT]).then_inc(rstd_ok, 1)
                if n < 3:
                    dve.memset(ssum[:, :], 0.0).then_inc(ss_acc, 1)
                dve.wait_ge(rstd_ok, n + 1)

            def read_wide(dst, r, scale=None):
                return dve.tensor_tensor(two(dst), wide(r), two(rstd[:, :]), ALU.mult).then_inc(evac, 1)

            def read_seq(dst, r, scale=1.0):
                if scale == 1.0:
                    return dve.tensor_tensor(dst, proj[:, r, 0:SEQ], rstd[:, META:NT], ALU.mult).then_inc(evac, 1)
                return dve.scalar_tensor_tensor(out=dst, in0=proj[:, r, 0:SEQ], scalar=scale, in1=rstd[:, META:NT],
                                                op0=ALU.mult, op1=ALU.mult).then_inc(evac, 1)

            def up(n, g0, t0):
                tok0 = 0 if n == 0 else META
                with dve.Fori(0, FT // 2) as i:
                    for j in range(2):
                        for b, dst in enumerate((zg, zu)):
                            r = (t0 + 2 * j + b) % 2
                            dve.wait_ge(w_used, i * 4 + (g0 + 2 * j + b + 1))
                            if tok0 == 0:
                                read_wide(dst[:, :], r)
                            else:
                                read_seq(dst[:, META:NT], r)
                        dve.wait_ge(sig, i * 2 + (FT * n + j + 1))
                        dve.wait_ge(evac, i * 4 + (t0 + 2 * j + 2))
                        dve.tensor_tensor(zg[:, tok0:NT], zg[:, tok0:NT], sg[:, tok0:NT], ALU.mult).then_inc(gated, 1)
                        dve.wait_ge(gated, i * 2 + (FT * n + j + 1))
                        dve.tensor_tensor(zu[:, tok0:NT], zg[:, tok0:NT], zu[:, tok0:NT], ALU.mult).then_inc(act_f, 1)
                        dve.wait_ge(act_hi, i * 2 + (FT * n + j + 1))
                        dve.tensor_tensor(al[:, i * 2 + j, tok0:NT], zu[:, tok0:NT], f(ah[:, i * 2 + j, tok0:NT]),
                                          ALU.subtract).then_inc(act_lo, 1)
                        dve.wait_ge(act_lo, i * 2 + (FT * n + j + 1))

            def down(n, g0, t0, norm, gain):
                tok0 = 0 if n == 0 else META
                with dve.Fori(0, KT // 2) as i:
                    for j in range(2):
                        m, r = i * 2 + j, (t0 + j) % 2
                        dve.wait_ge(w_used, i * 8 + (g0 + 4 * j + 4))
                        if tok0 == 0:
                            h_, p_ = two(hT[:, m, :]), wide(r)
                        else:
                            h_, p_ = hT[:, m, META:NT], proj[:, r, 0:SEQ]
                        dve.scalar_tensor_tensor(out=h_, in0=p_, scalar=0.5, in1=h_, op0=ALU.mult, op1=ALU.add)\
                           .then_inc(evac, 1)
                        dve.wait_ge(evac, i * 2 + (t0 + j + 1))
                        x_tile(norm, m, tok0, gain)

            dve.memset(eps[:, :], EPS).then_inc(evac, 1)
            dve.memset(rstd[:, :], 0.0).then_inc(evac, 1)
            dve.memset(ssum[:, :], 0.0).then_inc(ss_acc, 1)
            dve.wait_ge(consts, 32)
            for m in range(KT):
                if m % 2 == 0:
                    dve.wait_ge(h_in[m // 2], 16)
                x_low(0, m, 0, V_FFN1)
            for m in range(KT):
                add_square(0, m, 0)
            inv_rms(0, 0)
            up(0, G_UP1, T_UP1)
            down(0, G_DOWN1, T_DOWN1, 1, V_MIX)
            inv_rms(1, 0)

            def gate_bias(h):
                dve.wait_ge(z_mm, h + 1)
                apart(dve)
                dve.tensor_scalar(two(blog[:, h, :]), ps[:, h % 2, :].rearrange("p (b n) -> p b n", b=2)[:, :, 0:HALF],
                                  vecs[:, V_BLR + h:V_BLR + h + 1], None, ALU.add).then_inc(zb_ok, 1)

            def expo(hd, l):
                m = LEVELS[l]
                if l >= 2:
                    dve.wait_ge(e_ok, hd * 7 + (l - 1))
                b = blog[:, hd, META:NT].rearrange("p (b two m) -> p b two m", two=2, m=m)
                d = Dl[:, l % 2, :].rearrange("p (b two m) -> p b two m", two=2, m=m)
                ref = b[:, :, 0, m - 1:m].to_broadcast([P, SEQ // (2 * m), m])
                dve.tensor_tensor(d[:, :, 1, :], b[:, :, 1, :], ref, ALU.subtract).then_inc(d_ok, 1)
                dve.tensor_tensor(d[:, :, 0, :], ref, b[:, :, 0, :], ALU.subtract).then_inc(d_ok, 1)

            def index_scores(i):
                s_i = score[:, COL[i]:COL[i] + WIDTH[i]]
                for e in range(IH):
                    n = i * IH + e
                    dve.wait_ge(s_relu, n + 1)
                    if e == 0:
                        dve.tensor_scalar(s_i, t1[:, n % 2, 0:WIDTH[i]], iwq[:, i, e:e + 1], 0.0, ALU.mult, ALU.add)\
                           .then_inc(s_acc, 1)
                    else:
                        dve.wait_ge(s_acc, n)
                        dve.scalar_tensor_tensor(out=s_i, in0=t1[:, n % 2, 0:WIDTH[i]], scalar=iwq[:, i, e:e + 1],
                                                 in1=s_i, op0=ALU.mult, op1=ALU.add).then_inc(s_acc, 1)

            dve.wait_ge(w_used, G_IDX + 1)
            read_wide(misc[:, :], T_IDX % 2)
            dve.wait_ge(w_used, G_IDX + 2)
            read_seq(iq[:, 0, :], (T_IDX + 1) % 2)
            dve.wait_ge(iwT_mm, 1)
            iw = ps[:, 1, 0:SEQ].rearrange("p (i n) -> p i n", i=QT)[:, :, IW_ROW:IW_ROW + IH]
            dve.tensor_scalar(iwq[:, :, :], iw, IH ** -0.5 * IDH ** -0.5, None, ALU.mult).then_inc(iw_ok, 1)
            gate_bias(0)
            dve.wait_ge(consts2, 16 * 6)
            dve.tensor_copy(lvlmask[:, :, :].rearrange("p l n -> p (l n)"), on[:, :, :].rearrange("p c n -> p (c n)"))\
               .then_inc(lvl_ok, 1)
            dve.wait_ge(w_used, G_IDX + 3)
            read_seq(iq[:, 1, :], (T_IDX + 2) % 2)
            gate_bias(1)
            gate_bias(2)
            dve.wait_ge(w_used, G_IDX + 4)
            read_seq(iq[:, 2, :], (T_IDX + 3) % 2)
            gate_bias(3)
            dve.wait_ge(w_used, G_IDX + 5)
            read_seq(iq[:, 3, :], (T_IDX + 4) % 2)
            dve.wait_ge(line_mm, 1)
            dve.tensor_copy(line[:, :], ps[0:DH_HEADS, 0, 0:LINE]).then_inc(line_ok, 1)
            dve.wait_ge(iw_ok, 1)
            for i in range(QT):
                dve.wait_ge(w_used, G_GLA + i + 1)
                if i == 1:
                    read_seq(qT[:, :], (T_GLA + 1) % 2, DK ** -0.5)
                else:
                    read_wide((vT[:, 0, :], None, kT[:, :], vT[:, 1, :])[i], (T_GLA + i) % 2)
                index_scores(i)
                dve.wait_ge(s_acc, (i + 1) * IH)
                last_keys = score[:, COL[i] + WIDTH[i] - P:COL[i] + WIDTH[i]]
                dve.tensor_tensor(last_keys, last_keys, triu[:, :], ALU.min).then_inc(tk, 1)
                dve.wait_ge(tk, 2 * i + 1)
                dve.tensor_copy(work[:, COL[i]:COL[i] + WIDTH[i]], score[:, COL[i]:COL[i] + WIDTH[i]]).then_inc(tk, 1)
                if i == 0:
                    dve.wait_ge(softp, 3)
                    dve.wait_ge(zb_ok, GH)
                    dve.scalar_tensor_tensor(out=sp[:, :, :], in0=blog[:, :, :], scalar=0.0, in1=sp[:, :, :],
                                             op0=ALU.min, op1=ALU.subtract).then_inc(ls_ok, 1)
                    dve.wait_ge(ls_ok, 1)
                    for h in range(GH):
                        dve.tensor_tensor_scan(blog[:, h, :], chunk0[:, :], sp[:, h, :], 0.0, ALU.mult, ALU.add)\
                           .then_inc(b_ok, 1)
                    dve.wait_ge(b_ok, GH)
                    expo(0, 0)
                    expo(0, 1)
                elif i == 2:
                    expo(0, 2)
            dve.wait_ge(setup, 2)
            dve.wait_ge(lvl_ok, 1)

            ROUNDS = TOPK // 8 // GH
            TURNS = (1, 3, 2, 0)

            def gla_head(hd, last=False):
                def top_rounds(i):
                    w_i = work[:, COL[i]:COL[i] + WIDTH[i]]
                    turn = TURNS.index(i)
                    for n in range(ROUNDS):
                        at_ = 2 * QT + 2 * (turn * ROUNDS + n)
                        dve.wait_ge(tk, hd * (2 * QT * ROUNDS) + at_)
                        apart(dve)
                        dve.max(m8[:, i, :], w_i).then_inc(tk, 1)
                        dve.wait_ge(tk, hd * (2 * QT * ROUNDS) + (at_ + 1))
                        apart(dve)
                        dve.match_replace(w_i, m8[:, i, :], w_i, NEG).then_inc(tk, 1)

                def merge_level(l):
                    turn = ORDER.index(l)
                    dve.wait_ge(g_mm, hd * 8 + (turn + 1))
                    o = (turn % 2) * 512
                    apart(dve)
                    if turn >= 1:
                        dve.wait_ge(a_ok, hd * 8 + turn)
                        apart(dve)
                    if l != DIAG:
                        m = LEVELS[l]
                        b = P // (2 * m)
                        into = A[:, :].rearrange("p (c b two m) -> p c b two m", c=QT, two=2, m=m)[:, :, :, 1, :]
                        where = lvlmask[:, l, :].rearrange("p (b two m) -> p b two m", two=2, m=m)[:, :, 1, :]\
                            .unsqueeze(1).to_broadcast([P, QT, b, m])
                        new = ps[:, 0, o:o + SEQ // 2].rearrange("p (c b m) -> p c b m", c=QT, m=m)
                    else:
                        into = A[:, :].rearrange("p (c t) -> p c t", c=QT)
                        where = lvlmask[:, l, :].unsqueeze(1).to_broadcast([P, QT, P])
                        new = ps[:, 0, o:o + SEQ].rearrange("p (c t) -> p c t", c=QT)
                    dve.copy_predicated(into, where, new).then_inc(a_ok, 1)

                def read_ahead(j):
                    dve.wait_ge(w_used, hd * 4 + (G_GLA + 4 + j + 1))
                    r = (T_GLA + j) % 2
                    if last:
                        if j in (1, 2):
                            read_wide((dkT if j == 1 else dvT)[:, :], r)
                        elif j == 0:
                            read_seq(dqT[:, :], r, DH ** -0.5)
                        else:
                            read_seq(zr[:, :], r)
                    elif j == 1:
                        dve.wait_ge(qk_ok, hd * 2 + 2)
                        read_seq(qT[:, :], r, DK ** -0.5)
                    else:
                        read_wide((vT[:, 0, :], None, kT[:, :], vT[:, 1, :])[j], r)

                expo(hd, 3)
                merge_level(0)
                merge_level(1)
                expo(hd, 4)
                merge_level(2)
                for n, (src, size) in enumerate(((blog[:, hd, META:NT], P), (blog[:, hd, 0:META], META))):
                    b = src.rearrange("p (c t) -> p c t", t=size)
                    d = (sq[:, META:NT] if n == 0 else sq[:, 0:META]).rearrange("p (c t) -> p c t", t=size)
                    nch = QT if n == 0 else 1
                    dve.tensor_tensor(d, b, b[:, :, size - 1:size].to_broadcast([P, nch, size]), ALU.subtract)\
                       .then_inc(de_ok, 1)
                expo(hd, 5)
                expo(hd, 6)
                top_rounds(1)
                for l in (3, 4, DIAG, 5, 6):
                    merge_level(l)
                read_ahead(0)
                top_rounds(3)
                dve.wait_ge(u_mm, hd + 1)
                dve.tensor_copy(S[:, 0, :], ps[:, 1, 0:DV]).then_inc(s_ok, 1)
                dve.wait_ge(ex_ok, hd * 3 + 3)
                for c in range(1, QT):
                    dve.wait_ge(s_ok, hd * 4 + c)
                    dve.scalar_tensor_tensor(out=S[:, c, :], in0=S[:, c - 1, :], scalar=eb[:, c - 1:c],
                                             in1=ps[:, 1, c * DV:(c + 1) * DV], op0=ALU.mult, op1=ALU.add)\
                       .then_inc(s_ok, 1)
                read_ahead(1)
                if not last:
                    expo(hd + 1, 0)
                    expo(hd + 1, 1)
                top_rounds(2)
                read_ahead(2)
                if not last:
                    expo(hd + 1, 2)
                dve.wait_ge(orms_ok, hd + 1)
                dve.reciprocal(orstd[:, :], orms[:, :]).then_inc(orstd_ok, 1)
                dve.wait_ge(orstd_ok, hd + 1)
                for c in range(QT):
                    dve.tensor_scalar(on[:, c, :], ps[:, 0, c * DV:(c + 1) * DV], orstd[:, c:c + 1], None, ALU.mult)\
                       .then_inc(on_ok, 1)
                top_rounds(0)
                read_ahead(3)

            with dve.Fori(0, GH - 1) as hd:
                gla_head(hd)
            gla_head(GH - 1, last=True)

            def biased(i, h):
                w, b = WIDTH[i], i % 2
                if i == 0:
                    dve.wait_ge(strip_in, h * 16 + 16)
                dve.wait_ge(qk_mm, h * 4 + (i + 1))
                if i >= 2:
                    dve.wait_ge(pt_mm, h * 4 + (i - 1))
                dve.tensor_tensor(logit[:, b, 0:w], ps[:, 0, 0:w], strip[:, NT - w:NT], ALU.add).then_inc(lg_ok, 1)

            biased(0, 0)

            dve.wait_ge(tk, 2 * QT + 2 * QT * (TOPK // 8))
            dve.tensor_tensor(score[:, :], work[:, :], score[:, :], ALU.is_equal).then_inc(tk, 1)
            dve.wait_ge(tk, 2 * QT + 1 + 2 * QT * (TOPK // 8))
            dve.wait_ge(ot_ok, 2 * GH)
            dve.tensor_scalar(score[:, :], score[:, :], MASKED, None, ALU.mult).then_inc(mask_ok, 1)
            dve.wait_ge(mask_ok, 1)

            def dsa_head(h, last=False):
                def masked(i):
                    w, b = WIDTH[i], i % 2
                    dve.wait_ge(lg_ok, h * 4 + (i + 1))
                    apart(dve)
                    dve.tensor_tensor_reduce(logit[:, b, 0:w], logit[:, b, 0:w], score[:, COL[i]:COL[i] + w], -1.0,
                                             3.0e38, ALU.add, ALU.min, nmax[:, b:b + 1]).then_inc(lm_ok, 1)

                def normalise(i):
                    w, b = WIDTH[i], i % 2
                    dve.wait_ge(p_ok, h * 4 + (i + 1))
                    dve.reciprocal(rinv[:, b:b + 1], rowsum[:, b:b + 1]).then_inc(ri_ok, 1)
                    dve.wait_ge(ri_ok, h * 4 + (i + 1))
                    dve.tensor_scalar(logit[:, b, 0:w], logit[:, b, 0:w], rinv[:, b:b + 1], None, ALU.mult)\
                       .then_inc(pn_ok, 1)

                def y_low(i):
                    dve.wait_ge(yb_hi, h * 4 + (i + 1))
                    dve.tensor_tensor(ybl[:, h, i * P:(i + 1) * P], ps[:, 0, 640:640 + P],
                                      f(ybh[:, h, i * P:(i + 1) * P]), ALU.subtract).then_inc(yb_lo, 1)

                def read_ahead(j):
                    dve.wait_ge(w_used, h * 4 + (G_DSA + 4 + j + 1))
                    r = (T_DSA + j) % 2
                    if j in (0, 2):
                        read_wide((dvT if j == 0 else dkT)[:, :], r)
                    elif j == 1:
                        read_seq(dqT[:, :], r, DH ** -0.5)
                    else:
                        read_seq(zr[:, :], r)

                def read_gate(j):
                    dve.wait_ge(w_used, G_MERGE + j + 1)
                    read_seq((sga, sgb)[j][:, :], (T_MERGE + j) % 2)

                biased(1, h)
                masked(0)
                dve.wait_ge(r_sig, h + 1)
                dve.tensor_tensor(sr[:, :], zr[:, :], sr[:, :], ALU.mult).then_inc(r_g, 1)
                dve.wait_ge(r_g, h + 1)
                dve.tensor_tensor(zr[:, :], sr[:, :], oT[:, h, :], ALU.mult).then_inc(ya_f, 1)
                normalise(0)
                masked(1)
                normalise(1)
                read_gate(0) if last else read_ahead(0)
                biased(2, h)
                y_low(0)
                masked(2)
                normalise(2)
                biased(3, h)
                masked(3)
                normalise(3)
                dve.wait_ge(ya_hi, h + 1)
                dve.tensor_tensor(yal[:, h, :], zr[:, :], f(yah[:, h, :]), ALU.subtract).then_inc(ya_lo, 1)
                read_gate(1) if last else read_ahead(1)
                y_low(1)
                if not last:
                    read_ahead(2)
                y_low(2)
                if not last:
                    dve.wait_ge(ya_lo, h + 1)
                    read_ahead(3)
                    biased(0, h + 1)
                y_low(3)

            dsa_head(0)
            with dve.Fori(0, DH_HEADS - 2) as h:
                dsa_head(h + 1)
            dsa_head(DH_HEADS - 1, last=True)

            def merge(m, first=False):
                if not first:
                    for j, gate in enumerate((sga, sgb)):
                        dve.wait_ge(w_used, m * 4 + (G_MERGE + j + 1))
                        read_seq(gate[:, :], (T_MERGE + j) % 2)
                dve.wait_ge(w_used, m * 4 + (G_MERGE + 3))
                dve.wait_ge(m_sig, m * 2 + 1)
                dve.tensor_tensor(ma[:, :], proj[:, (T_MERGE + 2) % 2, 0:SEQ], sga[:, :], ALU.mult).then_inc(evac, 1)
                dve.wait_ge(w_used, m * 4 + (G_MERGE + 4))
                dve.wait_ge(m_sig, m * 2 + 2)
                dve.tensor_tensor(sgb[:, :], proj[:, (T_MERGE + 3) % 2, 0:SEQ], sgb[:, :], ALU.mult).then_inc(evac, 1)
                dve.wait_ge(evac, m * 4 + (T_MERGE + 4))
                dve.tensor_tensor(ma[:, :], ma[:, :], sgb[:, :], ALU.add).then_inc(m_sum, 1)
                dve.wait_ge(m_hi, m + 1)
                dve.tensor_tensor(ml[:, m, :], ma[:, :], f(mh[:, m, :]), ALU.subtract).then_inc(m_lo, 1)

            merge(0, first=True)
            with dve.Fori(0, KT - 1) as m:
                merge(m + 1)

            with dve.Fori(0, KT // 4) as i:
                for j in range(4):
                    m = i * 4 + j
                    dve.wait_ge(w_used, i * 4 + (G_OUT + j + 1))
                    dve.tensor_tensor(hT[:, m, META:NT], proj[:, (T_OUT + j) % 2, 0:SEQ], hT[:, m, META:NT], ALU.add)\
                       .then_inc(evac, 1)
                    dve.wait_ge(evac, i * 4 + (T_OUT + j + 1))
                    x_tile(2, m, META, V_FFN2)
            inv_rms(2, META)
            up(1, G_UP2, T_UP2)
            down(1, G_DOWN2, T_DOWN2, 3, None)
            inv_rms(3, META)
            for m in range(KT):
                dve.scalar_tensor_tensor(out=final[:, m, :], in0=hT[:, m, META:NT], scalar=col(V_FINAL, m),
                                         in1=rstd[:, META:NT], op0=ALU.mult, op1=ALU.mult).then_inc(out_ok, 1)


def rel_bucket(dist):
    n = np.maximum(dist, 0)
    exact = BUCKETS // 2
    nf = np.maximum(n, exact).astype(np.float32)
    large = exact + (np.log(nf / np.float32(exact)) / np.float32(math.log(MAX_DIST / exact))
                     * np.float32(BUCKETS - exact)).astype(np.int32)
    return np.where(n < exact, n, np.minimum(large, BUCKETS - 1))


def constants():
    p, t = np.arange(P)[:, None], np.arange(P)[None, :]
    masks = []
    for m in LEVELS:
        same = p // (2 * m) == t // (2 * m)
        masks.append(same & (p // m % 2 == 0) & (t // m % 2 == 1))
    masks.append(p == t)
    bucket = rel_bucket(NT - 1 - np.arange(LINE))
    chunk0 = np.ones((P, NT), np.float32)
    chunk0[:, [0] + [META + P * c for c in range(QT)]] = 0.0
    return {
        "ident": np.eye(P, dtype=np.float32),
        "lvlmask": np.stack(masks, 1).astype(np.float32).reshape(P, -1),
        "triu": np.where(t <= p, -NEG, NEG).astype(np.float32),
        "chunk0": chunk0,
        "oneh": (np.arange(BUCKETS)[:, None] == bucket[None, :]).astype(np.float32),
    }


def feature_tiles(w, cols=None):
    k, m = w.shape
    return np.ascontiguousarray(w.reshape(k // P, P, m // P, P).transpose(2, 1, 0, 3).reshape(m // P, P, k))


def lay_out(inputs):
    g = {n: np.asarray(a) for n, a in inputs.items()}
    w_in = g["w_in"][0]
    sizes = (GH * DK, GH * DK, GH * DV, GH * DV, LOWRANK, D, D, D, IH * IDH, IDH, IH, D, D)
    cuts = np.cumsum((0,) + sizes)
    gq, gk, gv, gr, glr, dq, dk, dv, iq, ik, iw, ga, gb = (w_in[:, a:b] for a, b in zip(cuts[:-1], cuts[1:]))
    misc = np.zeros((D, P), np.float32)
    misc[:, 0:IDH], misc[:, GLR_ROW:GLR_ROW + LOWRANK], misc[:, IW_ROW:IW_ROW + IH] = ik, glr, iw
    order = [misc, iq]
    for h in range(GH):
        v = gv[:, h * DV:(h + 1) * DV]
        order += [v[:, 0:P], gq[:, h * DK:(h + 1) * DK], gk[:, h * DK:(h + 1) * DK], v[:, P:DV]]
    for h in range(DH_HEADS):
        order += [x[:, h * P:(h + 1) * P] for x in ((dq, dk, dv, gr) if h == 0 else (dv, dq, dk, gr))]
    for m in range(KT):
        order += [x[:, m * P:(m + 1) * P] for x in (ga, gb, g["w_up_a"][0], g["w_up_b"][0])]
    order.append(g["w_out"][0])
    out = {"w_mix": feature_tiles(np.concatenate(order, axis=1))}
    for n in (1, 2):
        gate, up = g[f"ffn{n}_w_gate"][0], g[f"ffn{n}_w_up"][0]
        both = np.stack([gate.reshape(D, FT, P), up.reshape(D, FT, P)], axis=2).reshape(D, 2 * DFF)
        out[f"w_up{n}"] = feature_tiles(both)
        out[f"w_down{n}"] = feature_tiles(g[f"ffn{n}_w_down"][0])
    tokens = np.concatenate([g["meta_tokens"], g["x"][0]], axis=0)
    out["xT"] = np.ascontiguousarray(tokens.T.reshape(KT, P, NT).transpose(1, 0, 2))
    vectors = [g["norm_ffn1"][0], g["norm_mix"][0], g["norm_ffn2"][0], g["norm_final"], g["gla_norm"][0],
               g["gla_b_lr"][0]]
    out["vecs"] = np.ascontiguousarray(np.concatenate(vectors).reshape(NVEC, P).T)
    out["w_lr"] = np.ascontiguousarray(g["gla_w_lr"][0])
    out["rel_bias"] = np.ascontiguousarray(g["rel_bias"])
    return {**out, **constants()}


def kernel(**inputs):
    import concourse.bacc as bacc
    from concourse.bass_utils import run_bass_kernel_spmd

    arrays = lay_out(inputs)
    nc = bacc.Bacc("TRN2", target_bir_lowering=False, num_devices=1)
    io = {n: nc.dram_tensor(f"in_{n}", a.shape, mybir.dt.from_np(a.dtype), kind="ExternalInput").ap()
          for n, a in arrays.items()}
    io["outT"] = nc.dram_tensor("outT", (KT, P, SEQ), F32, kind="ExternalOutput").ap()
    build(nc, io)
    r = run_bass_kernel_spmd(nc, [{f"in_{n}": a for n, a in arrays.items()}], core_ids=[0])
    got = r.results[0]["outT"]
    return np.ascontiguousarray(got.reshape(D, SEQ).T.reshape(1, SEQ, D))
```
